# Optimizing a Trainium2 kernel written in Bass

```python
import jax, jax.numpy as jnp
from jax import lax
import numpy as np

D_MODEL = 1024
BATCH = 1
SEQ = 1024
DEPTH = 1

POOL_WINDOWS = (2, 4, 8, 16)
POOL_GROUPS = len(POOL_WINDOWS)
POOL_WIDTH = D_MODEL // 2
POOL_GROUP_DIM = POOL_WIDTH // POOL_GROUPS
HEAD_DIM = 64
ATTN_WIDTH = D_MODEL // 2
N_HEADS = ATTN_WIDTH // HEAD_DIM
Q_BLOCK = 128
N_BRANCHES = 2
D_FF = ((8 * D_MODEL + 3 * 256 - 1) // (3 * 256)) * 256
RMS_EPS = 1e-6
IN_SPLITS = (POOL_WIDTH, ATTN_WIDTH, ATTN_WIDTH, ATTN_WIDTH, N_HEADS, D_MODEL, D_MODEL)
IN_WIDTH = sum(IN_SPLITS)

kernel_name = "hybrid_pool_fox_gated_block"

def rmsnorm(x, g):
    xf = x.astype(jnp.float32)
    r = lax.rsqrt(jnp.mean(xf * xf, axis=-1, keepdims=True) + RMS_EPS)
    return (xf * r).astype(x.dtype) * g

def causal_multiscale_pool(u):
    B, S, _ = u.shape
    ug = u.reshape(B, S, POOL_GROUPS, POOL_GROUP_DIM)
    c = jnp.cumsum(ug.astype(jnp.float32), axis=1)
    t = jnp.arange(S)
    outs = []
    for g, w in enumerate(POOL_WINDOWS):
        cg = c[:, :, g]
        c_prev = jnp.pad(cg, ((0, 0), (w, 0), (0, 0)))[:, :S]
        cnt = jnp.minimum(t + 1, w).astype(jnp.float32)[None, :, None]
        outs.append((cg - c_prev) / cnt)
    mean = jnp.stack(outs, axis=2)
    return (mean - ug.astype(jnp.float32)).astype(u.dtype)

def forgetting_attention(q, k, v, log_f):
    B, S, H, Dh = q.shape
    q = q.transpose(0, 2, 1, 3)
    k = k.transpose(0, 2, 1, 3)
    v = v.transpose(0, 2, 1, 3)
    F = jnp.cumsum(log_f, axis=1).transpose(0, 2, 1)
    scale = HEAD_DIM ** -0.5
    outs = []
    for i in range(S // Q_BLOCK):
        lo, hi = i * Q_BLOCK, (i + 1) * Q_BLOCK
        s = jnp.einsum('bhqd,bhkd->bhqk', q[:, :, lo:hi], k[:, :, :hi]).astype(jnp.float32) * scale
        s = s + F[:, :, lo:hi, None] - F[:, :, None, :hi]
        mask = (lo + jnp.arange(Q_BLOCK))[:, None] >= jnp.arange(hi)[None, :]
        s = jnp.where(mask, s, -jnp.inf)
        p = jax.nn.softmax(s, axis=-1).astype(v.dtype)
        outs.append(jnp.einsum('bhqk,bhkd->bhqd', p, v[:, :, :hi]))
    o = jnp.concatenate(outs, axis=2)
    return o.transpose(0, 2, 1, 3).reshape(B, S, H * Dh)

def setup_inputs(seed: int = 0) -> dict:
    key = jax.random.key(seed)
    ks = jax.random.split(key, 16)
    f32 = jnp.float32
    n = lambda k, shape, fan_in: jax.random.normal(k, shape, f32) * (fan_in ** -0.5)
    return {
        "x": jax.random.normal(ks[0], (BATCH, SEQ, D_MODEL), f32),
        "norm1_g": 1.0 + 0.02 * jax.random.normal(ks[1], (DEPTH, D_MODEL), f32),
        "w_in": n(ks[2], (DEPTH, D_MODEL, IN_WIDTH), D_MODEL),
        "b_forget": 2.0 + 0.5 * jax.random.normal(ks[3], (DEPTH, N_HEADS), f32),
        "pool_mix": n(ks[4], (DEPTH, POOL_GROUPS, POOL_GROUP_DIM, POOL_GROUP_DIM), POOL_GROUP_DIM),
        "pool_scale": 1.0 + 0.1 * jax.random.normal(ks[5], (DEPTH, POOL_WIDTH), f32),
        "w_pool_out": n(ks[6], (DEPTH, POOL_WIDTH, D_MODEL), POOL_WIDTH),
        "w_attn_out": n(ks[7], (DEPTH, ATTN_WIDTH, D_MODEL), ATTN_WIDTH),
        "w_out": n(ks[8], (DEPTH, D_MODEL, D_MODEL), D_MODEL),
        "norm2_g": 1.0 + 0.02 * jax.random.normal(ks[9], (DEPTH, D_MODEL), f32),
        "w_ffn_gate": n(ks[10], (DEPTH, D_MODEL, D_FF), D_MODEL),
        "w_ffn_up": n(ks[11], (DEPTH, D_MODEL, D_FF), D_MODEL),
        "w_ffn_down": n(ks[12], (DEPTH, D_FF, D_MODEL), D_FF),
        "norm_f_g": 1.0 + 0.02 * jax.random.normal(ks[13], (D_MODEL,), f32),
    }

def reference(x, norm1_g, w_in, b_forget, pool_mix, pool_scale, w_pool_out, w_attn_out, w_out,
              norm2_g, w_ffn_gate, w_ffn_up, w_ffn_down, norm_f_g):
    B, S, _ = x.shape
    offs = np.cumsum((0,) + IN_SPLITS)
    for l in range(DEPTH):
        h = rmsnorm(x, norm1_g[l])
        z = h @ w_in[l]
        u, q, k, v, fl, gp, ga = [z[..., int(offs[i]):int(offs[i + 1])] for i in range(len(IN_SPLITS))]

        p = causal_multiscale_pool(u)
        p = jnp.einsum('bsgc,gcd->bsgd', p, pool_mix[l]).reshape(B, S, POOL_WIDTH) * pool_scale[l]
        pool_y = p @ w_pool_out[l]

        log_f = jax.nn.log_sigmoid(fl.astype(jnp.float32) + b_forget[l].astype(jnp.float32))
        a = forgetting_attention(q.reshape(B, S, N_HEADS, HEAD_DIM), k.reshape(B, S, N_HEADS, HEAD_DIM),
                                 v.reshape(B, S, N_HEADS, HEAD_DIM), log_f)
        attn_y = a @ w_attn_out[l]

        merged = jax.nn.sigmoid(gp) * pool_y + jax.nn.sigmoid(ga) * attn_y
        x = x + merged @ w_out[l]

        h2 = rmsnorm(x, norm2_g[l])
        x = x + (jax.nn.silu(h2 @ w_ffn_gate[l]) * (h2 @ w_ffn_up[l])) @ w_ffn_down[l]
    return rmsnorm(x, norm_f_g)


_drawn_inputs = setup_inputs


def setup_inputs(seed=0):
    import zlib

    import numpy as np

    out = dict(_drawn_inputs(seed))
    spreads = {}
    factors = {'norm1_g': 4.346, 'norm2_g': 4.239, 'norm_f_g': 2.742}
    for name, (base, spread) in spreads.items():
        noise = np.random.default_rng([zlib.crc32(name.encode()), seed]).standard_normal(out[name].shape)
        drawn = base * np.exp(spread * noise) if base else spread * noise
        out[name] = __import__('jax').numpy.asarray(drawn.astype(out[name].dtype))
    for name, factor in factors.items():
        out[name] = (out[name] * factor).astype(out[name].dtype)
    return out
```

```python
import concourse.bass as bass
from concourse import mybir
from contextlib import ExitStack

P = 128
S = 1024
D = 1024
NT = S // P
KD = D // P
HALF = 512
BW = 512
NH = 8
DH = 64
NG = 4
DFF = 2816
KF = DFF // P
EPS = 1e-6
NEG = -1.0e30
COL_U, COL_Q, COL_K, COL_V = 0, BW, 2 * BW, 3 * BW
COL_F = 4 * BW
COL_GP = COL_F + NH
COL_GA = COL_GP + D
VF = BW + NH
VH = VF // 2

C_QK, C_U, C_GATE = 0, 8, 12
C_OUT = C_GATE + 3 * KD
C_FFN = C_OUT + 2 * KD
C_DOWN = C_FFN + 2 * KF
C_END = C_DOWN + 2 * KF

ROUNDS = [1 if (s % 8) < 4 else 2 for s in range(16)]
RSUM = [0]
for _s in range(32):
    RSUM.append(RSUM[-1] + ROUNDS[_s % 16])
RPAIR = RSUM[16]


def wait(eng, sem, value):
    if not isinstance(value, int) or value > 0:
        eng.wait_ge(sem, value)


def hybrid_block(nc, x, norm1_g, w_in, b_forget, pool_mix, pool_scale, w_pool_out, w_attn_out,
                 w_out, norm2_g, w_gate, w_up, w_down, norm_f_g, out):
    f32, f32r = mybir.dt.float32, mybir.dt.float32r
    ACT, ALU, AX = mybir.ActivationFunctionType, mybir.AluOpType, mybir.AxisListType

    x_d = x[0].rearrange("(t p) d -> t p d", p=P)
    out_d = out[0].rearrange("(t p) d -> t p d", p=P)
    win_d = w_in[0].rearrange("(k p) m -> p k m", p=P)
    wpool_d = w_pool_out[0].rearrange("(k p) m -> p k m", p=P)
    wattn_d = w_attn_out[0].rearrange("(k p) m -> p k m", p=P)
    wout_d = w_out[0].rearrange("(k p) m -> k p m", p=P)
    wgate_d = w_gate[0].rearrange("(k p) m -> p k m", p=P)
    wup_d = w_up[0].rearrange("(k p) m -> p k m", p=P)
    wdown_d = w_down[0].rearrange("(k p) m -> k p m", p=P)
    mix_d = pool_mix[0].rearrange("g c d -> c g d")
    scale_d = pool_scale[0].rearrange("(g c) -> g c", c=P)
    frow_q = nc.dram_tensor("frow_q", (NH, 4, S), f32, kind="Internal").ap()
    frow_k = nc.dram_tensor("frow_k", (NH, 4, S), f32, kind="Internal").ap()
    at_d = nc.dram_tensor("at_d", (NH, DH, S), f32, kind="Internal").ap()
    at_rows = at_d.rearrange("h d t -> (h d) t")
    x2_d = nc.dram_tensor("x2_d", (NT, P, D), f32, kind="Internal").ap()

    ctx = ExitStack()
    with ctx:
        base = -(-nc.sbuf_base // 32) * 32
        slab_words = (nc.sbuf_usable_end - base) // 4 // 8 * 8 - 16
        ctx.enter_context(nc.sbuf_tensor("slab", [P, slab_words], f32))
        end = base + slab_words * 4
        at = [base]

        def place(name, shape, dt=f32):
            n = 4
            for d in shape[1:]:
                n *= d
            t = nc.alloc_sbuf_tensor_at(name, shape, dt, offset=at[0])
            at[0] += -(-n // 32) * 32
            assert at[0] <= end, (name, at[0] - end)
            return t

        w_raw = [place(f"w_raw{i}", [P, 1024]) for i in range(2)]
        w_hi = [place(f"w_hi{i}", [P, 1024], f32r) for i in range(2)]
        w_lo = [place(f"w_lo{i}", [P, 1024], f32r) for i in range(2)]
        h_hi = place("h_hi", [P, KD, S], f32r)
        h_lo = place("h_lo", [P, KD, S], f32r)
        gain = place("gain", [P, D])
        ident = place("ident", [P, P])
        ident_r = place("ident_r", [P, P], f32r)
        mask_f = place("mask_f", [P, P])
        mask_r = place("mask_r", [P, P], f32r)
        tri = place("tri", [P, P])
        ones = place("ones", [P, P])
        neg_half = place("neg_half", [P, 1])
        ssq = place("ssq", [P, 24])
        var = place("var", [P, 24])
        rstd = place("rstd", [P, 24])
        negmax = [place(f"negmax{i}", [P, 1]) for i in range(2)]
        rowsum = [place(f"rowsum{i}", [P, 1]) for i in range(2)]
        rowinv = [place(f"rowinv{i}", [P, 1]) for i in range(2)]
        pscale = place("pscale", [P, NG])
        inv_cnt = place("inv_cnt", [P, 16])
        phase = at[0]

        v_raw = place("v_raw", [P, NT, BW])
        after_v = at[0]
        xt = [place(f"xt{i}", [P, D]) for i in range(2)]
        xn = [place(f"xn{i}", [P, D]) for i in range(2)]
        wv_raw = place("wv_raw", [P, KD, VF])
        wv_hi = place("wv_hi", [P, KD, VF], f32r)
        wv_lo = place("wv_lo", [P, KD, VF], f32r)
        hs_hi = [place(f"hs_hi{i}", [P, KD, P], f32r) for i in range(2)]
        hs_lo = [place(f"hs_lo{i}", [P, KD, P], f32r) for i in range(2)]
        f_hi = place("f_hi", [NH, 2, S])
        f_neg = place("f_neg", [NH, 2, S])
        f_one = place("f_one", [NH, 2, S])
        fz = place("fz", [P, NT, NH])
        fa = place("fa", [P, NT, NH])
        fe = place("fe", [P, NT, NH])
        fl = place("fl", [P, NT, NH])
        fbias = place("fbias", [P, NH])
        at[0] = after_v
        vs = [place(f"vs{i}", [P, NT, 2 * DH], f32r) for i in range(2)]
        at_st = [place(f"at_st{i}", [DH, HALF]) for i in range(2)]
        q1 = [place(f"q1_{i}", [P, S], f32r) for i in range(2)]
        q2 = [place(f"q2_{i}", [P, S], f32r) for i in range(2)]
        k1 = [place(f"k1_{i}", [P, S], f32r) for i in range(2)]
        k2 = [place(f"k2_{i}", [P, S], f32r) for i in range(2)]
        q_raw = place("q_raw", [P, S])
        k_raw = place("k_raw", [P, S])
        p_raw = place("p_raw", [P, S])
        p_hi = [place(f"p_hi{i}", [P, S], f32r) for i in range(2)]
        p_lo = [place(f"p_lo{i}", [P, S], f32r) for i in range(2)]
        pt_hi = place("pt_hi", [P, NT, HALF], f32r)
        pt_lo = place("pt_lo", [P, NT, HALF], f32r)
        pv_tmp = place("pv_tmp", [DH, HALF])
        at[0] = phase
        a_hi = place("a_hi", [P, NG, S], f32r)
        a_lo = place("a_lo", [P, NG, S], f32r)
        pp_hi = place("pp_hi", [P, NG, S], f32r)
        pp_lo = place("pp_lo", [P, NG, S], f32r)
        after_branches = at[0]
        u_sb = [place(f"u_sb{i}", [P, S]) for i in range(2)]
        win = [place(f"win{i}", [P, S]) for i in range(2)]
        pool = place("pool", [P, S])
        head_tmp = place("head_tmp", [P, 16])
        pool_hi = [place(f"pool_hi{i}", [P, S], f32r) for i in range(2)]
        pool_lo = [place(f"pool_lo{i}", [P, S], f32r) for i in range(2)]
        mix_raw = place("mix_raw", [P, NG, P])
        mix_hi = place("mix_hi", [P, NG, P], f32r)
        mix_lo = place("mix_lo", [P, NG, P], f32r)
        a_raw = [place(f"a_raw{i}", [P, S]) for i in range(2)]
        at[0] = after_branches
        merged = place("merged", [P, KD, S])
        sig_p = place("sig_p", [P, S])
        sig_a = place("sig_a", [P, S])
        after_merged = at[0]
        at[0] = phase
        x2 = place("x2", [P, NT, D])
        xn2 = place("xn2", [P, NT, D])
        assert at[0] <= after_branches
        at[0] = after_merged
        le_hi = [place(f"le_hi{i}", [P, HALF], f32r) for i in range(2)]
        le_lo = [place(f"le_lo{i}", [P, HALF], f32r) for i in range(2)]
        junk_e = place("junk_e", [P, D])
        at[0] = phase
        prod = place("prod", [P, KF, S])
        after_prod = at[0]
        sig_g = [place(f"sig_g{i}", [P, HALF]) for i in range(2)]
        silu = [place(f"silu{i}", [P, HALF]) for i in range(2)]
        at[0] = after_prod
        lg_hi = [place(f"lg_hi{i}", [P, HALF], f32r) for i in range(2)]
        lg_lo = [place(f"lg_lo{i}", [P, HALF], f32r) for i in range(2)]
        y = place("y", [P, 4, D])
        y_out = [place(f"y_out{i}", [P, D]) for i in range(2)]
        junk_g = place("junk_g", [P, D])

        ps = ctx.enter_context(nc.psum_tensor("ps", [P, 8, HALF], f32))
        ps_flat = ps[:].rearrange("p b n -> p (b n)")

        def sem(name):
            return ctx.enter_context(nc.semaphore(name))

        s_wraw = [sem(f"s_wraw{i}") for i in range(2)]
        s_whi, s_wlo = sem("s_whi"), sem("s_wlo")
        s_gain = sem("s_gain")
        s_const = sem("s_const")
        s_cid = sem("s_cid")
        s_x = [sem(f"s_x{i}") for i in range(2)]
        s_wv = [sem(f"s_wv{i}") for i in range(4)]
        s_wvhi, s_wvlo = sem("s_wvhi"), sem("s_wvlo")
        s_fb = sem("s_fb")
        s_sq, s_var, s_rstd = sem("s_sq"), sem("s_var"), sem("s_rstd")
        s_xn = sem("s_xn")
        s_tp = sem("s_tp")
        s_hshi, s_hthi = sem("s_hshi"), sem("s_hthi")
        s_hslo, s_htlo = sem("s_hslo"), sem("s_htlo")
        s_v = sem("s_v")
        s_vev_a, s_vev_d = sem("s_vev_a"), sem("s_vev_d")
        s_fz, s_fa, s_fcum, s_frow = sem("s_fz"), sem("s_fa"), sem("s_fcum"), sem("s_frow")
        s_fhi, s_flo = sem("s_fhi"), sem("s_flo")
        s_fst = sem("s_fst")
        s_pj, s_pjev = sem("s_pj"), sem("s_pjev")
        s_sta, s_std, s_stp = sem("s_sta"), sem("s_std"), sem("s_stp")
        s_frd = [sem(f"s_frd{i}") for i in range(2)]
        s_z = sem("s_z")
        s_vshi, s_vslo = sem("s_vshi"), sem("s_vslo")
        s_s, s_mx, s_exp, s_rc = sem("s_s"), sem("s_mx"), sem("s_exp"), sem("s_rc")
        s_phi, s_plo = sem("s_phi"), sem("s_plo")
        s_th, s_tl = sem("s_th"), sem("s_tl")
        s_evh, s_evl = sem("s_evh"), sem("s_evl")
        s_pv, s_pvt, s_pvev = sem("s_pv"), sem("s_pvt"), sem("s_pvev")
        s_atst = [sem(f"s_atst{i}") for i in range(2)]
        s_u, s_uev = sem("s_u"), sem("s_uev")
        s_dve = sem("s_dve")
        s_pool, s_plh, s_pll = sem("s_pool"), sem("s_plh"), sem("s_pll")
        s_mixw, s_mixhi, s_mixlo = sem("s_mixw"), sem("s_mixhi"), sem("s_mixlo")
        s_mix, s_pph, s_ppl = sem("s_mix"), sem("s_pph"), sem("s_ppl")
        s_araw = [sem(f"s_araw{i}") for i in range(2)]
        s_ahi, s_alo = sem("s_ahi"), sem("s_alo")
        s_gp, s_ga, s_py, s_ay = sem("s_gp"), sem("s_ga"), sem("s_py"), sem("s_ay")
        s_sgp, s_sga, s_mul, s_mrg = sem("s_sgp"), sem("s_sga"), sem("s_mul"), sem("s_mrg")
        s_lhi, s_llo = sem("s_lhi"), sem("s_llo")
        s_kused, s_tile = sem("s_kused"), sem("s_tile")
        s_add = sem("s_add")
        s_xr = sem("s_xr")
        s_x2st = sem("s_x2st")
        s_xn2, s_tp2, s_h2hi, s_h2lo = sem("s_xn2"), sem("s_tp2"), sem("s_h2hi"), sem("s_h2lo")
        s_fg, s_fu, s_sig, s_silu, s_prod = sem("s_fg"), sem("s_fu"), sem("s_sig"), sem("s_silu"), sem("s_prod")
        s_yld = sem("s_yld")
        s_yn = sem("s_yn")
        s_out = [sem(f"s_out{i}") for i in range(2)]

        block = ctx.enter_context(nc.Block())

        @block.sync
        def _(sp):
            def load_chunk(c, dc, src0, src1):
                wait(sp, s_wlo, c - 1 + dc)
                sp.dma_start(w_raw[c % 2][:, 0:512], src0).then_inc(s_wraw[c % 2], 16)
                sp.dma_start(w_raw[c % 2][:, 512:1024], src1).then_inc(s_wraw[c % 2], 16)

            def load_cols(c, dc, w, col):
                wait(sp, s_wlo, c - 1 + dc)
                for j in range(2):
                    sp.dma_start(w_raw[c % 2][:, 512 * j:512 * j + 512].rearrange("p (k m) -> p k m", m=P),
                                 w[:, 4 * j:4 * j + 4, bass.ds(col, P)]).then_inc(s_wraw[c % 2], 16)

            def load_x(j, u):
                wait(sp, s_xn, 2 * j + u - 1)
                sp.dma_start(xt[u][:], x_d[2 * j + u]).then_inc(s_x[u], 16)

            load_x(0, 0)
            sp.dma_start(gain[:], norm1_g[0].partition_broadcast(P)).then_inc(s_gain, 16)
            load_x(0, 1)
            for i in range(4):
                sp.dma_start(wv_raw[:, 2 * i:2 * i + 2, :],
                             win_d[:, 2 * i:2 * i + 2, COL_V:COL_V + VF]).then_inc(s_wv[i], 16)
            sp.dma_start(fbias[:], b_forget[0].partition_broadcast(P)).then_inc(s_fb, 16)
            load_cols(0, 0, win_d, COL_Q)
            load_cols(1, 0, win_d, COL_K)
            for j in range(1, 4):
                for u in range(2):
                    load_x(j, u)
            load_cols(2, 0, win_d, COL_Q + P)
            load_cols(3, 0, win_d, COL_K + P)

            wait(sp, s_flo, 4)
            wait(sp, s_fhi, 4)
            wait(sp, s_const, 6)
            sp.dma_start(frow_q[:, 0:2, :], f_hi[:]).then_inc(s_fst, 16)
            sp.dma_start(frow_q[:, 2:4, :], f_one[:]).then_inc(s_fst, 16)
            sp.dma_start(frow_k[:, 0:2, :], f_one[:]).then_inc(s_fst, 16)
            sp.dma_start(frow_k[:, 2:4, :], f_neg[:]).then_inc(s_fst, 16)
            wait(sp, s_fst, 64)

            def load_frows(p, e):
                r0 = DH * (1 - e)
                sp.dma_start(q2[e][r0:r0 + 4, :].bitcast(f32), frow_q[2 * p + e]).then_inc(s_frd[e], 16)
                sp.dma_start(k2[e][r0:r0 + 4, :].bitcast(f32), frow_k[2 * p + e]).then_inc(s_frd[e], 16)

            def store_at(p, g4):
                wait(sp, s_pvev, 4 * p + g4 + 1)
                sp.dma_start(at_d[2 * p + g4 // 2, :, HALF * (g4 % 2):HALF * (g4 % 2) + HALF],
                             at_st[g4 % 2][:]).then_inc(s_atst[g4 % 2], 16)

            wait(sp, s_z, 4)
            load_frows(0, 0)
            for p in range(4):
                for j, col in ((0, COL_Q), (1, COL_K)):
                    if p < 2:
                        load_cols(2 * p + 4 + j, 0, win_d, col + P * (p + 2))
                    elif p == 2:
                        load_cols(C_U + j, 0, win_d, COL_U + P * (3 - j))
                wait(sp, s_s, 16 * p)
                load_frows(p, 1)
                store_at(p, 0)
                if p < 3:
                    wait(sp, s_s, 16 * p + 8)
                    load_frows(p + 1, 0)
                for g4 in range(1, 4):
                    store_at(p, g4)

            wait(sp, s_atst[0], 16 * 8)
            wait(sp, s_atst[1], 16 * 8)
            wait(sp, s_pvev, 16)
            sp.dma_start(mix_raw[:], mix_d).then_inc(s_mixw, 16)
            for g in range(NG):
                sp.dma_start(pscale[:, g:g + 1], scale_d[g].rearrange("(c o) -> c o", o=1),
                             allow_slow_non_contiguous=True).then_inc(s_mixw, 16)
            for n in range(2):
                sp.dma_start(a_raw[n][:], at_rows[P * n:P * n + P, :]).then_inc(s_araw[n], 16)
            load_cols(C_U + 2, 0, win_d, COL_U + P)
            load_cols(C_U + 3, 0, win_d, COL_U)
            for n in range(2, 4):
                wait(sp, s_alo, n - 1)
                sp.dma_start(a_raw[n % 2][:], at_rows[P * n:P * n + P, :]).then_inc(s_araw[n % 2], 16)

            with sp.Fori(1, KD // 2 + 1) as j:
                for u in range(2):
                    c, dc, m = C_GATE + 3 * u, 6 * j - 6, 2 * j + (u - 2)
                    load_cols(c, dc, win_d, COL_GP + m * P)
                    load_cols(c + 1, dc, win_d, COL_GA + m * P)
                    wait(sp, s_wlo, c + 1 + dc)
                    for i, w in enumerate((wpool_d, wattn_d)):
                        sp.dma_start(w_raw[c % 2][:, 512 * i:512 * i + 512].rearrange("p (k m) -> p k m", m=P),
                                     w[:, :, bass.ds(2 * P * j + P * (u - 2), P)]).then_inc(s_wraw[c % 2], 16)

            def rows_chunk(c, dc, w, k):
                load_chunk(c, dc, w[k, :, 0:512], w[k, :, 512:1024])

            rows_chunk(C_OUT, 0, wout_d, 0)
            rows_chunk(C_OUT + 1, 0, wout_d, 1)
            wait(sp, s_py, 2 * KD)
            wait(sp, s_ay, 2 * KD)
            sp.dma_start(gain[:], norm2_g[0].partition_broadcast(P)).then_inc(s_gain, 16)
            for t in range(NT):
                sp.dma_start(x2[:, t, :], x_d[t]).then_inc(s_xr, 16)
            for hh in range(2):
                for k in range(2 if hh == 0 else 0, KD):
                    rows_chunk(C_OUT + KD * hh + k, 0, wout_d, k)
            load_cols(C_FFN, 0, wgate_d, 0)
            load_cols(C_FFN + 1, 0, wup_d, 0)
            for t in range(NT):
                wait(sp, s_add, 2 * (t + 1))
                sp.dma_start(x2_d[t], x2[:, t, :]).then_inc(s_x2st, 16)

            with sp.Fori(1, KF) as m:
                load_cols(C_FFN, 2 * m, wgate_d, m * P)
                load_cols(C_FFN + 1, 2 * m, wup_d, m * P)
            wait(sp, s_xn2, NT)
            sp.dma_start(gain[:], norm_f_g.partition_broadcast(P)).then_inc(s_gain, 16)

            def down_chunks(j0, j1, hh):
                with sp.Fori(j0, j1) as j:
                    for u in range(2):
                        rows_chunk(C_DOWN + KF * hh + u, 2 * j, wdown_d, 2 * j + u)

            down_chunks(0, KF // 2 - 3, 0)
            wait(sp, s_x2st, 16 * NT)
            wait(sp, s_prod, 2 * KF)
            for tt in range(4):
                sp.dma_start(y[:, tt, :], x2_d[tt]).then_inc(s_yld, 16)
            down_chunks(KF // 2 - 3, KF // 2, 0)
            down_chunks(0, KF // 2, 1)
            wait(sp, s_out[0], 16 * 4)
            wait(sp, s_out[1], 16 * 4)

        @block.gpsimd
        def _(pool):
            g = nc.gpsimd

            def w_low(c, dc=0):
                wait(pool, s_whi, c + 1 + dc)
                g.tensor_tensor(w_lo[c % 2][:], w_raw[c % 2][:], w_hi[c % 2][:].bitcast(f32),
                                ALU.subtract).then_inc(s_wlo, 1)

            def inv_root(n, col):
                wait(pool, s_var, n + 1)
                g.tensor_tensor(rstd[:, bass.ds(col, 1)], var[:, bass.ds(col, 1)], neg_half[:],
                                ALU.pow).then_inc(s_rstd, 1)

            g.memset(neg_half[:], -0.5).then_inc(s_cid, 1)
            g.memset(ident[:], 0.0).then_inc(s_cid, 1)
            pool.wait_ge(s_cid, 2)
            g.affine_select(out=ident[:], in_=ident[:], compare_op=ALU.not_equal, fill=1.0, base=0,
                            pattern=[[-1, P]], channel_multiplier=1).then_inc(s_const, 1)
            inv_root(0, 0)
            inv_root(1, 1)
            g.memset(mask_f[:], 0.0).then_inc(s_cid, 1)
            g.memset(tri[:], 1.0).then_inc(s_cid, 1)
            g.memset(ones[:], 1.0).then_inc(s_const, 1)
            g.memset(f_one[:], 1.0).then_inc(s_const, 1)
            pool.wait_ge(s_cid, 4)
            g.affine_select(out=mask_f[:], in_=mask_f[:], compare_op=ALU.is_ge, fill=NEG, base=0,
                            pattern=[[-1, P]], channel_multiplier=1).then_inc(s_const, 1)
            g.affine_select(out=tri[:], in_=tri[:], compare_op=ALU.is_ge, fill=0.0, base=0,
                            pattern=[[1, P]], channel_multiplier=-1).then_inc(s_const, 1)
            for t in range(16):
                last = g.memset(inv_cnt[:, t:t + 1], 1.0 / (t + 1))
            last.then_inc(s_const, 1)
            for n in range(2, NT):
                inv_root(n, n)
            w_low(0)
            w_low(1)

            def stack_low(p, e):
                r = slice(DH * e, DH * e + DH)
                wait(pool, s_std, 3 * (2 * p + e) + 2)
                wait(pool, s_z, 4)
                if not isinstance(p, int) or 2 * p + e > 1:
                    wait(pool, s_s, 16 * p + (0 if e else -8))
                g.tensor_tensor(k2[e][r, :], k_raw[r, :], k1[e][r, :].bitcast(f32),
                                ALU.subtract).then_inc(s_stp, 1)
                wait(pool, s_stp, 2 * p + e + 1)

            def v_low(p, e):
                wait(pool, s_vshi, 2 * p + e + 1)
                g.tensor_tensor(vs[e][:, :, DH:2 * DH], v_raw[:, :, bass.ds((2 * p + e) * DH, DH)],
                                vs[e][:, :, 0:DH].bitcast(f32), ALU.subtract).then_inc(s_vslo, 1)

            wait(pool, s_fst, 64)
            for e in range(2):
                r = slice(DH * (1 - e), DH * (1 - e) + DH)
                g.memset(q2[e][r, :].bitcast(f32), 0.0).then_inc(s_z, 1)
                g.memset(k2[e][r, :].bitcast(f32), 0.0).then_inc(s_z, 1)
            pool.wait_ge(s_z, 4)
            v_low(0, 0)
            w_low(2)
            w_low(3)
            stack_low(0, 0)

            def attention(p, last):
                stack_low(p, 1)
                v_low(p, 1)
                if not last:
                    w_low(4, 2 * p)
                    v_low(p + 1, 0)
                    w_low(5, 2 * p)
                    stack_low(p + 1, 0)

            attention(0, False)
            with pool.Fori(1, 3) as p:
                attention(p, False)
            attention(3, True)

            wait(pool, s_mixhi, 1)
            g.tensor_tensor(mix_lo[:], mix_raw[:], mix_hi[:].bitcast(f32), ALU.subtract).then_inc(s_mixlo, 1)

            def a_low(n):
                wait(pool, s_ahi, n + 1)
                g.tensor_tensor(a_lo[:, n, :], a_raw[n % 2][:], a_hi[:, n, :].bitcast(f32),
                                ALU.subtract).then_inc(s_alo, 1)

            for n in range(NG):
                w_low(C_U + 2 + n)
                a_low(n)
            with pool.Fori(0, KD // 2) as j:
                for i in range(6):
                    w_low(C_GATE + 2 + i, 6 * j)
            for c in range(C_OUT + 2, C_FFN):
                w_low(c)
                if c - C_OUT - 2 >= 8 and c - C_OUT - 2 < 12:
                    inv_root(c - C_OUT - 2, c - C_OUT - 2)
            for n in range(4):
                inv_root(12 + n, 12 + n)
                if n < 2:
                    w_low(C_FFN + n)
            with pool.Fori(0, KF) as m:
                w_low(C_FFN + 2, 2 * m)
                w_low(C_FFN + 3, 2 * m)
            w_low(C_DOWN + 2)
            w_low(C_DOWN + 3)
            with pool.Fori(0, KF // 2 - 1) as j:
                w_low(C_DOWN + 4, 2 * j)
                w_low(C_DOWN + 5, 2 * j)
            for n in range(4):
                w_low(C_DOWN + KF + 2 + n)
                inv_root(16 + n, 16 + n)
            with pool.Fori(0, (KF - 6) // 2) as j:
                w_low(C_DOWN + KF + 6, 2 * j)
                w_low(C_DOWN + KF + 7, 2 * j)
            for n in range(4, 8):
                inv_root(16 + n, 16 + n)

        @block.scalar
        def _(act):
            a = nc.scalar

            def w_high(c, dc=0):
                wait(act, s_wraw[c % 2], 32 * (c // 2 + 1) + 16 * dc)
                a.activation(w_hi[c % 2][:], w_raw[c % 2][:], ACT.Copy).then_inc(s_whi, 1)

            def square(j, u):
                wait(act, s_x[u], 16 * (j + 1))
                wait(act, s_tp, 2 * (2 * j + u - 1))
                a.activation(xn[u][:], xt[u][:], ACT.Square,
                             accum_out=ssq[:, bass.ds(2 * j + u, 1)]).then_inc(s_sq, 1)

            def high_h(j, u):
                t = 2 * j + u
                wait(act, s_v, t - 1)
                for b in range(2):
                    wait(act, s_tp, 2 * t + b + 1)
                    src = ps[:, 2 * u + b, :].rearrange("p (k n) -> p k n", n=P)
                    a.activation(hs_hi[u][:, 4 * b:4 * b + 4, :], src, ACT.Copy).then_inc(s_hshi, 1)
                    a.activation(h_hi[:, 4 * b:4 * b + 4, bass.ds(t * P, P)], src, ACT.Copy).then_inc(s_hthi, 1)

            def evac_v(j, u):
                t = 2 * j + u
                wait(act, s_v, t + 1)
                a.activation(v_raw[:, bass.ds(t, 1), 0:VH],
                             ps[:, 4 + 2 * u, 0:VH].rearrange("p (o n) -> p o n", o=1),
                             ACT.Copy).then_inc(s_vev_a, 1)

            square(0, 0)
            square(0, 1)
            for i in range(4):
                act.wait_ge(s_wv[i], 16)
                a.activation(wv_hi[:, 2 * i:2 * i + 2, :], wv_raw[:, 2 * i:2 * i + 2, :],
                             ACT.Copy).then_inc(s_wvhi, 1)
            high_h(0, 0)

            def stage_a(j):
                square(j + 1, 0)
                high_h(j, 1)
                evac_v(j, 0)
                square(j + 1, 1)
                high_h(j + 1, 0)
                evac_v(j, 1)

            stage_a(0)
            with act.Fori(1, 3) as j:
                stage_a(j)
            w_high(0)
            w_high(1)
            high_h(3, 1)
            evac_v(3, 0)
            evac_v(3, 1)

            act.wait_ge(s_fz, 3)
            a.activation(fe[:], fa[:], ACT.Exp, scale=-1.0).then_inc(s_fa, 1)
            act.wait_ge(s_fa, 1)
            a.activation(fl[:], fe[:], ACT.Ln, bias=1.0).then_inc(s_fa, 1)

            def evac_qk(p, n, bank):
                wait(act, s_pj, 4 * p + n + 1)
                dst = (q_raw, k_raw)[n // 2]
                a.activation(dst[:, HALF * (n % 2):HALF * (n % 2) + HALF], ps[:, bank, :], ACT.Copy,
                             scale=(DH ** -0.5 if n < 2 else 1.0)).then_inc(s_pjev, 1)

            def stack_high(p, e):
                r = slice(DH * e, DH * e + DH)
                wait(act, s_pjev, 4 * (p + 1))
                wait(act, s_s, 16 * p + (0 if e else -8))
                a.activation(q2[e][r, :], q_raw[r, :], ACT.Copy).then_inc(s_sta, 1)
                a.activation(q1[e][r, :], q_raw[r, :], ACT.Copy).then_inc(s_sta, 1)

            def v_high(p, e):
                wait(act, s_pv, 4 * p + (0 if e else -2))
                a.activation(vs[e][:, :, 0:DH], v_raw[:, :, bass.ds((2 * p + e) * DH, DH)],
                             ACT.Copy).then_inc(s_vshi, 1)

            def softmax_exp(p, s):
                n = ((s % 8) + 1) * P
                wait(act, s_mx, 16 * p + s + 1)
                wait(act, s_plo, 16 * p + s)
                wait(act, s_rc, 16 * p + s - 1)
                b = 1024 * (s % 2)
                a.activation(p_raw[:, 0:n], ps_flat[:, b:b + n], ACT.Exp, bias=negmax[s % 2][:],
                             accum_out=rowsum[s % 2][:]).then_inc(s_exp, 1)

            def p_high(p, s):
                n = ((s % 8) + 1) * P
                wait(act, s_rc, 16 * p + s + 1)
                wait(act, s_exp, 16 * p + s + 1)
                wait(act, s_th, RPAIR * p + RSUM[s - 1] if s > 0 else RPAIR * p - ROUNDS[15])
                a.activation(p_hi[s % 2][:, 0:n], p_raw[:, 0:n], ACT.Copy,
                             scale=rowinv[s % 2][:]).then_inc(s_phi, 1)

            def evac_t(p, s):
                i = s % 8
                if i % 4 == 0:
                    wait(act, s_pv, 4 * p + s // 4)
                for r in range(ROUNDS[s]):
                    n = min(4, i + 1 - 4 * r)
                    wait(act, s_th, RPAIR * p + RSUM[s] + r + 1)
                    a.activation(pt_hi[:, 4 * r:4 * r + n, (i % 4) * P:(i % 4) * P + P],
                                 ps[:, 4, 0:n * P].rearrange("p (k n) -> p k n", n=P),
                                 ACT.Copy).then_inc(s_evh, 1)

            def evac_pv(p, g4):
                wait(act, s_pv, 4 * p + g4 + 1)
                wait(act, s_pvev, 4 * p + g4)
                a.activation(pv_tmp[:], ps[DH:2 * DH, 6, :], ACT.Copy).then_inc(s_pvt, 1)

            def f_high(b):
                act.wait_ge(s_frow, b + 1)
                a.activation(f_hi[:, 0, HALF * b:HALF * b + HALF].bitcast(f32r),
                             ps[0:NH, 1 + b, :], ACT.Copy).then_inc(s_fhi, 1)
                act.wait_ge(s_fhi, 2 * b + 1)
                a.activation(f_neg[:, 0, HALF * b:HALF * b + HALF],
                             f_hi[:, 0, HALF * b:HALF * b + HALF], ACT.Copy, scale=-1.0).then_inc(s_fhi, 1)

            f_high(0)
            f_high(1)
            act.wait_ge(s_fst, 64)
            v_high(0, 0)
            for n in range(4):
                evac_qk(0, n, 7 - n)
                if n % 2:
                    w_high(2 + n // 2)
            act.wait_ge(s_z, 4)
            stack_high(0, 0)
            softmax_exp(0, 0)
            p_high(0, 0)
            softmax_exp(0, 1)

            def attention(p, last):
                for s in range(16):
                    if s == 0:
                        stack_high(p, 1)
                    if s < 15 or not last:
                        p_high(p, s + 1)
                    evac_t(p, s)
                    if s < 14 or not last:
                        softmax_exp(p, s + 2)
                    if s in (4, 8, 12):
                        evac_pv(p, s // 4 - 1)
                    if s == 1:
                        v_high(p, 1)
                    if last:
                        continue
                    if s < 12 and s % 3 == 2:
                        if s == 2:
                            wait(act, s_std, 3 * (2 * p + 2))
                            wait(act, s_stp, 2 * p + 2)
                        evac_qk(p + 1, s // 3, 7)
                        if s % 6 == 5:
                            w_high(4 + s // 6, 2 * p)
                    if s == 9:
                        v_high(p + 1, 0)
                    if s == 11:
                        stack_high(p + 1, 0)
                evac_pv(p, 3)

            attention(0, False)
            with act.Fori(1, 3) as p:
                attention(p, False)
            attention(3, True)

            act.wait_ge(s_mixw, 16 * (1 + NG))
            a.activation(mix_hi[:], mix_raw[:], ACT.Copy).then_inc(s_mixhi, 1)

            def a_high(n):
                wait(act, s_araw[n % 2], 16 * (n // 2 + 1))
                a.activation(a_hi[:, n, :], a_raw[n % 2][:], ACT.Copy).then_inc(s_ahi, 1)

            def pool_high(n):
                wait(act, s_pool, n + 1)
                wait(act, s_mix, 2 * (n - 1))
                a.activation(pool_hi[n % 2][:], pool[:], ACT.Copy).then_inc(s_plh, 1)

            def pp_high(n):
                g = NG - 1 - n
                for b in range(2):
                    wait(act, s_mix, 2 * n + b + 1)
                    a.activation(pp_hi[:, g, HALF * b:HALF * b + HALF], ps[:, 4 + 2 * (n % 2) + b, :], ACT.Copy,
                                 scale=pscale[:, g:g + 1]).then_inc(s_pph, 1)

            for n in range(NG):
                for b in range(2):
                    wait(act, s_u, 2 * n + b + 1)
                    wait(act, s_pool, n - 1)
                    a.activation(u_sb[n % 2][:, HALF * b:HALF * b + HALF], ps[:, 2 * (n % 2) + b, :],
                                 ACT.Copy).then_inc(s_uev, 1)
                w_high(C_U + 2 + n)
                a_high(n)
                if n:
                    pp_high(n - 1)
                pool_high(n)
            pp_high(NG - 1)

            def gates(j):
                for u in range(2):
                    m = 2 * j + u
                    for s_in, s_done, dst, bank in ((s_gp, s_sgp, sig_p, 0), (s_ga, s_sga, sig_a, 2)):
                        for b in range(2):
                            wait(act, s_in, 2 * m + b + 1)
                            if b == 0:
                                wait(act, s_mrg, m)
                            a.activation(dst[:, HALF * b:HALF * b + HALF], ps[:, bank + b, :],
                                         ACT.Sigmoid).then_inc(s_done, 1)
                        w_high(C_GATE + 2 + 3 * u + bank // 2, 6 * j)
                    wait(act, s_ay, 2 * m + 2)
                    w_high(C_GATE + 4 + 3 * u, 6 * j)

            gates(0)
            with act.Fori(1, KD // 2) as j:
                gates(j)

            def left_high(n, src, k, hh, dst):
                a.activation(dst[n % 2][:], src[:, k, HALF * hh:HALF * hh + HALF] if isinstance(k, int)
                             else src[:, bass.ds(k, 1), HALF * hh:HALF * hh + HALF].rearrange("p o n -> p (o n)"),
                             ACT.Copy).then_inc(s_lhi, 1)

            def norm_square(n, src, junk):
                wait(act, s_sq, n)
                a.activation(junk[:], src, ACT.Square, accum_out=ssq[:, n:n + 1]).then_inc(s_sq, 1)

            act.wait_ge(s_mrg, KD)
            left_high(0, merged, 0, 0, le_hi)
            left_high(1, merged, 1, 0, le_hi)
            for n in range(2 * KD):
                if n % KD == KD - 1:
                    wait(act, s_tile, 4 * (n // KD + 1))
                else:
                    wait(act, s_kused, n + 1 - n // KD)
                if n + 2 < 2 * KD:
                    left_high(n + 2, merged, (n + 2) % KD, (n + 2) // KD, le_hi)
                w_high(C_OUT + 2 + n)
                if n in (8, 9, 10, 11):
                    wait(act, s_add, 2 * (n - 7))
                    norm_square(n, x2[:, n - 8, :], junk_e)

            def h2_high(t):
                for b in range(2):
                    wait(act, s_tp2, 2 * t + b + 1)
                    a.activation(h_hi[:, 4 * b:4 * b + 4, t * P:t * P + P],
                                 ps[:, 2 * (t % 4) + b, :].rearrange("p (k n) -> p k n", n=P),
                                 ACT.Copy).then_inc(s_h2hi, 1)

            for t in range(4):
                wait(act, s_add, 2 * (5 + t))
                norm_square(12 + t, x2[:, 4 + t, :], junk_e)
                h2_high(t)
            for t in range(4, 8):
                h2_high(t)

            def ffn_gate(m, dm, b, n):
                wait(act, s_fg, 2 * m + 2 * dm + b + 1)
                wait(act, s_silu, 2 * m + 2 * dm + b - 1)
                a.activation(sig_g[b][:], ps[:, 4 * (m % 2) + b, :], ACT.Sigmoid).then_inc(s_sig, 1)

            def ffn(m, dm):
                for b in range(2):
                    ffn_gate(m, dm, b, 0)
                w_high(C_FFN + 2 + 2 * m, 2 * dm)
                wait(act, s_fu, 2 * m + 2 * dm + 2)
                w_high(C_FFN + 3 + 2 * m, 2 * dm)

            ffn(0, 0)
            ffn(1, 0)
            with act.Fori(1, KF // 2) as j:
                ffn(0, 2 * j)
                ffn(1, 2 * j)

            act.wait_ge(s_prod, 2 * KF)
            left_high(0, prod, 0, 0, lg_hi)
            left_high(1, prod, 1, 0, lg_hi)
            used0 = 2 * KD - 2

            def down(n, dn, hh, k):
                wait(act, s_kused, used0 + n + 1 - hh + dn)
                left_high(n, prod, k, hh, lg_hi)
                w_high(C_DOWN + 2 + n, dn)

            with act.Fori(0, KF // 2 - 1) as j:
                down(0, 2 * j, 0, 2 * j + 2)
                down(1, 2 * j, 0, 2 * j + 3)
            wait(act, s_kused, used0 + KF - 1)
            left_high(0, prod, 0, 1, lg_hi)
            w_high(C_DOWN + KF)
            wait(act, s_tile, 8 + 4)
            left_high(1, prod, 1, 1, lg_hi)
            w_high(C_DOWN + KF + 1)

            def store(t):
                wait(act, s_yn, t + 1)
                act.dma_start(out_d[t], y_out[t % 2][:]).then_inc(s_out[t % 2], 16)

            for i in range(6):
                down(KF + i, 0, 1, 2 + i)
                if i < 4:
                    wait(act, s_add, 16 + 2 * (i + 1))
                    norm_square(16 + i, y[:, i, :], junk_g)
                if 0 < i < 5:
                    store(i - 1)
                    act.dma_start(y[:, i - 1, :], x2_d[3 + i]).then_inc(s_yld, 16)
            with act.Fori(3, KF // 2 - 1) as j:
                down(KF, 2 * j, 1, 2 * j + 2)
                down(KF + 1, 2 * j, 1, 2 * j + 3)
            for t in range(4):
                wait(act, s_add, 16 + 2 * (5 + t))
                norm_square(20 + t, y[:, t, :], junk_g)
                if t:
                    store(3 + t)
            store(7)

        @block.vector
        def _(dve):
            v = nc.vector

            def variance(n):
                wait(dve, s_sq, n + 1)
                v.tensor_scalar(var[:, bass.ds(n, 1)], ssq[:, bass.ds(n, 1)], 1.0 / D, EPS,
                                ALU.mult, ALU.add).then_inc(s_var, 1)

            def normalise(n, dst, src, done):
                wait(dve, s_rstd, n + 1)
                v.scalar_tensor_tensor(dst, src, rstd[:, bass.ds(n, 1)], gain[:],
                                       ALU.mult, ALU.mult).then_inc(done, 1)

            def norm_x(j, u):
                variance(2 * j + u)
                wait(dve, s_tp, 2 * (2 * j + u - 1))
                normalise(2 * j + u, xn[u][:], xt[u][:], s_xn)

            def low_h(j, u):
                t = 2 * j + u
                wait(dve, s_v, t - 1)
                for b in range(2):
                    wait(dve, s_hshi, 2 * t + b + 1)
                    wait(dve, s_hthi, 2 * t + b + 1)
                    v.tensor_tensor(hs_lo[u][:, 4 * b:4 * b + 4, :],
                                    ps[:, 2 * u + b, :].rearrange("p (k n) -> p k n", n=P),
                                    hs_hi[u][:, 4 * b:4 * b + 4, :].bitcast(f32),
                                    ALU.subtract).then_inc(s_hslo, 1)
                wait(dve, s_hslo, 2 * t + 2)
                v.tensor_copy(h_lo[:, :, bass.ds(t * P, P)], hs_lo[u][:].bitcast(f32)).then_inc(s_htlo, 1)

            def evac_v(j, u):
                t = 2 * j + u
                wait(dve, s_v, t + 1)
                v.tensor_copy(v_raw[:, bass.ds(t, 1), VH:BW],
                              ps[:, 5 + 2 * u, 0:BW - VH].rearrange("p (o n) -> p o n", o=1))
                v.tensor_copy(fz[:, bass.ds(t, 1), :],
                              ps[:, 5 + 2 * u, BW - VH:VH].rearrange("p (o n) -> p o n", o=1)).then_inc(s_vev_d, 1)

            dve.wait_ge(s_gain, 16)
            norm_x(0, 0)
            norm_x(0, 1)
            for i in range(4):
                if i == 1:
                    low_h(0, 0)
                dve.wait_ge(s_wvhi, i + 1)
                v.tensor_tensor(wv_lo[:, 2 * i:2 * i + 2, :], wv_raw[:, 2 * i:2 * i + 2, :],
                                wv_hi[:, 2 * i:2 * i + 2, :].bitcast(f32), ALU.subtract).then_inc(s_wvlo, 1)

            def stage_a(j):
                norm_x(j + 1, 0)
                low_h(j, 1)
                evac_v(j, 0)
                norm_x(j + 1, 1)
                low_h(j + 1, 0)
                evac_v(j, 1)

            stage_a(0)
            with dve.Fori(1, 3) as j:
                stage_a(j)
            low_h(3, 1)
            evac_v(3, 0)
            dve.wait_ge(s_const, 6)
            v.tensor_copy(ident_r[:], ident[:]).then_inc(s_cid, 1)
            v.tensor_copy(mask_r[:], mask_f[:]).then_inc(s_cid, 1)
            evac_v(3, 1)

            dve.wait_ge(s_fb, 16)
            dve.wait_ge(s_vev_d, NT)
            v.tensor_tensor(fz[:], fz[:], fbias[:].rearrange("p (o h) -> p o h", o=1).to_broadcast([P, NT, NH]),
                            ALU.add).then_inc(s_fz, 1)
            dve.wait_ge(s_fz, 1)
            v.tensor_scalar(fa[:], fz[:], -1.0, None, ALU.mult).then_inc(s_fz, 1)
            dve.wait_ge(s_fz, 2)
            v.tensor_tensor(fa[:], fa[:], fz[:], ALU.max).then_inc(s_fz, 1)
            dve.wait_ge(s_fa, 2)
            v.scalar_tensor_tensor(fe[:], fz[:], 0.0, fl[:], ALU.min, ALU.subtract).then_inc(s_fz, 1)
            dve.wait_ge(s_fcum, 1)
            v.tensor_copy(fa[:], ps[:, 0, 0:NT * NH].rearrange("p (t h) -> p t h", h=NH)).then_inc(s_fz, 1)
            for b in range(2):
                dve.wait_ge(s_fhi, 2 * b + 2)
                dst = f_hi[:, 1, HALF * b:HALF * b + HALF]
                v.tensor_tensor(dst.bitcast(f32r), ps[0:NH, 1 + b, :], f_hi[:, 0, HALF * b:HALF * b + HALF],
                                ALU.subtract).then_inc(s_flo, 1)
                dve.wait_ge(s_flo, 2 * b + 1)
                v.tensor_scalar(f_neg[:, 1, HALF * b:HALF * b + HALF], dst, -1.0, None,
                                ALU.mult).then_inc(s_flo, 1)

            def stack_mid(p, e):
                r = slice(DH * e, DH * e + DH)
                o = slice(DH * (1 - e), DH * (1 - e) + DH)
                n = 2 * p + e
                wait(dve, s_pjev, 4 * (p + 1))
                wait(dve, s_s, 16 * p + (0 if e else -8))
                v.tensor_copy(k1[e][o, :], k_raw[r, :]).then_inc(s_std, 1)
                v.tensor_copy(k1[e][r, :], k_raw[r, :]).then_inc(s_std, 1)
                wait(dve, s_sta, 2 * n + 1)
                v.tensor_tensor(q1[e][o, :], q_raw[r, :], q2[e][r, :].bitcast(f32),
                                ALU.subtract).then_inc(s_std, 1)

            def row_max(p, s):
                n = ((s % 8) + 1) * P
                wait(dve, s_s, 16 * p + s + 1)
                wait(dve, s_exp, 16 * p + s - 1)
                b = 1024 * (s % 2)
                v.reduce_max(negmax[s % 2][:], ps_flat[:, b:b + n], axis=AX.X, negate=True).then_inc(s_mx, 1)

            def row_inv(p, s):
                wait(dve, s_exp, 16 * p + s + 1)
                wait(dve, s_phi, 16 * p + s - 1)
                v.reciprocal(rowinv[s % 2][:], rowsum[s % 2][:]).then_inc(s_rc, 1)

            def p_low(p, s):
                n = ((s % 8) + 1) * P
                wait(dve, s_phi, 16 * p + s + 1)
                wait(dve, s_rc, 16 * p + s + 1)
                wait(dve, s_tl, RPAIR * p + RSUM[s - 1] if s > 0 else RPAIR * p - ROUNDS[15])
                v.scalar_tensor_tensor(p_lo[s % 2][:, 0:n], p_raw[:, 0:n], rowinv[s % 2][:],
                                       p_hi[s % 2][:, 0:n].bitcast(f32), ALU.mult,
                                       ALU.subtract).then_inc(s_plo, 1)

            def evac_t(p, s):
                i = s % 8
                if i % 4 == 0:
                    wait(dve, s_pv, 4 * p + s // 4)
                for r in range(ROUNDS[s]):
                    n = min(4, i + 1 - 4 * r)
                    wait(dve, s_tl, RPAIR * p + RSUM[s] + r + 1)
                    v.tensor_copy(pt_lo[:, 4 * r:4 * r + n, (i % 4) * P:(i % 4) * P + P],
                                  ps[:, 5, 0:n * P].rearrange("p (k n) -> p k n", n=P)).then_inc(s_evl, 1)

            def evac_pv(p, g4):
                wait(dve, s_pvt, 4 * p + g4 + 1)
                wait(dve, s_atst[g4 % 2], 16 * (2 * p + g4 // 2))
                v.tensor_tensor(at_st[g4 % 2][:], ps[0:DH, 6, :], pv_tmp[:], ALU.add).then_inc(s_pvev, 1)

            dve.wait_ge(s_fst, 64)
            dve.wait_ge(s_z, 4)
            stack_mid(0, 0)
            row_max(0, 0)
            row_inv(0, 0)
            p_low(0, 0)
            row_max(0, 1)
            row_inv(0, 1)

            def attention(p, last):
                for s in range(16):
                    if s == 0:
                        stack_mid(p, 1)
                    if s < 15 or not last:
                        p_low(p, s + 1)
                    evac_t(p, s)
                    if s < 14 or not last:
                        row_max(p, s + 2)
                        row_inv(p, s + 2)
                    if s in (4, 8, 12):
                        evac_pv(p, s // 4 - 1)
                    if s == 11 and not last:
                        stack_mid(p + 1, 0)
                evac_pv(p, 3)

            attention(0, False)
            with dve.Fori(1, 3) as p:
                attention(p, False)
            attention(3, True)

            link = [0]

            def chain(ins):
                link[0] += 1
                ins.then_inc(s_dve, 1)
                dve.wait_ge(s_dve, link[0])

            def pp_low(n):
                g = NG - 1 - n
                for b in range(2):
                    wait(dve, s_pph, 2 * n + b + 1)
                    v.scalar_tensor_tensor(pp_lo[:, g, HALF * b:HALF * b + HALF],
                                           ps[:, 4 + 2 * (n % 2) + b, :], pscale[:, g:g + 1],
                                           pp_hi[:, g, HALF * b:HALF * b + HALF].bitcast(f32),
                                           ALU.mult, ALU.subtract).then_inc(s_ppl, 1)

            for n in range(NG):
                g = NG - 1 - n
                w = 2 << g
                wait(dve, s_uev, 2 * n + 2)
                u = u_sb[n % 2]
                cur = u
                for i in range(g + 1):
                    d = 1 << i
                    nxt = win[i % 2]
                    v.tensor_copy(nxt[:, 0:d], cur[:, 0:d])
                    chain(v.tensor_tensor(nxt[:, d:S], cur[:, d:S], cur[:, 0:S - d], ALU.add))
                    cur = nxt
                wait(dve, s_plh, n)
                wait(dve, s_pll, n)
                v.tensor_tensor(head_tmp[:, 0:w], cur[:, 0:w], inv_cnt[:, 0:w], ALU.mult)
                chain(v.scalar_tensor_tensor(pool[:, w:S], cur[:, w:S], 1.0 / w, u[:, w:S],
                                             ALU.mult, ALU.subtract))
                v.tensor_tensor(pool[:, 0:w], head_tmp[:, 0:w], u[:, 0:w], ALU.subtract).then_inc(s_pool, 1)
                wait(dve, s_plh, n + 1)
                wait(dve, s_mix, 2 * (n - 1))
                v.tensor_tensor(pool_lo[n % 2][:], pool[:], pool_hi[n % 2][:].bitcast(f32),
                                ALU.subtract).then_inc(s_pll, 1)
                if n:
                    pp_low(n - 1)
            pp_low(NG - 1)

            def merge(j):
                for u in range(2):
                    m = 2 * j + u
                    for s_in, s_gate, sig, bank in ((s_py, s_sgp, sig_p, 4), (s_ay, s_sga, sig_a, 6)):
                        for b in range(2):
                            wait(dve, s_gate, 2 * m + b + 1)
                            wait(dve, s_in, 2 * m + b + 1)
                            h = slice(HALF * b, HALF * b + HALF)
                            v.tensor_tensor(sig[:, h], ps[:, bank + b, :], sig[:, h], ALU.mult).then_inc(s_mul, 1)
                    wait(dve, s_mul, 4 * m + 4)
                    v.tensor_tensor(merged[:, bass.ds(m, 1), :],
                                    sig_p[:].rearrange("p (o n) -> p o n", o=1),
                                    sig_a[:].rearrange("p (o n) -> p o n", o=1), ALU.add).then_inc(s_mrg, 1)

            merge(0)
            with dve.Fori(1, KD // 2) as j:
                merge(j)

            def left_low(n, src, k, hh, hi, lo):
                s_ap = (src[:, k, HALF * hh:HALF * hh + HALF] if isinstance(k, int)
                        else src[:, bass.ds(k, 1), HALF * hh:HALF * hh + HALF].rearrange("p o n -> p (o n)"))
                v.tensor_tensor(lo[n % 2][:], s_ap, hi[n % 2][:].bitcast(f32), ALU.subtract).then_inc(s_llo, 1)

            def add_tile(t, n, dst):
                wait(dve, s_tile, n + 1)
                for f in range(2):
                    d = dst[:, HALF * f:HALF * f + HALF]
                    v.tensor_tensor(d, ps[:, 2 * (t % 4) + f, :], d, ALU.add).then_inc(s_add, 1)

            def h2_low(t):
                for b in range(2):
                    wait(dve, s_h2hi, 2 * t + b + 1)
                    hd = h_hi[:, 4 * b:4 * b + 4, t * P:t * P + P]
                    v.tensor_tensor(h_lo[:, 4 * b:4 * b + 4, t * P:t * P + P],
                                    ps[:, 2 * (t % 4) + b, :].rearrange("p (k n) -> p k n", n=P),
                                    hd.bitcast(f32), ALU.subtract).then_inc(s_h2lo, 1)

            dve.wait_ge(s_xr, 16 * NT)
            dve.wait_ge(s_gain, 32)
            for n in range(2 * KD):
                dve.wait_ge(s_lhi, n + 1)
                left_low(n, merged, n % KD, n // KD, le_hi, le_lo)
                if KD - 1 < n - 1 < KD + 4:
                    t = n - 1 - KD
                    variance(KD + t)
                    normalise(KD + t, xn2[:, t, :], x2[:, t, :], s_xn2)
                if n == KD + 1 - 2 + 0:
                    for t in range(4):
                        add_tile(t, t, x2[:, t, :])
            for t in range(4):
                add_tile(4 + t, 4 + t, x2[:, 4 + t, :])
                h2_low(t)
            for t in range(4):
                variance(12 + t)
                normalise(12 + t, xn2[:, 4 + t, :], x2[:, 4 + t, :], s_xn2)
            for t in range(4, 8):
                h2_low(t)

            def ffn(m, dm):
                for b in range(2):
                    wait(dve, s_sig, 2 * m + 2 * dm + b + 1)
                    wait(dve, s_prod, 2 * m + 2 * dm + b - 1)
                    v.tensor_tensor(silu[b][:], ps[:, 4 * (m % 2) + b, :], sig_g[b][:], ALU.mult).then_inc(s_silu, 1)
                for b in range(2):
                    wait(dve, s_fu, 2 * m + 2 * dm + b + 1)
                    wait(dve, s_silu, 2 * m + 2 * dm + b + 1)
                    v.tensor_tensor(prod[:, bass.ds(m + dm, 1), HALF * b:HALF * b + HALF],
                                    ps[:, 4 * (m % 2) + 2 + b, :].rearrange("p (o n) -> p o n", o=1),
                                    silu[b][:].rearrange("p (o n) -> p o n", o=1), ALU.mult).then_inc(s_prod, 1)

            dve.wait_ge(s_x2st, 16 * NT)
            ffn(0, 0)
            ffn(1, 0)
            with dve.Fori(1, KF // 2) as j:
                ffn(0, 2 * j)
                ffn(1, 2 * j)

            l0 = 2 * KD

            def down(n, dn, hh, k):
                wait(dve, s_lhi, l0 + n + dn + 1)
                left_low(n, prod, k, hh, lg_hi, lg_lo)

            with dve.Fori(0, KF // 2) as j:
                down(0, 2 * j, 0, 2 * j)
                down(1, 2 * j, 0, 2 * j + 1)
            down(KF, 0, 1, 0)
            dve.wait_ge(s_yld, 16 * 4)
            dve.wait_ge(s_gain, 48)
            for t in range(4):
                add_tile(t, 8 + t, y[:, t, :])
            down(KF + 1, 0, 1, 1)

            def final(n, t):
                variance(16 + n)
                wait(dve, s_out[n % 2], 16 * (n // 2))
                normalise(16 + n, y_out[n % 2][:], y[:, t, :], s_yn)

            for t in range(4):
                down(KF + 2 + t, 0, 1, 2 + t)
                final(t, t)
            with dve.Fori(3, KF // 2) as j:
                down(KF, 2 * j, 1, 2 * j)
                down(KF + 1, 2 * j, 1, 2 * j + 1)
            dve.wait_ge(s_yld, 16 * 8)
            add_tile(4, 12, y[:, 0, :])
            for t in range(4):
                if t < 3:
                    add_tile(5 + t, 13 + t, y[:, 1 + t, :])
                final(4 + t, t)

        @block.tensor
        def _(pe):
            mm = nc.tensor.matmul

            def group(bank, stats, movs, first=True, last=True):
                n = len(stats)
                for i in range(n):
                    ins = mm(bank, stats[i], movs[i], start=first and i == 0, stop=last and i == n - 1)
                return ins

            def three(wh, wl, hh, hl):
                return wh + wh + wl, hh + hl + hh

            def w_tiles(c, k0, n):
                cut = lambda t: [t[c % 2][:, P * k:P * k + P] for k in range(k0, k0 + n)]
                return cut(w_hi), cut(w_lo)

            def cols(hi, lo, b, n):
                cut = lambda t: [t[:, k, HALF * b:HALF * b + HALF] for k in range(n)]
                return cut(hi), cut(lo)

            def column_product(c, b, bank):
                return group(ps[:, bank, :], *three(*w_tiles(c, 0, KD), *cols(h_hi, h_lo, b, KD)))

            def transpose_x(j, u):
                t = 2 * j + u
                wait(pe, s_xn, t + 1)
                wait(pe, s_hthi, 2 * (t - 1))
                wait(pe, s_hslo, 2 * (t - 1))
                for b in range(2):
                    for k in range(4):
                        ins = nc.tensor.transpose(ps[:, 2 * u + b, P * k:P * k + P],
                                                  xn[u][:, (4 * b + k) * P:(4 * b + k + 1) * P], ident[:])
                    ins.then_inc(s_tp, 1)

            def v_product(j, u):
                t = 2 * j + u
                wait(pe, s_htlo, t + 1)
                wait(pe, s_hthi, 2 * t + 2)
                wait(pe, s_vev_a, t - 1)
                wait(pe, s_vev_d, t - 1)
                for k in range(KD):
                    if isinstance(t, int) and t == 0 and k % 2 == 0:
                        pe.wait_ge(s_wvlo, k // 2 + 1)
                    for i, (l, r) in enumerate(((hs_hi, wv_hi), (hs_hi, wv_lo), (hs_lo, wv_hi))):
                        for b in range(2):
                            ins = mm(ps[:, 4 + 2 * u + b, 0:VH], l[u][:, k, :], r[:, k, VH * b:VH * b + VH],
                                     start=(k == 0 and i == 0), stop=(k == KD - 1 and i == 2))
                ins.then_inc(s_v, 1)

            pe.wait_ge(s_const, 1)
            transpose_x(0, 0)

            def stage_a(j):
                transpose_x(j, 1)
                v_product(j, 0)
                transpose_x(j + 1, 0)
                v_product(j, 1)

            stage_a(0)
            with pe.Fori(1, 3) as j:
                stage_a(j)
            transpose_x(3, 1)
            v_product(3, 0)
            v_product(3, 1)

            pe.wait_ge(s_htlo, NT)
            pe.wait_ge(s_hthi, 2 * NT)
            pe.wait_ge(s_vev_a, NT)
            pe.wait_ge(s_vev_d, NT)
            for n in range(4):
                if n % 2 == 0:
                    wait(pe, s_wlo, 1 + n // 2)
                if n == 2:
                    pe.wait_ge(s_fz, 4)
                    mm(ps[:, 0, 0:NT * NH], tri[:], fe[:].rearrange("p t h -> p (t h)"), start=True, stop=False)
                    for t in range(NT - 1):
                        rest = NT - 1 - t
                        ins = mm(ps[:, 0, NH * (t + 1):NH * NT].rearrange("p (t h) -> p t h", h=NH), ones[:],
                                 fe[:, t:t + 1, :].to_broadcast([P, rest, NH]),
                                 start=False, stop=(t == NT - 2))
                    ins.then_inc(s_fcum, 1)
                column_product(n // 2, n % 2, 7 - n).then_inc(s_pj, 1)
                if n == 2:
                    pe.wait_ge(s_fz, 5)
                    for b in range(2):
                        for t in range(4):
                            ins = nc.tensor.transpose(ps[0:NH, 1 + b, P * t:P * t + P], fa[:, 4 * b + t, :], ident[:])
                        ins.then_inc(s_frow, 1)

            def scores(p, s):
                e, i = (s // 8) % 2, s % 8
                n = (i + 1) * P
                if i == 0:
                    b = 2 * p + s // 8
                    wait(pe, s_sta, 2 * (b + 1))
                    wait(pe, s_std, 3 * (b + 1))
                    wait(pe, s_stp, b + 1)
                    wait(pe, s_frd[e], 32 * (p + s // 16 + 1))
                wait(pe, s_exp, 16 * p + s - 1)
                qt = slice(i * P, i * P + P)
                for h in range(0, n, HALF):
                    w = min(HALF, n - h)
                    bank = ps[:, 2 * (s % 2) + h // HALF, :]
                    diag = h + w == n
                    mm(bank[:, 0:w], q1[e][:, qt], k1[e][:, h:h + w], start=True, stop=False)
                    ins = mm(bank[:, 0:w], q2[e][:, qt], k2[e][:, h:h + w], start=False, stop=not diag)
                    if diag:
                        ins = mm(bank[:, w - P:w], ident_r[:], mask_r[:], start=False, stop=True)
                ins.then_inc(s_s, 1)

            def transposes(p, s, r):
                i = s % 8
                n = min(4, i + 1 - 4 * r)
                for src, ready, free, done, bank in ((p_hi, s_phi, s_evh, s_th, 4), (p_lo, s_plo, s_evl, s_tl, 5)):
                    if r == 0:
                        wait(pe, ready, 16 * p + s + 1)
                    wait(pe, free, RPAIR * p + RSUM[s] + r)
                    for k in range(n):
                        ins = nc.tensor.transpose(ps[:, bank, P * k:P * k + P].bitcast(f32r),
                                                  src[s % 2][:, (4 * r + k) * P:(4 * r + k + 1) * P], ident_r[:])
                    ins.then_inc(done, 1)

            def values(p, s):
                e, g = s // 8, (s % 8) // 4
                wait(pe, s_vslo, 2 * p + e + 1)
                wait(pe, s_evh, RPAIR * p + RSUM[s + 1])
                wait(pe, s_evl, RPAIR * p + RSUM[s + 1])
                wait(pe, s_pvev, 4 * p + s // 4)
                nk = 4 * g + 4
                for x_, pt in enumerate((pt_hi, pt_lo)):
                    for k in range(nk):
                        q0 = max(0, k - 4 * g) * P
                        ins = mm(ps[:, 6, q0:HALF], vs[e][:, k, :], pt[:, k, q0:HALF],
                                 start=(x_ == 0 and k == 0), stop=(x_ == 1 and k == nk - 1))
                ins.then_inc(s_pv, 1)

            def next_pair(p, s):
                n = s // 3
                if s % 3 == 0:
                    wait(pe, s_pjev, 4 * (p + 1) + n)
                if s % 6 == 0:
                    wait(pe, s_wlo, 2 * p + 3 + s // 6)
                st, mv = three(*w_tiles(s // 6, 0, KD), *cols(h_hi, h_lo, n % 2, KD))
                part = slice(KD * (s % 3), KD * (s % 3) + KD)
                ins = group(ps[:, 7, :], st[part], mv[part], first=(s % 3 == 0), last=(s % 3 == 2))
                if s % 3 == 2:
                    ins.then_inc(s_pj, 1)

            pe.wait_ge(s_cid, 6)
            pe.wait_ge(s_flo, 4)
            pe.wait_ge(s_fhi, 4)
            scores(0, 0)
            scores(0, 1)

            def attention(p, last):
                for s in range(16):
                    if s < 12 and not last:
                        next_pair(p, s)
                    transposes(p, s, 0)
                    if s < 14 or not last:
                        scores(p, s + 2)
                    if ROUNDS[s] == 2:
                        transposes(p, s, 1)
                    if s % 4 == 3:
                        values(p, s)

            attention(0, False)
            with pe.Fori(1, 3) as p:
                attention(p, False)
            attention(3, True)

            def mix(n):
                g = NG - 1 - n
                wait(pe, s_mixlo, 1)
                wait(pe, s_plh, n + 1)
                wait(pe, s_pll, n + 1)
                wait(pe, s_pph, 2 * (n - 1))
                wait(pe, s_ppl, 2 * (n - 1))
                for b in range(2):
                    h = slice(HALF * b, HALF * b + HALF)
                    w, l = mix_hi[:, g, :], mix_lo[:, g, :]
                    hi, lo = pool_hi[n % 2][:, h], pool_lo[n % 2][:, h]
                    group(ps[:, 4 + 2 * (n % 2) + b, :], [w, w, l], [hi, lo, hi]).then_inc(s_mix, 1)

            pe.wait_ge(s_exp, 64)
            pe.wait_ge(s_evh, 4 * RPAIR)
            pe.wait_ge(s_evl, 4 * RPAIR)
            for n in range(NG):
                wait(pe, s_wlo, C_U + n + 1)
                wait(pe, s_uev, 2 * (n - 1))
                for b in range(2):
                    column_product(C_U + n, b, 2 * (n % 2) + b).then_inc(s_u, 1)
                if n == 0:
                    pe.wait_ge(s_pvev, 16)
                if n:
                    mix(n - 1)
            mix(NG - 1)

            pe.wait_ge(s_uev, 2 * NG)
            pe.wait_ge(s_ppl, 2 * NG)
            pe.wait_ge(s_pph, 2 * NG)
            pe.wait_ge(s_alo, NG)

            def gated(j):
                for u in range(2):
                    m, c = 2 * j + u, C_GATE + 3 * u
                    for i, (done, free, bank) in enumerate(((s_gp, s_sgp, 0), (s_ga, s_sga, 2))):
                        wait(pe, s_wlo, c + i + 1 + 6 * j)
                        wait(pe, free, 2 * m)
                        for b in range(2):
                            column_product(c + i, b, bank + b).then_inc(done, 1)
                    wait(pe, s_wlo, c + 3 + 6 * j)
                    wait(pe, s_mrg, m)
                    for hi, lo, k0, done, bank in ((pp_hi, pp_lo, 0, s_py, 4), (a_hi, a_lo, 4, s_ay, 6)):
                        for b in range(2):
                            group(ps[:, bank + b, :],
                                  *three(*w_tiles(c + 2, k0, 4), *cols(hi, lo, b, 4))).then_inc(done, 1)

            gated(0)
            with pe.Fori(1, KD // 2) as j:
                gated(j)

            def row_step(n, c, lhi, llo, first, last, add0):
                for t in range(4):
                    if first and add0 is not None:
                        wait(pe, s_add, add0 + 2 * t + 2)
                    ts_ = slice(P * t, P * t + P)
                    hi, lo = lhi[n % 2][:, ts_], llo[n % 2][:, ts_]
                    for i, (l, w) in enumerate(((hi, w_hi), (hi, w_lo), (lo, w_hi))):
                        for f in range(2):
                            ins = mm(ps[:, 2 * t + f, :], l, w[c % 2][:, HALF * f:HALF * f + HALF],
                                     start=first and i == 0, stop=last and i == 2)
                    if last:
                        ins.then_inc(s_tile, 1)
                if not last:
                    ins.then_inc(s_kused, 1)

            pe.wait_ge(s_mrg, KD)
            pe.wait_ge(s_sga, 2 * KD)
            for n in range(2 * KD):
                pe.wait_ge(s_wlo, C_OUT + n + 1)
                pe.wait_ge(s_llo, n + 1)
                row_step(n, C_OUT + n, le_hi, le_lo, n % KD == 0, n % KD == KD - 1,
                         0 if n == KD else None)

            for t in range(NT):
                wait(pe, s_xn2, t + 1)
                wait(pe, s_add, 2 * (5 + t) if t < 4 else 16)
                if t >= 4:
                    wait(pe, s_h2lo, 2 * (t - 3))
                    wait(pe, s_h2hi, 2 * (t - 3))
                for b in range(2):
                    for k in range(4):
                        ins = nc.tensor.transpose(ps[:, 2 * (t % 4) + b, P * k:P * k + P],
                                                  xn2[:, t, (4 * b + k) * P:(4 * b + k + 1) * P], ident[:])
                    ins.then_inc(s_tp2, 1)

            def ffn(m, dm):
                for i, done in enumerate((s_fg, s_fu)):
                    wait(pe, s_wlo, C_FFN + 2 * m + i + 1 + 2 * dm)
                    wait(pe, s_silu if i == 0 else s_prod, 2 * m + 2 * dm - 2)
                    for b in range(2):
                        column_product(C_FFN + i, b, 4 * (m % 2) + 2 * i + b).then_inc(done, 1)

            pe.wait_ge(s_h2lo, 2 * NT)
            ffn(0, 0)
            ffn(1, 0)
            with pe.Fori(1, KF // 2) as j:
                ffn(0, 2 * j)
                ffn(1, 2 * j)

            pe.wait_ge(s_prod, 2 * KF)
            l0 = 2 * KD

            def down(n, dn, first, last, add0):
                wait(pe, s_wlo, C_DOWN + n + 1 + dn)
                wait(pe, s_llo, l0 + n + 1 + dn)
                row_step(n, C_DOWN + n, lg_hi, lg_lo, first, last, add0)

            for hh in range(2):
                n0 = KF * hh
                down(n0, 0, True, False, 16 if hh else None)
                down(n0 + 1, 0, False, False, None)
                with pe.Fori(1, KF // 2 - 1) as j:
                    down(n0, 2 * j, False, False, None)
                    down(n0 + 1, 2 * j, False, False, None)
                down(n0 + KF - 2, 0, False, False, None)
                down(n0 + KF - 1, 0, False, True, None)


_INS = ["x", "norm1_g", "w_in", "b_forget", "pool_mix", "pool_scale", "w_pool_out", "w_attn_out",
        "w_out", "norm2_g", "w_ffn_gate", "w_ffn_up", "w_ffn_down", "norm_f_g"]


def kernel(**inputs):
    import numpy as np
    import concourse.bacc as bacc
    from concourse.bass_utils import run_bass_kernel_spmd

    nc = bacc.Bacc("TRN2", target_bir_lowering=False, num_devices=1, dynamic_dma_scratch_size=1024)
    arrays, args = {}, []
    for name in _INS:
        a = np.ascontiguousarray(inputs[name])
        arrays[f"in_{name}"] = a
        args.append(nc.dram_tensor(f"in_{name}", a.shape, mybir.dt.from_np(a.dtype), kind="ExternalInput").ap())
    out = nc.dram_tensor("out_0", (1, S, D), mybir.dt.float32, kind="ExternalOutput").ap()
    hybrid_block(nc, *args, out)
    r = run_bass_kernel_spmd(nc, [arrays], core_ids=[0])
    return r.results[0]["out_0"]
```

```python
import concourse.bass as bass
from concourse import mybir
from contextlib import ExitStack

P = 128
S = 1024
D = 1024
NT = S // P
KD = D // P
HALF = 512
BW = 512
NH = 8
DH = 64
NG = 4
DFF = 2816
KF = DFF // P
EPS = 1e-6
NEG = -1.0e30
COL_U, COL_Q, COL_K, COL_V = 0, BW, 2 * BW, 3 * BW
COL_F = 4 * BW
COL_GP = COL_F + NH
COL_GA = COL_GP + D
VF = BW + NH
VH = VF // 2

C_QK, C_U, C_GATE = 0, 8, 12
C_OUT = C_GATE + 3 * KD
C_FFN = C_OUT + 2 * KD
C_DOWN = C_FFN + 2 * KF
C_END = C_DOWN + 2 * KF

ROUNDS = [1 if (s % 8) < 4 else 2 for s in range(16)]
RSUM = [0]
for _s in range(32):
    RSUM.append(RSUM[-1] + ROUNDS[_s % 16])
RPAIR = RSUM[16]
FILL = [(0, 0, 8), (0, 8, 16), (0, 16, 24), (1, 0, 12), (1, 12, 24),
        (2, 0, 8), (2, 8, 16), (2, 16, 24), (3, 0, 12), (3, 12, 24)]
FILLED = {s: n for s, (n, _, b) in enumerate(FILL) if b == 24}
AHEAD = 3


def wait(eng, sem, value):
    if not isinstance(value, int) or value > 0:
        eng.wait_ge(sem, value)


def hybrid_block(nc, x, norm1_g, w_in, b_forget, pool_mix, pool_scale, w_pool_out, w_attn_out,
                 w_out, norm2_g, w_gate, w_up, w_down, norm_f_g, out):
    f32, f32r = mybir.dt.float32, mybir.dt.float32r
    ACT, ALU, AX = mybir.ActivationFunctionType, mybir.AluOpType, mybir.AxisListType

    x_d = x[0].rearrange("(t p) d -> t p d", p=P)
    out_d = out[0].rearrange("(t p) d -> t p d", p=P)
    win_d = w_in[0].rearrange("(k p) m -> p k m", p=P)
    wpool_d = w_pool_out[0].rearrange("(k p) m -> p k m", p=P)
    wattn_d = w_attn_out[0].rearrange("(k p) m -> p k m", p=P)
    wout_d = w_out[0].rearrange("(k p) m -> k p m", p=P)
    wgate_d = w_gate[0].rearrange("(k p) m -> p k m", p=P)
    wup_d = w_up[0].rearrange("(k p) m -> p k m", p=P)
    wdown_d = w_down[0].rearrange("(k p) m -> k p m", p=P)
    mix_d = pool_mix[0].rearrange("g c d -> c g d")
    scale_d = pool_scale[0].rearrange("(g c) -> g c", c=P)
    frow_q = nc.dram_tensor("frow_q", (NH, 4, S), f32, kind="Internal").ap()
    frow_k = nc.dram_tensor("frow_k", (NH, 4, S), f32, kind="Internal").ap()
    at_d = nc.dram_tensor("at_d", (NH, DH, S), f32, kind="Internal").ap()
    at_rows = at_d.rearrange("h d t -> (h d) t")
    x2_d = nc.dram_tensor("x2_d", (NT, P, D), f32, kind="Internal").ap()

    ctx = ExitStack()
    with ctx:
        base = -(-nc.sbuf_base // 32) * 32
        slab_words = (nc.sbuf_usable_end - base) // 4 // 8 * 8 - 16
        ctx.enter_context(nc.sbuf_tensor("slab", [P, slab_words], f32))
        end = base + slab_words * 4
        at = [base]

        def place(name, shape, dt=f32):
            n = 4
            for d in shape[1:]:
                n *= d
            t = nc.alloc_sbuf_tensor_at(name, shape, dt, offset=at[0])
            at[0] += -(-n // 32) * 32
            assert at[0] <= end, (name, at[0] - end)
            return t

        w_raw = [place(f"w_raw{i}", [P, 1024]) for i in range(2)]
        w_hi = [place(f"w_hi{i}", [P, 1024], f32r) for i in range(2)]
        w_lo = [place(f"w_lo{i}", [P, 1024], f32r) for i in range(2)]
        after_ring = at[0]
        w_end_hi = place("w_end_hi", [P, 1024], f32r)
        w_end_lo = place("w_end_lo", [P, 1024], f32r)
        at[0] = after_ring
        h_hi = place("h_hi", [P, KD, S], f32r)
        h_lo = place("h_lo", [P, KD, S], f32r)
        gain = place("gain", [P, D])
        ident = place("ident", [P, P])
        ident_r = place("ident_r", [P, P], f32r)
        mask_f = place("mask_f", [P, P])
        mask_r = place("mask_r", [P, P], f32r)
        tri = place("tri", [P, P])
        ones = place("ones", [P, P])
        neg_half = place("neg_half", [P, 1])
        ssq = place("ssq", [P, 24])
        var = place("var", [P, 24])
        rstd = place("rstd", [P, 24])
        negmax = [place(f"negmax{i}", [P, 1]) for i in range(2)]
        rowsum = [place(f"rowsum{i}", [P, 1]) for i in range(2)]
        rowinv = [place(f"rowinv{i}", [P, 1]) for i in range(2)]
        pscale = place("pscale", [P, NG])
        inv_cnt = place("inv_cnt", [P, 16])
        phase = at[0]

        v_raw = place("v_raw", [P, NT, BW])
        after_v = at[0]
        xt = [place(f"xt{i}", [P, D]) for i in range(2)]
        xn = [place(f"xn{i}", [P, D]) for i in range(2)]
        wv_raw = place("wv_raw", [P, KD, VF])
        wv_hi = place("wv_hi", [P, KD, VF], f32r)
        wv_lo = place("wv_lo", [P, KD, VF], f32r)
        hs_hi = [place(f"hs_hi{i}", [P, KD, P], f32r) for i in range(2)]
        hs_lo = [place(f"hs_lo{i}", [P, KD, P], f32r) for i in range(2)]
        f_hi = place("f_hi", [NH, 2, S])
        f_neg = place("f_neg", [NH, 2, S])
        f_one = place("f_one", [NH, 2, S])
        fz = place("fz", [P, NT, NH])
        fa = place("fa", [P, NT, NH])
        fe = place("fe", [P, NT, NH])
        fl = place("fl", [P, NT, NH])
        fbias = place("fbias", [P, NH])
        at[0] = after_v
        vs = [place(f"vs{i}", [P, NT, 2 * DH], f32r) for i in range(2)]
        at_st = [place(f"at_st{i}", [DH, HALF]) for i in range(2)]
        q1 = [place(f"q1_{i}", [P, S], f32r) for i in range(2)]
        q2 = [place(f"q2_{i}", [P, S], f32r) for i in range(2)]
        k1 = [place(f"k1_{i}", [P, S], f32r) for i in range(2)]
        k2 = [place(f"k2_{i}", [P, S], f32r) for i in range(2)]
        q_raw = place("q_raw", [P, S])
        k_raw = place("k_raw", [P, S])
        p_raw = [place(f"p_raw{i}", [P, S]) for i in range(2)]
        p_hi = [place(f"p_hi{i}", [P, S], f32r) for i in range(2)]
        p_lo = [place(f"p_lo{i}", [P, S], f32r) for i in range(2)]
        pt_hi = place("pt_hi", [P, NT, HALF], f32r)
        pt_lo = place("pt_lo", [P, NT, HALF], f32r)
        pv_tmp = place("pv_tmp", [DH, HALF])
        at[0] = phase
        a_hi = place("a_hi", [P, NG, S], f32r)
        a_lo = place("a_lo", [P, NG, S], f32r)
        pp_hi = place("pp_hi", [P, NG, S], f32r)
        pp_lo = place("pp_lo", [P, NG, S], f32r)
        after_branches = at[0]
        a_raw = [place(f"a_raw{i}", [P, S]) for i in range(2)]
        u_sb = [place(f"u_sb{i}", [P, S]) for i in range(2)]
        win = [place(f"win{i}", [P, S]) for i in range(2)]
        pool = place("pool", [P, S])
        head_tmp = place("head_tmp", [P, 16])
        pool_hi = [place(f"pool_hi{i}", [P, S], f32r) for i in range(2)]
        pool_lo = [place(f"pool_lo{i}", [P, S], f32r) for i in range(2)]
        mix_raw = place("mix_raw", [P, NG, P])
        mix_hi = place("mix_hi", [P, NG, P], f32r)
        mix_lo = place("mix_lo", [P, NG, P], f32r)
        at[0] = after_branches
        sig_p = place("sig_p", [P, S])
        sig_a = place("sig_a", [P, S])
        merged = place("merged", [P, KD, S])
        after_merged = at[0]
        at[0] = phase
        x2 = place("x2", [P, NT, D])
        xn2 = place("xn2", [P, NT, D])
        assert at[0] <= after_branches
        at[0] = after_merged
        le_hi = [place(f"le_hi{i}", [P, HALF], f32r) for i in range(2)]
        le_lo = [place(f"le_lo{i}", [P, HALF], f32r) for i in range(2)]
        junk_e = place("junk_e", [P, D])
        at[0] = phase
        prod = place("prod", [P, KF, S])
        after_prod = at[0]
        sig_g = [place(f"sig_g{i}", [P, HALF]) for i in range(2)]
        silu = [place(f"silu{i}", [P, HALF]) for i in range(2)]
        at[0] = after_prod
        lg_hi = [place(f"lg_hi{i}", [P, HALF], f32r) for i in range(2)]
        lg_lo = [place(f"lg_lo{i}", [P, HALF], f32r) for i in range(2)]
        y = place("y", [P, 4, D])
        y_out = [place(f"y_out{i}", [P, D]) for i in range(2)]
        junk_g = place("junk_g", [P, D])

        ps = ctx.enter_context(nc.psum_tensor("ps", [P, 8, HALF], f32))
        ps_flat = ps[:].rearrange("p b n -> p (b n)")

        def sem(name):
            return ctx.enter_context(nc.semaphore(name))

        s_wraw = [sem(f"s_wraw{i}") for i in range(2)]
        s_whi, s_wlo = sem("s_whi"), sem("s_wlo")
        s_gain = sem("s_gain")
        s_const = sem("s_const")
        s_cid = sem("s_cid")
        s_x = [sem(f"s_x{i}") for i in range(2)]
        s_wv = [sem(f"s_wv{i}") for i in range(4)]
        s_wvhi, s_wvlo = sem("s_wvhi"), sem("s_wvlo")
        s_fb = sem("s_fb")
        s_sq, s_var, s_rstd = sem("s_sq"), sem("s_var"), sem("s_rstd")
        s_xn = sem("s_xn")
        s_tp = sem("s_tp")
        s_hshi, s_hthi = sem("s_hshi"), sem("s_hthi")
        s_hslo, s_htlo = sem("s_hslo"), sem("s_htlo")
        s_v = sem("s_v")
        s_vev_a, s_vev_d = sem("s_vev_a"), sem("s_vev_d")
        s_fz, s_fa, s_fcum, s_frow = sem("s_fz"), sem("s_fa"), sem("s_fcum"), sem("s_frow")
        s_fhi, s_flo = sem("s_fhi"), sem("s_flo")
        s_fst = sem("s_fst")
        s_pj, s_pjev = sem("s_pj"), sem("s_pjev")
        s_sta, s_std, s_stp = sem("s_sta"), sem("s_std"), sem("s_stp")
        s_frd = [sem(f"s_frd{i}") for i in range(2)]
        s_z = sem("s_z")
        s_vshi, s_vslo = sem("s_vshi"), sem("s_vslo")
        s_s, s_mx, s_exp, s_rc = sem("s_s"), sem("s_mx"), sem("s_exp"), sem("s_rc")
        s_phi, s_plo = sem("s_phi"), sem("s_plo")
        s_th, s_tl = sem("s_th"), sem("s_tl")
        s_evh, s_evl = sem("s_evh"), sem("s_evl")
        s_pv, s_pvt, s_pvev = sem("s_pv"), sem("s_pvt"), sem("s_pvev")
        s_atst = [sem(f"s_atst{i}") for i in range(2)]
        s_u, s_uev = sem("s_u"), sem("s_uev")
        s_dve = sem("s_dve")
        s_pool, s_plh, s_pll = sem("s_pool"), sem("s_plh"), sem("s_pll")
        s_mixw, s_mixhi, s_mixlo = sem("s_mixw"), sem("s_mixhi"), sem("s_mixlo")
        s_mix, s_pph, s_ppl = sem("s_mix"), sem("s_pph"), sem("s_ppl")
        s_araw = [sem(f"s_araw{i}") for i in range(2)]
        s_ahi, s_alo = sem("s_ahi"), sem("s_alo")
        s_gp, s_ga, s_py, s_ay = sem("s_gp"), sem("s_ga"), sem("s_py"), sem("s_ay")
        s_sgp, s_sga, s_mul, s_mrg = sem("s_sgp"), sem("s_sga"), sem("s_mul"), sem("s_mrg")
        s_lhi, s_llo = sem("s_lhi"), sem("s_llo")
        s_kused, s_tile = sem("s_kused"), sem("s_tile")
        s_add = sem("s_add")
        s_xr = [sem(f"s_xr{i}") for i in range(2)]
        s_x2st = sem("s_x2st")
        s_xn2, s_tp2, s_h2hi, s_h2lo = sem("s_xn2"), sem("s_tp2"), sem("s_h2hi"), sem("s_h2lo")
        s_fg, s_fu, s_sig, s_silu, s_prod = sem("s_fg"), sem("s_fu"), sem("s_sig"), sem("s_silu"), sem("s_prod")
        s_yld = sem("s_yld")
        s_yn = sem("s_yn")
        s_out = [sem(f"s_out{i}") for i in range(2)]

        block = ctx.enter_context(nc.Block())

        @block.sync
        def _(sp):
            def load_chunk(c, dc, src0, src1):
                wait(sp, s_wlo, c - 1 + dc)
                sp.dma_start(w_raw[c % 2][:, 0:512], src0).then_inc(s_wraw[c % 2], 16)
                sp.dma_start(w_raw[c % 2][:, 512:1024], src1).then_inc(s_wraw[c % 2], 16)

            def load_cols(c, dc, w, col):
                wait(sp, s_wlo, c - 1 + dc)
                for j in range(2):
                    sp.dma_start(w_raw[c % 2][:, 512 * j:512 * j + 512].rearrange("p (k m) -> p k m", m=P),
                                 w[:, 4 * j:4 * j + 4, bass.ds(col, P)]).then_inc(s_wraw[c % 2], 16)

            def load_x(j, u):
                wait(sp, s_xn, 2 * j + u - 1)
                sp.dma_start(xt[u][:], x_d[2 * j + u]).then_inc(s_x[u], 16)

            load_x(0, 0)
            sp.dma_start(gain[:], norm1_g[0].partition_broadcast(P)).then_inc(s_gain, 16)
            for i in range(4):
                if i == 2:
                    load_x(0, 1)
                sp.dma_start(wv_raw[:, 2 * i:2 * i + 2, :],
                             win_d[:, 2 * i:2 * i + 2, COL_V:COL_V + VF]).then_inc(s_wv[i], 16)
            sp.dma_start(fbias[:], b_forget[0].partition_broadcast(P)).then_inc(s_fb, 16)
            load_cols(0, 0, win_d, COL_Q)
            load_cols(1, 0, win_d, COL_K)
            for j in range(1, 4):
                for u in range(2):
                    load_x(j, u)
            load_cols(2, 0, win_d, COL_Q + P)
            load_cols(3, 0, win_d, COL_K + P)

            wait(sp, s_flo, 4)
            wait(sp, s_fhi, 4)
            wait(sp, s_const, 6)
            sp.dma_start(frow_q[:, 0:2, :], f_hi[:]).then_inc(s_fst, 16)
            sp.dma_start(frow_q[:, 2:4, :], f_one[:]).then_inc(s_fst, 16)
            sp.dma_start(frow_k[:, 0:2, :], f_one[:]).then_inc(s_fst, 16)
            sp.dma_start(frow_k[:, 2:4, :], f_neg[:]).then_inc(s_fst, 16)
            wait(sp, s_fst, 64)

            def load_frows(p, e):
                r0 = DH * (1 - e)
                sp.dma_start(q2[e][r0:r0 + 4, :].bitcast(f32), frow_q[2 * p + e]).then_inc(s_frd[e], 16)
                sp.dma_start(k2[e][r0:r0 + 4, :].bitcast(f32), frow_k[2 * p + e]).then_inc(s_frd[e], 16)

            def store_at(p, g4):
                wait(sp, s_pvev, 4 * p + g4 + 1)
                sp.dma_start(at_d[2 * p + g4 // 2, :, HALF * (g4 % 2):HALF * (g4 % 2) + HALF],
                             at_st[g4 % 2][:]).then_inc(s_atst[g4 % 2], 16)

            wait(sp, s_z, 4)
            load_frows(0, 0)
            for p in range(4):
                for j, col in ((0, COL_Q), (1, COL_K)):
                    if p < 2:
                        load_cols(2 * p + 4 + j, 0, win_d, col + P * (p + 2))
                    elif p == 2:
                        load_cols(C_U + j, 0, win_d, COL_U + P * (3 - j))
                wait(sp, s_s, 16 * p)
                load_frows(p, 1)
                store_at(p, 0)
                if p < 3:
                    wait(sp, s_s, 16 * p + 8)
                    load_frows(p + 1, 0)
                for g4 in range(1, 4):
                    store_at(p, g4)

            wait(sp, s_atst[0], 16 * 8)
            wait(sp, s_atst[1], 16 * 8)
            wait(sp, s_pvev, 16)
            sp.dma_start(mix_raw[:], mix_d).then_inc(s_mixw, 16)
            for g in range(NG):
                sp.dma_start(pscale[:, g:g + 1], scale_d[g].rearrange("(c o) -> c o", o=1),
                             allow_slow_non_contiguous=True).then_inc(s_mixw, 16)
            for n in range(2):
                sp.dma_start(a_raw[n][:], at_rows[P * n:P * n + P, :]).then_inc(s_araw[n], 16)
            load_cols(C_U + 2, 0, win_d, COL_U + P)
            load_cols(C_U + 3, 0, win_d, COL_U)
            for n in range(2, 4):
                wait(sp, s_alo, n - 1)
                sp.dma_start(a_raw[n % 2][:], at_rows[P * n:P * n + P, :]).then_inc(s_araw[n % 2], 16)

            wait(sp, s_xn, NT)
            sp.dma_start(gain[:], norm2_g[0].partition_broadcast(P)).then_inc(s_gain, 16)
            with sp.Fori(1, KD // 2 + 1) as j:
                for u in range(2):
                    c, dc, m = C_GATE + 3 * u, 6 * j - 6, 2 * j + (u - 2)
                    load_cols(c, dc, win_d, COL_GP + m * P)
                    load_cols(c + 1, dc, win_d, COL_GA + m * P)
                    wait(sp, s_wlo, c + 1 + dc)
                    for i, w in enumerate((wpool_d, wattn_d)):
                        sp.dma_start(w_raw[c % 2][:, 512 * i:512 * i + 512].rearrange("p (k m) -> p k m", m=P),
                                     w[:, :, bass.ds(2 * P * j + P * (u - 2), P)]).then_inc(s_wraw[c % 2], 16)

            def rows_chunk(c, dc, w, k):
                load_chunk(c, dc, w[k, :, 0:512], w[k, :, 512:1024])

            for n in range(2 * KD):
                rows_chunk(C_OUT + n, 0, wout_d, n % KD)
                if n == 3:
                    wait(sp, s_py, 2 * KD)
                    wait(sp, s_ay, 2 * KD)
                if 3 <= n < 3 + NT:
                    sp.dma_start(x2[:, n - 3, :], x_d[n - 3]).then_inc(s_xr[(n - 3) // 4], 16)
            load_cols(C_FFN, 0, wgate_d, 0)
            load_cols(C_FFN + 1, 0, wup_d, 0)
            for t in range(NT):
                wait(sp, s_add, 2 * (t + 1))
                sp.dma_start(x2_d[t], x2[:, t, :]).then_inc(s_x2st, 16)

            with sp.Fori(1, KF) as m:
                load_cols(C_FFN, 2 * m, wgate_d, m * P)
                load_cols(C_FFN + 1, 2 * m, wup_d, m * P)
            wait(sp, s_xn2, NT)
            sp.dma_start(gain[:], norm_f_g.partition_broadcast(P)).then_inc(s_gain, 16)

            def down_chunks(j0, j1, hh):
                with sp.Fori(j0, j1) as j:
                    for u in range(2):
                        rows_chunk(C_DOWN + KF * hh + u, 2 * j, wdown_d, 2 * j + u)

            down_chunks(0, KF // 2 - 3, 0)
            wait(sp, s_x2st, 16 * NT)
            wait(sp, s_prod, 2 * KF)
            for tt in range(4):
                sp.dma_start(y[:, tt, :], x2_d[tt]).then_inc(s_yld, 16)
            down_chunks(KF // 2 - 3, KF // 2, 0)
            down_chunks(0, KF // 2, 1)
            wait(sp, s_out[0], 16 * 4)
            wait(sp, s_out[1], 16 * 4)

        @block.gpsimd
        def _(pool):
            g = nc.gpsimd

            def w_low(c, dc=0):
                end = c in (C_FFN - 1, C_END - 1)
                hi, lo = (w_end_hi, w_end_lo) if end else (w_hi[c % 2], w_lo[c % 2])
                wait(pool, s_whi, c + 1 + dc)
                g.tensor_tensor(lo[:], w_raw[c % 2][:], hi[:].bitcast(f32), ALU.subtract).then_inc(s_wlo, 1)

            def inv_root(n, col):
                wait(pool, s_var, n + 1)
                g.tensor_tensor(rstd[:, bass.ds(col, 1)], var[:, bass.ds(col, 1)], neg_half[:],
                                ALU.pow).then_inc(s_rstd, 1)

            g.memset(neg_half[:], -0.5).then_inc(s_cid, 1)
            g.memset(ident[:], 0.0).then_inc(s_cid, 1)
            pool.wait_ge(s_cid, 2)
            g.affine_select(out=ident[:], in_=ident[:], compare_op=ALU.not_equal, fill=1.0, base=0,
                            pattern=[[-1, P]], channel_multiplier=1).then_inc(s_const, 1)
            inv_root(0, 0)
            inv_root(1, 1)
            g.memset(mask_f[:], 0.0).then_inc(s_cid, 1)
            g.memset(tri[:], 1.0).then_inc(s_cid, 1)
            g.memset(ones[:], 1.0).then_inc(s_const, 1)
            g.memset(f_one[:], 1.0).then_inc(s_const, 1)
            pool.wait_ge(s_cid, 4)
            g.affine_select(out=mask_f[:], in_=mask_f[:], compare_op=ALU.is_ge, fill=NEG, base=0,
                            pattern=[[-1, P]], channel_multiplier=1).then_inc(s_const, 1)
            g.affine_select(out=tri[:], in_=tri[:], compare_op=ALU.is_ge, fill=0.0, base=0,
                            pattern=[[1, P]], channel_multiplier=-1).then_inc(s_const, 1)
            for t in range(16):
                last = g.memset(inv_cnt[:, t:t + 1], 1.0 / (t + 1))
            last.then_inc(s_const, 1)
            for n in range(2, NT):
                inv_root(n, n)
            w_low(0)
            w_low(1)

            def stack_low(p, e):
                r = slice(DH * e, DH * e + DH)
                wait(pool, s_std, 3 * (2 * p + e) + 3)
                wait(pool, s_z, 4)
                if not isinstance(p, int) or 2 * p + e > 1:
                    wait(pool, s_s, 16 * p + (0 if e else -8))
                g.tensor_tensor(k2[e][r, :], k_raw[r, :], k1[e][r, :].bitcast(f32),
                                ALU.subtract).then_inc(s_stp, 1)
                wait(pool, s_stp, 2 * p + e + 1)

            def v_low(p, e):
                wait(pool, s_vshi, 2 * p + e + 1)
                g.tensor_tensor(vs[e][:, :, DH:2 * DH], v_raw[:, :, bass.ds((2 * p + e) * DH, DH)],
                                vs[e][:, :, 0:DH].bitcast(f32), ALU.subtract).then_inc(s_vslo, 1)

            wait(pool, s_v, NT)
            wait(pool, s_wlo, 2)
            for e in range(2):
                r = slice(DH * (1 - e), DH * (1 - e) + DH)
                g.memset(q2[e][r, :].bitcast(f32), 0.0).then_inc(s_z, 1)
                g.memset(k2[e][r, :].bitcast(f32), 0.0).then_inc(s_z, 1)
                wait(pool, s_z, 2 * e + 2)
            v_low(0, 0)
            w_low(2)
            w_low(3)
            stack_low(0, 0)

            def attention(p, last):
                stack_low(p, 1)
                v_low(p, 1)
                if not last:
                    w_low(4, 2 * p)
                    v_low(p + 1, 0)
                    stack_low(p + 1, 0)
                    w_low(5, 2 * p)
                    wait(pool, s_wlo, 2 * p + 6)

            attention(0, False)
            with pool.Fori(1, 3) as p:
                attention(p, False)
            attention(3, True)

            wait(pool, s_mixhi, 1)
            g.tensor_tensor(mix_lo[:], mix_raw[:], mix_hi[:].bitcast(f32), ALU.subtract).then_inc(s_mixlo, 1)

            def a_low(n):
                wait(pool, s_ahi, n + 1)
                g.tensor_tensor(a_lo[:, n, :], a_raw[n % 2][:], a_hi[:, n, :].bitcast(f32),
                                ALU.subtract).then_inc(s_alo, 1)

            for n in range(NG):
                w_low(C_U + 2 + n)
                a_low(n)
            with pool.Fori(0, KD // 2) as j:
                for i in range(6):
                    w_low(C_GATE + 2 + i, 6 * j)
            for c in range(C_OUT + 2, C_FFN):
                w_low(c)
                if c - C_OUT - 2 >= 8 and c - C_OUT - 2 < 12:
                    inv_root(c - C_OUT - 2, c - C_OUT - 2)
            for n in range(4):
                inv_root(12 + n, 12 + n)
                if n >= 2:
                    w_low(C_FFN + n - 2)
            with pool.Fori(0, KF) as m:
                w_low(C_FFN + 2, 2 * m)
                w_low(C_FFN + 3, 2 * m)
            w_low(C_DOWN + 2)
            w_low(C_DOWN + 3)
            with pool.Fori(0, KF // 2 - 1) as j:
                w_low(C_DOWN + 4, 2 * j)
                w_low(C_DOWN + 5, 2 * j)
            for n in range(4):
                w_low(C_DOWN + KF + 2 + n)
                inv_root(16 + n, 16 + n)
            with pool.Fori(0, (KF - 6) // 2 - 1) as j:
                w_low(C_DOWN + KF + 6, 2 * j)
                w_low(C_DOWN + KF + 7, 2 * j)
            w_low(C_END - 2)
            w_low(C_END - 1)
            for n in range(4, 8):
                inv_root(16 + n, 16 + n)

        @block.scalar
        def _(act):
            a = nc.scalar

            def w_high(c, dc=0):
                wait(act, s_wraw[c % 2], 32 * (c // 2 + 1) + 16 * dc)
                hi = w_end_hi if c in (C_FFN - 1, C_END - 1) else w_hi[c % 2]
                a.activation(hi[:], w_raw[c % 2][:], ACT.Copy).then_inc(s_whi, 1)

            def square(j, u):
                wait(act, s_x[u], 16 * (j + 1))
                wait(act, s_tp, 2 * (2 * j + u - 1))
                a.activation(xn[u][:], xt[u][:], ACT.Square,
                             accum_out=ssq[:, bass.ds(2 * j + u, 1)]).then_inc(s_sq, 1)

            def high_h(j, u):
                t = 2 * j + u
                wait(act, s_v, t - 1)
                for b in range(2):
                    wait(act, s_tp, 2 * t + b + 1)
                    src = ps[:, 2 * u + b, :].rearrange("p (k n) -> p k n", n=P)
                    a.activation(hs_hi[u][:, 4 * b:4 * b + 4, :], src, ACT.Copy).then_inc(s_hshi, 1)
                    a.activation(h_hi[:, 4 * b:4 * b + 4, bass.ds(t * P, P)], src, ACT.Copy).then_inc(s_hthi, 1)

            def evac_v(j, u):
                t = 2 * j + u
                wait(act, s_v, t + 1)
                a.activation(v_raw[:, bass.ds(t, 1), 0:VH],
                             ps[:, 4 + 2 * u, 0:VH].rearrange("p (o n) -> p o n", o=1),
                             ACT.Copy).then_inc(s_vev_a, 1)

            square(0, 0)
            square(0, 1)
            for i in range(4):
                act.wait_ge(s_wv[i], 16)
                a.activation(wv_hi[:, 2 * i:2 * i + 2, :], wv_raw[:, 2 * i:2 * i + 2, :],
                             ACT.Copy).then_inc(s_wvhi, 1)
            high_h(0, 0)

            def stage_a(j):
                square(j + 1, 0)
                high_h(j, 1)
                evac_v(j, 0)
                square(j + 1, 1)
                high_h(j + 1, 0)
                evac_v(j, 1)

            stage_a(0)
            with act.Fori(1, 3) as j:
                stage_a(j)
            w_high(0)
            w_high(1)
            high_h(3, 1)
            evac_v(3, 0)
            evac_v(3, 1)

            act.wait_ge(s_fz, 3)
            a.activation(fe[:], fa[:], ACT.Exp, scale=-1.0).then_inc(s_fa, 1)
            act.wait_ge(s_fa, 1)
            a.activation(fl[:], fe[:], ACT.Ln, bias=1.0).then_inc(s_fa, 1)

            def evac_qk(p, n, bank):
                wait(act, s_pj, 4 * p + n + 1)
                dst = (q_raw, k_raw)[n // 2]
                a.activation(dst[:, HALF * (n % 2):HALF * (n % 2) + HALF], ps[:, bank, :], ACT.Copy,
                             scale=(DH ** -0.5 if n < 2 else 1.0)).then_inc(s_pjev, 1)

            def stack_high(p, e):
                r = slice(DH * e, DH * e + DH)
                wait(act, s_pjev, 4 * p + 2)
                wait(act, s_s, 16 * p + (0 if e else -8))
                a.activation(q2[e][r, :], q_raw[r, :], ACT.Copy).then_inc(s_sta, 1)
                a.activation(q1[e][r, :], q_raw[r, :], ACT.Copy).then_inc(s_sta, 1)

            def v_high(p, e):
                wait(act, s_pv, 4 * p + (0 if e else -2))
                a.activation(vs[e][:, :, 0:DH], v_raw[:, :, bass.ds((2 * p + e) * DH, DH)],
                             ACT.Copy).then_inc(s_vshi, 1)

            def softmax_exp(p, s):
                n = ((s % 8) + 1) * P
                wait(act, s_mx, 16 * p + s + 1)
                wait(act, s_plo, 16 * p + s - 1)
                wait(act, s_rc, 16 * p + s - 1)
                b = 1024 * (s % 2)
                a.activation(p_raw[s % 2][:, 0:n], ps_flat[:, b:b + n], ACT.Exp, bias=negmax[s % 2][:],
                             accum_out=rowsum[s % 2][:]).then_inc(s_exp, 1)

            def p_high(p, s):
                n = ((s % 8) + 1) * P
                wait(act, s_rc, 16 * p + s + 1)
                wait(act, s_exp, 16 * p + s + 1)
                wait(act, s_th, RPAIR * p + RSUM[s - 1] if s > 0 else RPAIR * p - ROUNDS[15])
                a.activation(p_hi[s % 2][:, 0:n], p_raw[s % 2][:, 0:n], ACT.Copy,
                             scale=rowinv[s % 2][:]).then_inc(s_phi, 1)

            def evac_t(p, s):
                i = s % 8
                if i % 4 == 0:
                    wait(act, s_pv, 4 * p + s // 4)
                for r in range(ROUNDS[s]):
                    n = min(4, i + 1 - 4 * r)
                    wait(act, s_th, RPAIR * p + RSUM[s] + r + 1)
                    a.activation(pt_hi[:, 4 * r:4 * r + n, (i % 4) * P:(i % 4) * P + P],
                                 ps[:, 4, 0:n * P].rearrange("p (k n) -> p k n", n=P),
                                 ACT.Copy).then_inc(s_evh, 1)

            def evac_pv(p, g4):
                wait(act, s_pv, 4 * p + g4 + 1)
                wait(act, s_pvev, 4 * p + g4)
                a.activation(pv_tmp[:], ps[DH:2 * DH, 6, :], ACT.Copy).then_inc(s_pvt, 1)

            def f_high(b):
                act.wait_ge(s_frow, b + 1)
                a.activation(f_hi[:, 0, HALF * b:HALF * b + HALF].bitcast(f32r),
                             ps[0:NH, 1 + b, :], ACT.Copy).then_inc(s_fhi, 1)
                act.wait_ge(s_fhi, 2 * b + 1)
                a.activation(f_neg[:, 0, HALF * b:HALF * b + HALF],
                             f_hi[:, 0, HALF * b:HALF * b + HALF], ACT.Copy, scale=-1.0).then_inc(s_fhi, 1)

            act.wait_ge(s_v, NT)
            v_high(0, 0)
            evac_qk(0, 0, 7)
            evac_qk(0, 1, 6)
            w_high(2)
            act.wait_ge(s_z, 4)
            stack_high(0, 0)
            f_high(0)
            f_high(1)
            evac_qk(0, 2, 5)
            evac_qk(0, 3, 4)
            w_high(3)
            softmax_exp(0, 0)
            p_high(0, 0)
            softmax_exp(0, 1)
            act.wait_ge(s_fst, 64)

            def attention(p, last):
                for s in range(16):
                    if s == 0:
                        stack_high(p, 1)
                    if s < 15 or not last:
                        p_high(p, s + 1)
                    if s < 14 or not last:
                        softmax_exp(p, s + 2)
                    if s in FILLED and not last:
                        if FILLED[s] == 0:
                            wait(act, s_std, 3 * (2 * p + 2))
                            wait(act, s_stp, 2 * p + 2)
                        evac_qk(p + 1, FILLED[s], 7)
                    evac_t(p, s)
                    if s in (4, 8, 12):
                        evac_pv(p, s // 4 - 1)
                    if s == 1:
                        v_high(p, 1)
                    if last:
                        continue
                    if s in FILLED and FILLED[s] % 2:
                        w_high(4 + FILLED[s] // 2, 2 * p)
                    if s == 6:
                        stack_high(p + 1, 0)
                    if s == 10:
                        v_high(p + 1, 0)
                evac_pv(p, 3)

            attention(0, False)
            with act.Fori(1, 3) as p:
                attention(p, False)
            attention(3, True)

            act.wait_ge(s_mixw, 16 * (1 + NG))
            a.activation(mix_hi[:], mix_raw[:], ACT.Copy).then_inc(s_mixhi, 1)

            def a_high(n):
                wait(act, s_araw[n % 2], 16 * (n // 2 + 1))
                a.activation(a_hi[:, n, :], a_raw[n % 2][:], ACT.Copy).then_inc(s_ahi, 1)

            def pool_high(n):
                wait(act, s_pool, n + 1)
                wait(act, s_mix, 2 * (n - 1))
                a.activation(pool_hi[n % 2][:], pool[:], ACT.Copy).then_inc(s_plh, 1)

            def pp_high(n):
                g = NG - 1 - n
                for b in range(2):
                    wait(act, s_mix, 2 * n + b + 1)
                    a.activation(pp_hi[:, g, HALF * b:HALF * b + HALF], ps[:, 4 + 2 * (n % 2) + b, :], ACT.Copy,
                                 scale=pscale[:, g:g + 1]).then_inc(s_pph, 1)

            for n in range(NG):
                for b in range(2):
                    wait(act, s_u, 2 * n + b + 1)
                    wait(act, s_pool, n - 1)
                    a.activation(u_sb[n % 2][:, HALF * b:HALF * b + HALF], ps[:, 2 * (n % 2) + b, :],
                                 ACT.Copy).then_inc(s_uev, 1)
                w_high(C_U + 2 + n)
                a_high(n)
                if n:
                    pp_high(n - 1)
                pool_high(n)

            def gates(j):
                for u in range(2):
                    m = 2 * j + u
                    for s_in, s_done, dst, bank in ((s_gp, s_sgp, sig_p, 0), (s_ga, s_sga, sig_a, 2)):
                        for b in range(2):
                            wait(act, s_in, 2 * m + b + 1)
                            if b == 0:
                                wait(act, s_mrg, m)
                            a.activation(dst[:, HALF * b:HALF * b + HALF], ps[:, bank + b, :],
                                         ACT.Sigmoid).then_inc(s_done, 1)
                        w_high(C_GATE + 2 + 3 * u + bank // 2, 6 * j)
                    if isinstance(m, int) and m == 0:
                        pp_high(NG - 1)
                    wait(act, s_ay, 2 * m + 2)
                    w_high(C_GATE + 4 + 3 * u, 6 * j)

            act.wait_ge(s_alo, NG)
            gates(0)
            with act.Fori(1, KD // 2) as j:
                gates(j)

            def left_high(n, src, k, hh, dst):
                a.activation(dst[n % 2][:], src[:, k, HALF * hh:HALF * hh + HALF] if isinstance(k, int)
                             else src[:, bass.ds(k, 1), HALF * hh:HALF * hh + HALF].rearrange("p o n -> p (o n)"),
                             ACT.Copy).then_inc(s_lhi, 1)

            def norm_square(n, src, junk):
                wait(act, s_sq, n)
                a.activation(junk[:], src, ACT.Square, accum_out=ssq[:, n:n + 1]).then_inc(s_sq, 1)

            act.wait_ge(s_mrg, 2)
            left_high(0, merged, 0, 0, le_hi)
            left_high(1, merged, 1, 0, le_hi)
            for n in range(2 * KD - 2):
                if n == KD - 1:
                    wait(act, s_tile, 4)
                else:
                    wait(act, s_kused, n + 1 - n // KD)
                wait(act, s_mrg, min(n + 3, KD))
                left_high(n + 2, merged, (n + 2) % KD, (n + 2) // KD, le_hi)
                if n < 2 * KD - 3:
                    w_high(C_OUT + 2 + n)
                if n == 2 * KD - 4:
                    w_high(C_FFN - 1)
                if n in (8, 9, 10, 11):
                    wait(act, s_add, 2 * (n - 7))
                    norm_square(n, x2[:, n - 8, :], junk_e)

            def h2_high(t):
                for b in range(2):
                    wait(act, s_tp2, 2 * t + b + 1)
                    a.activation(h_hi[:, 4 * b:4 * b + 4, t * P:t * P + P],
                                 ps[:, 2 * (t if t < 4 else t % 2) + b, :].rearrange("p (k n) -> p k n", n=P),
                                 ACT.Copy).then_inc(s_h2hi, 1)

            for t in range(4):
                if t == 3:
                    wait(act, s_tile, 8)
                    w_high(C_FFN)
                wait(act, s_add, 2 * (5 + t))
                norm_square(12 + t, x2[:, 4 + t, :], junk_e)
            w_high(C_FFN + 1)
            for t in range(6):
                h2_high(t)

            def ffn_gate(m, dm, b, n):
                wait(act, s_fg, 2 * m + 2 * dm + b + 1)
                wait(act, s_silu, 2 * m + 2 * dm + b - 1)
                a.activation(sig_g[b][:], ps[:, 4 - 4 * (m % 2) + b, :], ACT.Sigmoid).then_inc(s_sig, 1)

            def ffn(m, dm, first=False):
                for b in range(2):
                    ffn_gate(m, dm, b, 0)
                    if first and b == 0:
                        for t in range(6, 8):
                            h2_high(t)
                w_high(C_FFN + 2 + 2 * m, 2 * dm)
                wait(act, s_fu, 2 * m + 2 * dm + 2)
                w_high(C_FFN + 3 + 2 * m, 2 * dm)

            ffn(0, 0, True)
            ffn(1, 0)
            with act.Fori(1, KF // 2) as j:
                ffn(0, 2 * j)
                ffn(1, 2 * j)

            act.wait_ge(s_prod, 2 * KF)
            left_high(0, prod, 0, 0, lg_hi)
            left_high(1, prod, 1, 0, lg_hi)
            used0 = 2 * KD - 3

            def down(n, dn, hh, k):
                wait(act, s_kused, used0 + n + 1 - hh + dn)
                left_high(n, prod, k, hh, lg_hi)
                w_high(C_DOWN + 2 + n, dn)

            with act.Fori(0, KF // 2 - 1) as j:
                down(0, 2 * j, 0, 2 * j + 2)
                down(1, 2 * j, 0, 2 * j + 3)
            wait(act, s_kused, used0 + KF - 1)
            left_high(0, prod, 0, 1, lg_hi)
            w_high(C_DOWN + KF)
            wait(act, s_tile, 8 + 4)
            left_high(1, prod, 1, 1, lg_hi)
            w_high(C_DOWN + KF + 1)

            def store(t):
                wait(act, s_yn, t + 1)
                act.dma_start(out_d[t], y_out[t % 2][:]).then_inc(s_out[t % 2], 16)

            for i in range(6):
                down(KF + i, 0, 1, 2 + i)
                if i < 4:
                    wait(act, s_add, 16 + 2 * (i + 1))
                    norm_square(16 + i, y[:, i, :], junk_g)
                if 0 < i < 5:
                    store(i - 1)
                    act.dma_start(y[:, i - 1, :], x2_d[3 + i]).then_inc(s_yld, 16)
            with act.Fori(3, KF // 2 - 2) as j:
                down(KF, 2 * j, 1, 2 * j + 2)
                down(KF + 1, 2 * j, 1, 2 * j + 3)
            down(2 * KF - 4, 0, 1, KF - 2)
            w_high(C_END - 1)
            wait(act, s_kused, used0 + 2 * KF - 3)
            left_high(1, prod, KF - 1, 1, lg_hi)
            for t in range(4):
                wait(act, s_add, 16 + 2 * (5 + t))
                norm_square(20 + t, y[:, t, :], junk_g)
                if t:
                    store(3 + t)
            store(7)

        @block.vector
        def _(dve):
            v = nc.vector

            def variance(n):
                wait(dve, s_sq, n + 1)
                v.tensor_scalar(var[:, bass.ds(n, 1)], ssq[:, bass.ds(n, 1)], 1.0 / D, EPS,
                                ALU.mult, ALU.add).then_inc(s_var, 1)

            def normalise(n, dst, src, done):
                wait(dve, s_rstd, n + 1)
                v.scalar_tensor_tensor(dst, src, rstd[:, bass.ds(n, 1)], gain[:],
                                       ALU.mult, ALU.mult).then_inc(done, 1)

            def norm_x(j, u):
                variance(2 * j + u)
                wait(dve, s_tp, 2 * (2 * j + u - 1))
                normalise(2 * j + u, xn[u][:], xt[u][:], s_xn)

            def low_h(j, u):
                t = 2 * j + u
                wait(dve, s_v, t - 1)
                for b in range(2):
                    wait(dve, s_hshi, 2 * t + b + 1)
                    wait(dve, s_hthi, 2 * t + b + 1)
                    v.tensor_tensor(hs_lo[u][:, 4 * b:4 * b + 4, :],
                                    ps[:, 2 * u + b, :].rearrange("p (k n) -> p k n", n=P),
                                    hs_hi[u][:, 4 * b:4 * b + 4, :].bitcast(f32),
                                    ALU.subtract).then_inc(s_hslo, 1)
                wait(dve, s_hslo, 2 * t + 2)
                v.tensor_copy(h_lo[:, :, bass.ds(t * P, P)], hs_lo[u][:].bitcast(f32)).then_inc(s_htlo, 1)

            def evac_v(j, u):
                t = 2 * j + u
                wait(dve, s_v, t + 1)
                v.tensor_copy(v_raw[:, bass.ds(t, 1), VH:BW],
                              ps[:, 5 + 2 * u, 0:BW - VH].rearrange("p (o n) -> p o n", o=1))
                v.tensor_copy(fz[:, bass.ds(t, 1), :],
                              ps[:, 5 + 2 * u, BW - VH:VH].rearrange("p (o n) -> p o n", o=1)).then_inc(s_vev_d, 1)

            dve.wait_ge(s_gain, 16)
            norm_x(0, 0)
            norm_x(0, 1)
            for i in range(4):
                if i == 1:
                    low_h(0, 0)
                dve.wait_ge(s_wvhi, i + 1)
                v.tensor_tensor(wv_lo[:, 2 * i:2 * i + 2, :], wv_raw[:, 2 * i:2 * i + 2, :],
                                wv_hi[:, 2 * i:2 * i + 2, :].bitcast(f32), ALU.subtract).then_inc(s_wvlo, 1)

            def stage_a(j):
                norm_x(j + 1, 0)
                low_h(j, 1)
                evac_v(j, 0)
                norm_x(j + 1, 1)
                low_h(j + 1, 0)
                evac_v(j, 1)

            stage_a(0)
            with dve.Fori(1, 3) as j:
                stage_a(j)
            low_h(3, 1)
            evac_v(3, 0)
            dve.wait_ge(s_const, 6)
            v.tensor_copy(ident_r[:], ident[:]).then_inc(s_cid, 1)
            v.tensor_copy(mask_r[:], mask_f[:]).then_inc(s_cid, 1)
            evac_v(3, 1)

            dve.wait_ge(s_fb, 16)
            dve.wait_ge(s_vev_d, NT)
            v.tensor_tensor(fz[:], fz[:], fbias[:].rearrange("p (o h) -> p o h", o=1).to_broadcast([P, NT, NH]),
                            ALU.add).then_inc(s_fz, 1)
            dve.wait_ge(s_fz, 1)
            v.tensor_scalar(fa[:], fz[:], -1.0, None, ALU.mult).then_inc(s_fz, 1)
            dve.wait_ge(s_fz, 2)
            v.tensor_tensor(fa[:], fa[:], fz[:], ALU.max).then_inc(s_fz, 1)
            dve.wait_ge(s_fa, 2)
            v.scalar_tensor_tensor(fe[:], fz[:], 0.0, fl[:], ALU.min, ALU.subtract).then_inc(s_fz, 1)
            dve.wait_ge(s_fcum, 1)
            v.tensor_copy(fa[:], ps[:, 0, 0:NT * NH].rearrange("p (t h) -> p t h", h=NH)).then_inc(s_fz, 1)
            for b in range(2):
                dve.wait_ge(s_fhi, 2 * b + 2)
                dst = f_hi[:, 1, HALF * b:HALF * b + HALF]
                v.tensor_tensor(dst.bitcast(f32r), ps[0:NH, 1 + b, :], f_hi[:, 0, HALF * b:HALF * b + HALF],
                                ALU.subtract).then_inc(s_flo, 1)
                dve.wait_ge(s_flo, 2 * b + 1)
                v.tensor_scalar(f_neg[:, 1, HALF * b:HALF * b + HALF], dst, -1.0, None,
                                ALU.mult).then_inc(s_flo, 1)

            def stack_q(p, e):
                r = slice(DH * e, DH * e + DH)
                o = slice(DH * (1 - e), DH * (1 - e) + DH)
                wait(dve, s_pjev, 4 * p + 2)
                wait(dve, s_s, 16 * p + (0 if e else -8))
                wait(dve, s_sta, 2 * (2 * p + e) + 1)
                v.tensor_tensor(q1[e][o, :], q_raw[r, :], q2[e][r, :].bitcast(f32),
                                ALU.subtract).then_inc(s_std, 1)

            def stack_k(p, e):
                r = slice(DH * e, DH * e + DH)
                o = slice(DH * (1 - e), DH * (1 - e) + DH)
                wait(dve, s_pjev, 4 * p + 4)
                v.tensor_copy(k1[e][r, :], k_raw[r, :]).then_inc(s_std, 1)
                v.tensor_copy(k1[e][o, :], k_raw[r, :]).then_inc(s_std, 1)

            def row_max(p, s):
                n = ((s % 8) + 1) * P
                wait(dve, s_s, 16 * p + s + 1)
                wait(dve, s_exp, 16 * p + s - 1)
                b = 1024 * (s % 2)
                v.reduce_max(negmax[s % 2][:], ps_flat[:, b:b + n], axis=AX.X, negate=True).then_inc(s_mx, 1)

            def row_inv(p, s):
                wait(dve, s_exp, 16 * p + s + 1)
                wait(dve, s_phi, 16 * p + s - 1)
                v.reciprocal(rowinv[s % 2][:], rowsum[s % 2][:]).then_inc(s_rc, 1)

            def p_low(p, s):
                n = ((s % 8) + 1) * P
                wait(dve, s_phi, 16 * p + s + 1)
                wait(dve, s_rc, 16 * p + s + 1)
                wait(dve, s_tl, RPAIR * p + RSUM[s - 1] if s > 0 else RPAIR * p - ROUNDS[15])
                v.scalar_tensor_tensor(p_lo[s % 2][:, 0:n], p_raw[s % 2][:, 0:n], rowinv[s % 2][:],
                                       p_hi[s % 2][:, 0:n].bitcast(f32), ALU.mult,
                                       ALU.subtract).then_inc(s_plo, 1)

            def evac_t(p, s):
                i = s % 8
                if i % 4 == 0:
                    wait(dve, s_pv, 4 * p + s // 4)
                for r in range(ROUNDS[s]):
                    n = min(4, i + 1 - 4 * r)
                    wait(dve, s_tl, RPAIR * p + RSUM[s] + r + 1)
                    v.tensor_copy(pt_lo[:, 4 * r:4 * r + n, (i % 4) * P:(i % 4) * P + P],
                                  ps[:, 5, 0:n * P].rearrange("p (k n) -> p k n", n=P)).then_inc(s_evl, 1)

            def evac_pv(p, g4):
                wait(dve, s_pvt, 4 * p + g4 + 1)
                wait(dve, s_atst[g4 % 2], 16 * (2 * p + g4 // 2))
                v.tensor_tensor(at_st[g4 % 2][:], ps[0:DH, 6, :], pv_tmp[:], ALU.add).then_inc(s_pvev, 1)

            dve.wait_ge(s_z, 4)
            stack_q(0, 0)
            stack_k(0, 0)
            row_max(0, 0)
            row_max(0, 1)
            row_inv(0, 0)
            p_low(0, 0)
            row_inv(0, 1)
            row_max(0, 2)
            dve.wait_ge(s_fst, 64)

            def attention(p, last):
                for s in range(16):
                    if s == 0:
                        stack_q(p, 1)
                        stack_k(p, 1)
                    if s < 15 or not last:
                        p_low(p, s + 1)
                    evac_t(p, s)
                    if s < 14 or not last:
                        row_inv(p, s + 2)
                    if s < 13 or not last:
                        row_max(p, s + 3)
                    if s in (4, 8, 12):
                        evac_pv(p, s // 4 - 1)
                    if s == 7 and not last:
                        stack_q(p + 1, 0)
                    if s == 9 and not last:
                        stack_k(p + 1, 0)
                evac_pv(p, 3)

            attention(0, False)
            with dve.Fori(1, 3) as p:
                attention(p, False)
            attention(3, True)

            link = [0]

            def chain(ins):
                link[0] += 1
                ins.then_inc(s_dve, 1)
                dve.wait_ge(s_dve, link[0])

            def pp_low(n):
                g = NG - 1 - n
                for b in range(2):
                    wait(dve, s_pph, 2 * n + b + 1)
                    v.scalar_tensor_tensor(pp_lo[:, g, HALF * b:HALF * b + HALF],
                                           ps[:, 4 + 2 * (n % 2) + b, :], pscale[:, g:g + 1],
                                           pp_hi[:, g, HALF * b:HALF * b + HALF].bitcast(f32),
                                           ALU.mult, ALU.subtract).then_inc(s_ppl, 1)

            for n in range(NG):
                g = NG - 1 - n
                w = 2 << g
                wait(dve, s_uev, 2 * n + 2)
                u = u_sb[n % 2]
                cur = u
                for i in range(g + 1):
                    d = 1 << i
                    nxt = win[i % 2]
                    v.tensor_copy(nxt[:, 0:d], cur[:, 0:d])
                    chain(v.tensor_tensor(nxt[:, d:S], cur[:, d:S], cur[:, 0:S - d], ALU.add))
                    cur = nxt
                wait(dve, s_plh, n)
                wait(dve, s_pll, n)
                v.tensor_tensor(head_tmp[:, 0:w], cur[:, 0:w], inv_cnt[:, 0:w], ALU.mult)
                chain(v.scalar_tensor_tensor(pool[:, w:S], cur[:, w:S], 1.0 / w, u[:, w:S],
                                             ALU.mult, ALU.subtract))
                v.tensor_tensor(pool[:, 0:w], head_tmp[:, 0:w], u[:, 0:w], ALU.subtract).then_inc(s_pool, 1)
                wait(dve, s_plh, n + 1)
                wait(dve, s_mix, 2 * (n - 1))
                v.tensor_tensor(pool_lo[n % 2][:], pool[:], pool_hi[n % 2][:].bitcast(f32),
                                ALU.subtract).then_inc(s_pll, 1)
                if n:
                    pp_low(n - 1)
            pp_low(NG - 1)

            def merge(j):
                for u in range(2):
                    m = 2 * j + u
                    for s_in, s_gate, sig, bank in ((s_py, s_sgp, sig_p, 4), (s_ay, s_sga, sig_a, 6)):
                        for b in range(2):
                            wait(dve, s_gate, 2 * m + b + 1)
                            wait(dve, s_in, 2 * m + b + 1)
                            h = slice(HALF * b, HALF * b + HALF)
                            v.tensor_tensor(sig[:, h], ps[:, bank + b, :], sig[:, h], ALU.mult).then_inc(s_mul, 1)
                    wait(dve, s_mul, 4 * m + 4)
                    v.tensor_tensor(merged[:, bass.ds(m, 1), :],
                                    sig_p[:].rearrange("p (o n) -> p o n", o=1),
                                    sig_a[:].rearrange("p (o n) -> p o n", o=1), ALU.add).then_inc(s_mrg, 1)

            merge(0)
            with dve.Fori(1, KD // 2) as j:
                merge(j)

            def left_low(n, src, k, hh, hi, lo):
                s_ap = (src[:, k, HALF * hh:HALF * hh + HALF] if isinstance(k, int)
                        else src[:, bass.ds(k, 1), HALF * hh:HALF * hh + HALF].rearrange("p o n -> p (o n)"))
                v.tensor_tensor(lo[n % 2][:], s_ap, hi[n % 2][:].bitcast(f32), ALU.subtract).then_inc(s_llo, 1)

            def add_tile(t, n, dst):
                wait(dve, s_tile, n + 1)
                for f in range(2):
                    d = dst[:, HALF * f:HALF * f + HALF]
                    v.tensor_tensor(d, ps[:, 2 * (t % 4) + f, :], d, ALU.add).then_inc(s_add, 1)

            def h2_low(t):
                for b in range(2):
                    wait(dve, s_h2hi, 2 * t + b + 1)
                    hd = h_hi[:, 4 * b:4 * b + 4, t * P:t * P + P]
                    v.tensor_tensor(h_lo[:, 4 * b:4 * b + 4, t * P:t * P + P],
                                    ps[:, 2 * (t if t < 4 else t % 2) + b, :].rearrange("p (k n) -> p k n", n=P),
                                    hd.bitcast(f32), ALU.subtract).then_inc(s_h2lo, 1)

            def norm2(t):
                normalise(KD + t, xn2[:, t, :], x2[:, t, :], s_xn2)

            for n in range(2 * KD):
                dve.wait_ge(s_lhi, n + 1)
                left_low(n, merged, n % KD, n // KD, le_hi, le_lo)
                if n == KD:
                    dve.wait_ge(s_xr[0], 64)
                    dve.wait_ge(s_gain, 32)
                    for t in range(4):
                        add_tile(t, t, x2[:, t, :])
                if KD + 1 < n < KD + 6:
                    norm2(n - 2 - KD)
                if KD < n < KD + 5:
                    variance(n - 1)
            dve.wait_ge(s_xr[1], 64)
            for t in range(4):
                add_tile(4 + t, 4 + t, x2[:, 4 + t, :])
                if t:
                    variance(KD + 3 + t)
                    norm2(3 + t)
            variance(KD + 7)
            norm2(7)
            for t in range(6):
                h2_low(t)

            def silu_half(m, dm, b):
                wait(dve, s_sig, 2 * m + 2 * dm + b + 1)
                wait(dve, s_prod, 2 * m + 2 * dm + b - 1)
                v.tensor_tensor(silu[b][:], ps[:, 4 - 4 * (m % 2) + b, :], sig_g[b][:], ALU.mult).then_inc(s_silu, 1)

            def prod_half(m, dm, b):
                wait(dve, s_fu, 2 * m + 2 * dm + b + 1)
                wait(dve, s_silu, 2 * m + 2 * dm + b + 1)
                v.tensor_tensor(prod[:, bass.ds(m + dm, 1), HALF * b:HALF * b + HALF],
                                ps[:, 6 - 4 * (m % 2) + b, :].rearrange("p (o n) -> p o n", o=1),
                                silu[b][:].rearrange("p (o n) -> p o n", o=1), ALU.mult).then_inc(s_prod, 1)

            def ffn(m, dm, first=False):
                if first:
                    silu_half(m, dm, 0)
                    for t in range(6, 8):
                        h2_low(t)
                    prod_half(m, dm, 0)
                    silu_half(m, dm, 1)
                    prod_half(m, dm, 1)
                    return
                for b in range(2):
                    silu_half(m, dm, b)
                for b in range(2):
                    prod_half(m, dm, b)

            dve.wait_ge(s_x2st, 16 * NT)
            ffn(0, 0, True)
            ffn(1, 0)
            with dve.Fori(1, KF // 2) as j:
                ffn(0, 2 * j)
                ffn(1, 2 * j)

            l0 = 2 * KD

            def down(n, dn, hh, k):
                wait(dve, s_lhi, l0 + n + dn + 1)
                left_low(n, prod, k, hh, lg_hi, lg_lo)

            with dve.Fori(0, KF // 2) as j:
                down(0, 2 * j, 0, 2 * j)
                down(1, 2 * j, 0, 2 * j + 1)
            down(KF, 0, 1, 0)
            dve.wait_ge(s_yld, 16 * 4)
            dve.wait_ge(s_gain, 48)
            for t in range(4):
                add_tile(t, 8 + t, y[:, t, :])
            down(KF + 1, 0, 1, 1)

            def final(n, t):
                variance(16 + n)
                wait(dve, s_out[n % 2], 16 * (n // 2))
                normalise(16 + n, y_out[n % 2][:], y[:, t, :], s_yn)

            for t in range(4):
                down(KF + 2 + t, 0, 1, 2 + t)
                final(t, t)
            with dve.Fori(3, KF // 2) as j:
                down(KF, 2 * j, 1, 2 * j)
                down(KF + 1, 2 * j, 1, 2 * j + 1)
            dve.wait_ge(s_yld, 16 * 8)
            add_tile(4, 12, y[:, 0, :])
            for t in range(4):
                if t < 3:
                    add_tile(5 + t, 13 + t, y[:, 1 + t, :])
                final(4 + t, t)

        @block.tensor
        def _(pe):
            mm = nc.tensor.matmul

            def group(bank, stats, movs, first=True, last=True):
                n = len(stats)
                for i in range(n):
                    ins = mm(bank, stats[i], movs[i], start=first and i == 0, stop=last and i == n - 1)
                return ins

            def three(wh, wl, hh, hl):
                return wh + wh + wl, hh + hl + hh

            def w_tiles(c, k0, n):
                cut = lambda t: [t[c % 2][:, P * k:P * k + P] for k in range(k0, k0 + n)]
                return cut(w_hi), cut(w_lo)

            def cols(hi, lo, b, n):
                cut = lambda t: [t[:, k, HALF * b:HALF * b + HALF] for k in range(n)]
                return cut(hi), cut(lo)

            def column_product(c, b, bank):
                return group(ps[:, bank, :], *three(*w_tiles(c, 0, KD), *cols(h_hi, h_lo, b, KD)))

            def transpose_x(j, u):
                t = 2 * j + u
                wait(pe, s_xn, t + 1)
                wait(pe, s_hthi, 2 * (t - 1))
                wait(pe, s_hslo, 2 * (t - 1))
                for b in range(2):
                    for k in range(4):
                        ins = nc.tensor.transpose(ps[:, 2 * u + b, P * k:P * k + P],
                                                  xn[u][:, (4 * b + k) * P:(4 * b + k + 1) * P], ident[:])
                    ins.then_inc(s_tp, 1)

            def v_product(j, u):
                t = 2 * j + u
                wait(pe, s_htlo, t + 1)
                wait(pe, s_hthi, 2 * t + 2)
                wait(pe, s_vev_a, t - 1)
                wait(pe, s_vev_d, t - 1)
                for k in range(KD):
                    if isinstance(t, int) and t == 0 and k % 2 == 0:
                        pe.wait_ge(s_wvlo, k // 2 + 1)
                    for i, (l, r) in enumerate(((hs_hi, wv_hi), (hs_hi, wv_lo), (hs_lo, wv_hi))):
                        for b in range(2):
                            ins = mm(ps[:, 4 + 2 * u + b, 0:VH], l[u][:, k, :], r[:, k, VH * b:VH * b + VH],
                                     start=(k == 0 and i == 0), stop=(k == KD - 1 and i == 2))
                ins.then_inc(s_v, 1)

            pe.wait_ge(s_const, 1)
            transpose_x(0, 0)

            def stage_a(j):
                transpose_x(j, 1)
                v_product(j, 0)
                transpose_x(j + 1, 0)
                v_product(j, 1)

            stage_a(0)
            with pe.Fori(1, 3) as j:
                stage_a(j)
            transpose_x(3, 1)
            v_product(3, 0)
            v_product(3, 1)

            pe.wait_ge(s_htlo, NT)
            pe.wait_ge(s_hthi, 2 * NT)
            pe.wait_ge(s_vev_a, NT)
            pe.wait_ge(s_vev_d, NT)
            for n in range(4):
                if n % 2 == 0:
                    wait(pe, s_wlo, 1 + n // 2)
                column_product(n // 2, n % 2, 7 - n).then_inc(s_pj, 1)
                if n == 0:
                    pe.wait_ge(s_fz, 4)
                    mm(ps[:, 0, 0:NT * NH], tri[:], fe[:].rearrange("p t h -> p (t h)"), start=True, stop=False)
                    for t in range(NT - 1):
                        rest = NT - 1 - t
                        ins = mm(ps[:, 0, NH * (t + 1):NH * NT].rearrange("p (t h) -> p t h", h=NH), ones[:],
                                 fe[:, t:t + 1, :].to_broadcast([P, rest, NH]),
                                 start=False, stop=(t == NT - 2))
                    ins.then_inc(s_fcum, 1)
                if n == 1:
                    pe.wait_ge(s_fz, 5)
                    for b in range(2):
                        for t in range(4):
                            ins = nc.tensor.transpose(ps[0:NH, 1 + b, P * t:P * t + P], fa[:, 4 * b + t, :], ident[:])
                        ins.then_inc(s_frow, 1)

            def scores(p, s):
                e, i = (s // 8) % 2, s % 8
                n = (i + 1) * P
                if i == 0:
                    b = 2 * p + s // 8
                    wait(pe, s_sta, 2 * (b + 1))
                    wait(pe, s_std, 3 * (b + 1))
                    wait(pe, s_stp, b + 1)
                    wait(pe, s_frd[e], 32 * (p + s // 16 + 1))
                wait(pe, s_exp, 16 * p + s - 1)
                qt = slice(i * P, i * P + P)
                for h in range(0, n, HALF):
                    w = min(HALF, n - h)
                    bank = ps[:, 2 * (s % 2) + h // HALF, :]
                    diag = h + w == n
                    mm(bank[:, 0:w], q1[e][:, qt], k1[e][:, h:h + w], start=True, stop=False)
                    ins = mm(bank[:, 0:w], q2[e][:, qt], k2[e][:, h:h + w], start=False, stop=not diag)
                    if diag:
                        ins = mm(bank[:, w - P:w], ident_r[:], mask_r[:], start=False, stop=True)
                ins.then_inc(s_s, 1)

            def transposes(p, s, r):
                i = s % 8
                n = min(4, i + 1 - 4 * r)
                for src, ready, free, done, bank in ((p_hi, s_phi, s_evh, s_th, 4), (p_lo, s_plo, s_evl, s_tl, 5)):
                    if r == 0:
                        wait(pe, ready, 16 * p + s + 1)
                    wait(pe, free, RPAIR * p + RSUM[s] + r)
                    for k in range(n):
                        ins = nc.tensor.transpose(ps[:, bank, P * k:P * k + P].bitcast(f32r),
                                                  src[s % 2][:, (4 * r + k) * P:(4 * r + k + 1) * P], ident_r[:])
                    ins.then_inc(done, 1)

            def values(p, s):
                e, g = s // 8, (s % 8) // 4
                wait(pe, s_vslo, 2 * p + e + 1)
                wait(pe, s_evh, RPAIR * p + RSUM[s + 1])
                wait(pe, s_evl, RPAIR * p + RSUM[s + 1])
                wait(pe, s_pvev, 4 * p + s // 4)
                nk = 4 * g + 4
                for x_, pt in enumerate((pt_hi, pt_lo)):
                    for k in range(nk):
                        q0 = max(0, k - 4 * g) * P
                        ins = mm(ps[:, 6, q0:HALF], vs[e][:, k, :], pt[:, k, q0:HALF],
                                 start=(x_ == 0 and k == 0), stop=(x_ == 1 and k == nk - 1))
                ins.then_inc(s_pv, 1)

            def next_pair(p, s):
                n, a, b = FILL[s]
                if a == 0:
                    wait(pe, s_pjev, 4 * (p + 1) + n)
                    if n % 2 == 0:
                        wait(pe, s_wlo, 2 * p + 3 + n // 2)
                st, mv = three(*w_tiles(n // 2, 0, KD), *cols(h_hi, h_lo, n % 2, KD))
                ins = group(ps[:, 7, :], st[a:b], mv[a:b], first=(a == 0), last=(b == 3 * KD))
                if b == 3 * KD:
                    ins.then_inc(s_pj, 1)

            pe.wait_ge(s_cid, 6)
            pe.wait_ge(s_flo, 4)
            pe.wait_ge(s_fhi, 4)
            for s in range(AHEAD):
                scores(0, s)

            def attention(p, last):
                for s in range(16):
                    if s < len(FILL) and not last:
                        next_pair(p, s)
                    transposes(p, s, 0)
                    if s + AHEAD < 16 or not last:
                        scores(p, s + AHEAD)
                    if ROUNDS[s] == 2:
                        transposes(p, s, 1)
                    if s % 4 == 3:
                        values(p, s)

            attention(0, False)
            with pe.Fori(1, 3) as p:
                attention(p, False)
            attention(3, True)

            def mix(n):
                g = NG - 1 - n
                wait(pe, s_mixlo, 1)
                wait(pe, s_plh, n + 1)
                wait(pe, s_pll, n + 1)
                wait(pe, s_pph, 2 * (n - 1))
                wait(pe, s_ppl, 2 * (n - 1))
                for b in range(2):
                    h = slice(HALF * b, HALF * b + HALF)
                    w, l = mix_hi[:, g, :], mix_lo[:, g, :]
                    hi, lo = pool_hi[n % 2][:, h], pool_lo[n % 2][:, h]
                    group(ps[:, 4 + 2 * (n % 2) + b, :], [w, w, l], [hi, lo, hi]).then_inc(s_mix, 1)

            pe.wait_ge(s_exp, 64)
            pe.wait_ge(s_evh, 4 * RPAIR)
            pe.wait_ge(s_evl, 4 * RPAIR)
            for n in range(NG):
                wait(pe, s_wlo, C_U + n + 1)
                wait(pe, s_uev, 2 * (n - 1))
                for b in range(2):
                    column_product(C_U + n, b, 2 * (n % 2) + b).then_inc(s_u, 1)
                if n == 0:
                    pe.wait_ge(s_pvev, 16)
                if n:
                    mix(n - 1)

            pe.wait_ge(s_uev, 2 * NG)

            def gated(j):
                for u in range(2):
                    m, c = 2 * j + u, C_GATE + 3 * u
                    for i, (done, free, bank) in enumerate(((s_gp, s_sgp, 0), (s_ga, s_sga, 2))):
                        wait(pe, s_wlo, c + i + 1 + 6 * j)
                        wait(pe, free, 2 * m)
                        for b in range(2):
                            column_product(c + i, b, bank + b).then_inc(done, 1)
                    wait(pe, s_wlo, c + 3 + 6 * j)
                    wait(pe, s_mrg, m)
                    if isinstance(m, int) and m == 0:
                        mix(NG - 1)
                        pe.wait_ge(s_ppl, 2 * NG)
                        pe.wait_ge(s_pph, 2 * NG)
                        pe.wait_ge(s_alo, NG)
                    for hi, lo, k0, done, bank in ((pp_hi, pp_lo, 0, s_py, 4), (a_hi, a_lo, 4, s_ay, 6)):
                        for b in range(2):
                            group(ps[:, bank + b, :],
                                  *three(*w_tiles(c + 2, k0, 4), *cols(hi, lo, b, 4))).then_inc(done, 1)

            gated(0)
            with pe.Fori(1, KD // 2) as j:
                gated(j)

            def row_tile(t, n, c, lhi, llo, first, last):
                cut = slice(P * t, P * t + P)
                hi, lo = lhi[n % 2][:, cut], llo[n % 2][:, cut]
                whi, wlo = (w_end_hi, w_end_lo) if c in (C_FFN - 1, C_END - 1) else (w_hi[c % 2], w_lo[c % 2])
                for i, (l, w) in enumerate(((hi, whi), (hi, wlo), (lo, whi))):
                    for f in range(2):
                        ins = mm(ps[:, 2 * t + f, :], l, w[:, HALF * f:HALF * f + HALF],
                                 start=first and i == 0, stop=last and i == 2)
                return ins

            def row_step(n, c, lhi, llo, first, last, free=None):
                for t in range(4):
                    if free is not None:
                        free(t)
                    ins = row_tile(t, n, c, lhi, llo, first, last)
                    if last:
                        ins.then_inc(s_tile, 1)
                if not last:
                    ins.then_inc(s_kused, 1)

            def row_end(n, c, lhi, llo, l0=0):
                pe.wait_ge(s_wlo, c + 1)
                pe.wait_ge(s_llo, l0 + n + 1)
                for t in range(4):
                    row_tile(t, n, c, lhi, llo, False, False)
                    if t == 0:
                        pe.wait_ge(s_wlo, c + 2)
                        pe.wait_ge(s_llo, l0 + n + 2)
                    row_tile(t, n + 1, c + 1, lhi, llo, False, True).then_inc(s_tile, 1)

            def free_e(t):
                if t < 2:
                    pe.wait_ge(s_sga, 2 * KD)
                else:
                    pe.wait_ge(s_mul, 4 * KD - 6 + 2 * t)

            for n in range(2 * KD - 2):
                pe.wait_ge(s_wlo, C_OUT + n + 1)
                pe.wait_ge(s_llo, n + 1)
                row_step(n, C_OUT + n, le_hi, le_lo, n % KD == 0, n % KD == KD - 1,
                         free_e if n == 0 else (lambda t: pe.wait_ge(s_add, 2 * t + 2)) if n == KD else None)
            row_end(2 * KD - 2, C_OUT + 2 * KD - 2, le_hi, le_lo)

            def transpose_h2(t):
                pair = t if t < 4 else t % 2
                wait(pe, s_xn2, t + 1)
                wait(pe, s_add, 2 * (5 + t) if t < 4 else 16)
                if t >= 4:
                    before = t - 4 if t < 6 else t - 2
                    wait(pe, s_h2lo, 2 * (before + 1))
                    wait(pe, s_h2hi, 2 * (before + 1))
                for b in range(2):
                    for k in range(4):
                        ins = nc.tensor.transpose(ps[:, 2 * pair + b, P * k:P * k + P],
                                                  xn2[:, t, (4 * b + k) * P:(4 * b + k + 1) * P], ident[:])
                    ins.then_inc(s_tp2, 1)

            for t in range(6):
                transpose_h2(t)

            def ffn(m, dm):
                for i, done in enumerate((s_fg, s_fu)):
                    wait(pe, s_wlo, C_FFN + 2 * m + i + 1 + 2 * dm)
                    wait(pe, s_silu if i == 0 else s_prod, 2 * m + 2 * dm - 2)
                    for b in range(2):
                        column_product(C_FFN + i, b, 4 - 4 * (m % 2) + 2 * i + b).then_inc(done, 1)

            for b in range(2):
                pe.wait_ge(s_h2lo, NT * (b + 1))
                pe.wait_ge(s_h2hi, NT * (b + 1))
                for i, done in enumerate((s_fg, s_fu)):
                    wait(pe, s_wlo, C_FFN + i + 1)
                    column_product(C_FFN + i, b, 4 + 2 * i + b).then_inc(done, 1)
                    if b == 0 and i == 0:
                        for t in range(6, 8):
                            transpose_h2(t)
            ffn(1, 0)
            with pe.Fori(1, KF // 2) as j:
                ffn(0, 2 * j)
                ffn(1, 2 * j)

            pe.wait_ge(s_prod, 2 * KF)
            l0 = 2 * KD

            def down(n, dn, first=False, last=False, free=None):
                wait(pe, s_wlo, C_DOWN + n + 1 + dn)
                wait(pe, s_llo, l0 + n + 1 + dn)
                row_step(n, C_DOWN + n, lg_hi, lg_lo, first, last, free)

            for hh in range(2):
                n0 = KF * hh
                down(n0, 0, first=True, free=(lambda t: pe.wait_ge(s_add, 18 + 2 * t)) if hh else None)
                down(n0 + 1, 0)
                with pe.Fori(1, KF // 2 - 1) as j:
                    down(n0, 2 * j)
                    down(n0 + 1, 2 * j)
                if hh == 0:
                    down(n0 + KF - 2, 0)
                    down(n0 + KF - 1, 0, last=True)
            row_end(2 * KF - 2, C_END - 2, lg_hi, lg_lo, l0)


_INS = ["x", "norm1_g", "w_in", "b_forget", "pool_mix", "pool_scale", "w_pool_out", "w_attn_out",
        "w_out", "norm2_g", "w_ffn_gate", "w_ffn_up", "w_ffn_down", "norm_f_g"]


def kernel(**inputs):
    import numpy as np
    import concourse.bacc as bacc
    from concourse.bass_utils import run_bass_kernel_spmd

    nc = bacc.Bacc("TRN2", target_bir_lowering=False, num_devices=1, dynamic_dma_scratch_size=1024)
    arrays, args = {}, []
    for name in _INS:
        a = np.ascontiguousarray(inputs[name])
        arrays[f"in_{name}"] = a
        args.append(nc.dram_tensor(f"in_{name}", a.shape, mybir.dt.from_np(a.dtype), kind="ExternalInput").ap())
    out = nc.dram_tensor("out_0", (1, S, D), mybir.dt.float32, kind="ExternalOutput").ap()
    hybrid_block(nc, *args, out)
    r = run_bass_kernel_spmd(nc, [arrays], core_ids=[0])
    return r.results[0]["out_0"]
```

```python
import concourse.bass as bass
from concourse import mybir
from contextlib import ExitStack

P = 128
S = 1024
D = 1024
NT = S // P
KD = D // P
HALF = 512
BW = 512
NH = 8
DH = 64
NG = 4
DFF = 2816
KF = DFF // P
EPS = 1e-6
NEG = -1.0e30
COL_U, COL_Q, COL_K, COL_V = 0, BW, 2 * BW, 3 * BW
COL_F = 4 * BW
COL_GP = COL_F + NH
COL_GA = COL_GP + D
VF = BW + NH
VH = VF // 2

C_U3 = 14
C_GATE = C_U3 + 1
C_OUT = C_GATE + 3 * KD
C_FFN = C_OUT + 2 * KD
C_DOWN = C_FFN + 2 * KF
C_END = C_DOWN + 2 * KF

ROUNDS = [1 if (s % 8) < 4 else 2 for s in range(16)]
RSUM = [0]
for _s in range(32):
    RSUM.append(RSUM[-1] + ROUNDS[_s % 16])
RPAIR = RSUM[16]
FILL = {1: (0, 0, 8), 2: (0, 8, 16), 3: (0, 16, 24), 4: (1, 0, 12), 5: (1, 12, 24),
        6: (2, 0, 8), 7: (2, 8, 16), 8: (2, 16, 24), 9: (3, 0, 12), 10: (3, 12, 24),
        11: (4, 0, 12), 12: (4, 12, 24), 13: (5, 0, 8), 14: (5, 8, 16), 15: (5, 16, 24)}
FILL_LAST = {1: (4, 0, 8), 2: (4, 8, 16), 3: (4, 16, 24), 4: (5, 0, 12), 5: (5, 12, 24),
             6: (6, 0, 12), 7: (6, 12, 24), 8: (7, 0, 12), 9: (7, 12, 24),
             10: (8, 0, 8), 11: (8, 8, 16), 12: (8, 16, 24), 13: (9, 0, 8), 14: (9, 8, 16), 15: (9, 16, 24)}
AHEAD = 3


def wait(eng, sem, value):
    if not isinstance(value, int) or value > 0:
        eng.wait_ge(sem, value)


def qk_units(p, n):
    return n + 1 if isinstance(p, int) and p == 0 else 6 * p - 1 + n


def fill_units(p, n, last):
    return 4 + 6 * 3 + n - 4 if last else 6 * p + 4 + n


def hybrid_block(nc, x, norm1_g, w_in, b_forget, pool_mix, pool_scale, w_pool_out, w_attn_out,
                 w_out, norm2_g, w_gate, w_up, w_down, norm_f_g, out):
    f32, f32r = mybir.dt.float32, mybir.dt.float32r
    ACT, ALU, AX = mybir.ActivationFunctionType, mybir.AluOpType, mybir.AxisListType

    x_d = x[0].rearrange("(t p) d -> t p d", p=P)
    out_d = out[0].rearrange("(t p) d -> t p d", p=P)
    win_d = w_in[0].rearrange("(k p) m -> p k m", p=P)
    wpool_d = w_pool_out[0].rearrange("(k p) m -> p k m", p=P)
    wattn_d = w_attn_out[0].rearrange("(k p) m -> p k m", p=P)
    wout_d = w_out[0].rearrange("(k p) m -> k p m", p=P)
    wgate_d = w_gate[0].rearrange("(k p) m -> p k m", p=P)
    wup_d = w_up[0].rearrange("(k p) m -> p k m", p=P)
    wdown_d = w_down[0].rearrange("(k p) m -> k p m", p=P)
    mix_d = pool_mix[0].rearrange("g c d -> c g d")
    scale_d = pool_scale[0].rearrange("(g c) -> g c", c=P)
    frow_q = nc.dram_tensor("frow_q", (NH, 4, S), f32, kind="Internal").ap()
    frow_k = nc.dram_tensor("frow_k", (NH, 4, S), f32, kind="Internal").ap()
    at_d = nc.dram_tensor("at_d", (NH, DH, S), f32, kind="Internal").ap()
    at_rows = at_d.rearrange("h d t -> (h d) t")
    u_d = nc.dram_tensor("u_d", (NG, P, S), f32, kind="Internal").ap()
    x2_d = nc.dram_tensor("x2_d", (NT, P, D), f32, kind="Internal").ap()

    ctx = ExitStack()
    with ctx:
        base = -(-nc.sbuf_base // 32) * 32
        slab_words = (nc.sbuf_usable_end - base) // 4 // 8 * 8 - 16
        ctx.enter_context(nc.sbuf_tensor("slab", [P, slab_words], f32))
        end = base + slab_words * 4
        at = [base]

        def place(name, shape, dt=f32):
            n = 4
            for d in shape[1:]:
                n *= d
            t = nc.alloc_sbuf_tensor_at(name, shape, dt, offset=at[0])
            at[0] += -(-n // 32) * 32
            assert at[0] <= end, (name, at[0] - end)
            return t

        w_raw = [place(f"w_raw{i}", [P, 1024]) for i in range(2)]
        w_hi = [place(f"w_hi{i}", [P, 1024], f32r) for i in range(2)]
        w_lo = [place(f"w_lo{i}", [P, 1024], f32r) for i in range(2)]
        at_h = at[0]
        h_hi = place("h_hi", [P, KD, S], f32r)
        h_lo = place("h_lo", [P, KD, S], f32r)
        gain_at = at[0]
        u_st = place("u_st", [P, S])
        at[0] = gain_at
        gain = place("gain", [P, D])
        ident = place("ident", [P, P])
        ident_r = place("ident_r", [P, P], f32r)
        mask_f = place("mask_f", [P, P])
        mask_r = place("mask_r", [P, P], f32r)
        tri = place("tri", [P, P])
        ones = place("ones", [P, P])
        neg_half = place("neg_half", [P, 1])
        ssq = place("ssq", [P, 24])
        var = place("var", [P, 24])
        rstd = place("rstd", [P, 24])
        negmax = [place(f"negmax{i}", [P, 1]) for i in range(2)]
        rowsum = [place(f"rowsum{i}", [P, 1]) for i in range(2)]
        rowinv = [place(f"rowinv{i}", [P, 1]) for i in range(2)]
        pscale = place("pscale", [P, NG])
        inv_cnt = place("inv_cnt", [P, 16])
        phase = at[0]

        v_raw = place("v_raw", [P, NT, BW])
        after_v = at[0]
        xt = [place(f"xt{i}", [P, D]) for i in range(2)]
        xn = [place(f"xn{i}", [P, D]) for i in range(2)]
        wv_raw = place("wv_raw", [P, KD, VF])
        wv_hi = place("wv_hi", [P, KD, VF], f32r)
        wv_lo = place("wv_lo", [P, KD, VF], f32r)
        hs_hi = [place(f"hs_hi{i}", [P, KD, P], f32r) for i in range(2)]
        hs_lo = [place(f"hs_lo{i}", [P, KD, P], f32r) for i in range(2)]
        f_hi = place("f_hi", [NH, 2, S])
        f_neg = place("f_neg", [NH, 2, S])
        f_one = place("f_one", [NH, 2, S])
        fz = place("fz", [P, NT, NH])
        fa = place("fa", [P, NT, NH])
        fe = place("fe", [P, NT, NH])
        fl = place("fl", [P, NT, NH])
        fbias = place("fbias", [P, NH])
        at[0] = after_v
        vs = [place(f"vs{i}", [P, NT, 2 * DH], f32r) for i in range(2)]
        at_st = [place(f"at_st{i}", [DH, HALF]) for i in range(2)]
        q1 = [place(f"q1_{i}", [P, S], f32r) for i in range(2)]
        q2 = [place(f"q2_{i}", [P, S], f32r) for i in range(2)]
        k1 = [place(f"k1_{i}", [P, S], f32r) for i in range(2)]
        k2 = [place(f"k2_{i}", [P, S], f32r) for i in range(2)]
        q_raw = place("q_raw", [P, S])
        k_raw = place("k_raw", [P, S])
        p_raw = [place(f"p_raw{i}", [P, S]) for i in range(2)]
        p_hi = [place(f"p_hi{i}", [P, S], f32r) for i in range(2)]
        p_lo = [place(f"p_lo{i}", [P, S], f32r) for i in range(2)]
        pt_hi = place("pt_hi", [P, NT, HALF], f32r)
        pt_lo = place("pt_lo", [P, NT, HALF], f32r)
        pv_tmp = place("pv_tmp", [DH, HALF])
        at[0] = phase
        a_hi = place("a_hi", [P, NG, S], f32r)
        a_lo = place("a_lo", [P, NG, S], f32r)
        pp_hi = place("pp_hi", [P, NG, S], f32r)
        pp_lo = place("pp_lo", [P, NG, S], f32r)
        after_branches = at[0]
        a_raw = [place(f"a_raw{i}", [P, S]) for i in range(2)]
        u_sb = [place(f"u_sb{i}", [P, S]) for i in range(2)]
        win = [place(f"win{i}", [P, S]) for i in range(2)]
        pool = place("pool", [P, S])
        head_tmp = place("head_tmp", [P, 16])
        pool_hi = [place(f"pool_hi{i}", [P, S], f32r) for i in range(2)]
        pool_lo = [place(f"pool_lo{i}", [P, S], f32r) for i in range(2)]
        mix_raw = place("mix_raw", [P, NG, P])
        mix_hi = place("mix_hi", [P, NG, P], f32r)
        mix_lo = place("mix_lo", [P, NG, P], f32r)
        sig_p = place("sig_p", [P, S])
        sig_a = place("sig_a", [P, S])
        at_sig = at[0] - 2 * 4 * S
        at[0] = after_branches
        merged = place("merged", [P, KD, S])
        after_merged = at[0]
        at[0] = phase
        x2 = place("x2", [P, NT, D])
        xn2 = place("xn2", [P, NT, D])
        assert at[0] <= after_branches
        at[0] = after_merged
        le_hi = [place(f"le_hi{i}", [P, HALF], f32r) for i in range(2)]
        le_lo = [place(f"le_lo{i}", [P, HALF], f32r) for i in range(2)]
        junk_e = place("junk_e", [P, D])
        at_le = at[0]
        last_e = [place(f"last_e{i}", [P, 1024], f32r) for i in range(2)]
        assert at_le <= at_sig
        at[0] = phase
        prod = place("prod", [P, KF, S])
        after_prod = at[0]
        sig_g = [place(f"sig_g{i}", [P, HALF]) for i in range(2)]
        silu = [place(f"silu{i}", [P, HALF]) for i in range(2)]
        lg_hi = [place(f"lg_hi{i}", [P, HALF], f32r) for i in range(2)]
        lg_lo = [place(f"lg_lo{i}", [P, HALF], f32r) for i in range(2)]
        y = place("y", [P, 4, D])
        junk_g = place("junk_g", [P, D])
        at[0] = after_prod
        y_out = [place(f"y_out{i}", [P, D]) for i in range(2)]
        at[0] = at_h
        last_g = [place(f"last_g{i}", [P, 1024], f32r) for i in range(2)]
        last_chunk = {C_FFN - 1: last_e, C_END - 1: last_g}

        def chunk_parts(c):
            return last_chunk.get(c, (w_hi[c % 2], w_lo[c % 2]))

        ps = ctx.enter_context(nc.psum_tensor("ps", [P, 8, HALF], f32))
        ps_flat = ps[:].rearrange("p b n -> p (b n)")

        def sem(name):
            return ctx.enter_context(nc.semaphore(name))

        s_wraw = [sem(f"s_wraw{i}") for i in range(2)]
        s_whi, s_wlo = sem("s_whi"), sem("s_wlo")
        s_gain = sem("s_gain")
        s_const = sem("s_const")
        s_cid = sem("s_cid")
        s_x = [sem(f"s_x{i}") for i in range(2)]
        s_wv = [sem(f"s_wv{i}") for i in range(4)]
        s_wvhi, s_wvlo = sem("s_wvhi"), sem("s_wvlo")
        s_fb = sem("s_fb")
        s_sq, s_var, s_rstd = sem("s_sq"), sem("s_var"), sem("s_rstd")
        s_xn = sem("s_xn")
        s_tp = sem("s_tp")
        s_hshi, s_hthi = sem("s_hshi"), sem("s_hthi")
        s_hslo, s_htlo = sem("s_hslo"), sem("s_htlo")
        s_v = sem("s_v")
        s_vev_a, s_vev_d = sem("s_vev_a"), sem("s_vev_d")
        s_fz, s_fa, s_fcum, s_frow = sem("s_fz"), sem("s_fa"), sem("s_fcum"), sem("s_frow")
        s_fhi, s_flo = sem("s_fhi"), sem("s_flo")
        s_fst = sem("s_fst")
        s_pj, s_pjev = sem("s_pj"), sem("s_pjev")
        s_sta, s_std, s_stp = sem("s_sta"), sem("s_std"), sem("s_stp")
        s_frd = [sem(f"s_frd{i}") for i in range(2)]
        s_z = sem("s_z")
        s_vshi, s_vslo = sem("s_vshi"), sem("s_vslo")
        s_s, s_mx, s_exp, s_rc = sem("s_s"), sem("s_mx"), sem("s_exp"), sem("s_rc")
        s_phi, s_plo = sem("s_phi"), sem("s_plo")
        s_th, s_tl = sem("s_th"), sem("s_tl")
        s_evh, s_evl = sem("s_evh"), sem("s_evl")
        s_pv, s_pvt, s_pvev = sem("s_pv"), sem("s_pvt"), sem("s_pvev")
        s_atst = [sem(f"s_atst{i}") for i in range(2)]
        s_ust = sem("s_ust")
        s_uld = [sem(f"s_uld{i}") for i in range(2)]
        s_dve = sem("s_dve")
        s_pool, s_plh, s_pll = sem("s_pool"), sem("s_plh"), sem("s_pll")
        s_mixw, s_mixhi, s_mixlo = sem("s_mixw"), sem("s_mixhi"), sem("s_mixlo")
        s_mix, s_pph, s_ppl = sem("s_mix"), sem("s_pph"), sem("s_ppl")
        s_araw = [sem(f"s_araw{i}") for i in range(2)]
        s_ahi, s_alo = sem("s_ahi"), sem("s_alo")
        s_gp, s_ga, s_py, s_ay = sem("s_gp"), sem("s_ga"), sem("s_py"), sem("s_ay")
        s_sgp, s_sga, s_mul, s_mrg = sem("s_sgp"), sem("s_sga"), sem("s_mul"), sem("s_mrg")
        s_lhi, s_llo = sem("s_lhi"), sem("s_llo")
        s_kused, s_tile = sem("s_kused"), sem("s_tile")
        s_add = sem("s_add")
        s_xr = [sem(f"s_xr{i}") for i in range(2)]
        s_x2st = sem("s_x2st")
        s_xn2, s_tp2, s_h2hi, s_h2lo = sem("s_xn2"), sem("s_tp2"), sem("s_h2hi"), sem("s_h2lo")
        s_fg, s_fu, s_sig, s_silu, s_prod = sem("s_fg"), sem("s_fu"), sem("s_sig"), sem("s_silu"), sem("s_prod")
        s_yld = sem("s_yld")
        s_yn = sem("s_yn")
        s_out = [sem(f"s_out{i}") for i in range(2)]

        block = ctx.enter_context(nc.Block())

        @block.sync
        def _(sp):
            def load_chunk(c, dc, src0, src1):
                wait(sp, s_wlo, c - 1 + dc)
                sp.dma_start(w_raw[c % 2][:, 0:512], src0).then_inc(s_wraw[c % 2], 16)
                sp.dma_start(w_raw[c % 2][:, 512:1024], src1).then_inc(s_wraw[c % 2], 16)

            def load_cols(c, dc, w, col):
                wait(sp, s_wlo, c - 1 + dc)
                for j in range(2):
                    sp.dma_start(w_raw[c % 2][:, 512 * j:512 * j + 512].rearrange("p (k m) -> p k m", m=P),
                                 w[:, 4 * j:4 * j + 4, bass.ds(col, P)]).then_inc(s_wraw[c % 2], 16)

            def load_half(c, w, col, k0):
                wait(sp, s_wlo, c - 1)
                for j in range(2):
                    sp.dma_start(w_raw[c % 2][:, 256 * j:256 * j + 256].rearrange("p (k m) -> p k m", m=P),
                                 w[:, k0 + 2 * j:k0 + 2 * j + 2, col:col + P]).then_inc(s_wraw[c % 2], 16)

            def load_x(j, u):
                wait(sp, s_xn, 2 * j + u - 1)
                sp.dma_start(xt[u][:], x_d[2 * j + u]).then_inc(s_x[u], 16)

            load_x(0, 0)
            sp.dma_start(gain[:], norm1_g[0].partition_broadcast(P)).then_inc(s_gain, 16)
            for i in range(4):
                if i == 2:
                    load_x(0, 1)
                sp.dma_start(wv_raw[:, 2 * i:2 * i + 2, :],
                             win_d[:, 2 * i:2 * i + 2, COL_V:COL_V + VF]).then_inc(s_wv[i], 16)
            sp.dma_start(fbias[:], b_forget[0].partition_broadcast(P)).then_inc(s_fb, 16)
            load_cols(0, 0, win_d, COL_Q)
            load_cols(1, 0, win_d, COL_K)
            for j in range(1, 4):
                for u in range(2):
                    load_x(j, u)
            load_cols(2, 0, win_d, COL_Q + P)
            load_cols(3, 0, win_d, COL_K + P)

            wait(sp, s_flo, 4)
            wait(sp, s_fhi, 4)
            wait(sp, s_const, 6)
            sp.dma_start(frow_q[:, 0:2, :], f_hi[:]).then_inc(s_fst, 16)
            sp.dma_start(frow_q[:, 2:4, :], f_one[:]).then_inc(s_fst, 16)
            sp.dma_start(frow_k[:, 0:2, :], f_one[:]).then_inc(s_fst, 16)
            sp.dma_start(frow_k[:, 2:4, :], f_neg[:]).then_inc(s_fst, 16)
            wait(sp, s_fst, 64)

            def load_frows(p, e):
                r0 = DH * (1 - e)
                sp.dma_start(q2[e][r0:r0 + 4, :].bitcast(f32), frow_q[2 * p + e]).then_inc(s_frd[e], 16)
                sp.dma_start(k2[e][r0:r0 + 4, :].bitcast(f32), frow_k[2 * p + e]).then_inc(s_frd[e], 16)

            def store_at(p, g4):
                wait(sp, s_pvev, 4 * p + g4 + 1)
                sp.dma_start(at_d[2 * p + g4 // 2, :, HALF * (g4 % 2):HALF * (g4 % 2) + HALF],
                             at_st[g4 % 2][:]).then_inc(s_atst[g4 % 2], 16)

            wait(sp, s_z, 4)
            load_frows(0, 0)
            def load_branches(c, dc, col):
                wait(sp, s_wlo, c - 1 + dc)
                for i, w in enumerate((wpool_d, wattn_d)):
                    sp.dma_start(w_raw[c % 2][:, 512 * i:512 * i + 512].rearrange("p (k m) -> p k m", m=P),
                                 w[:, :, bass.ds(col, P)]).then_inc(s_wraw[c % 2], 16)

            for p in range(4):
                if p < 3:
                    load_half(4 * p + 4, win_d, COL_U + P * p, 0)
                    load_half(4 * p + 5, win_d, COL_U + P * p, 4)
                else:
                    load_cols(C_GATE + 1, 0, win_d, COL_GA)
                wait(sp, s_s, 16 * p)
                load_frows(p, 1)
                store_at(p, 0)
                if p < 3:
                    wait(sp, s_s, 16 * p + 8)
                    load_frows(p + 1, 0)
                    load_cols(4 * p + 6, 0, win_d, COL_Q + P * (p + 2) if p < 2 else COL_U + P * 3)
                else:
                    load_cols(C_GATE + 2, 0, win_d, COL_GP + P)
                store_at(p, 1)
                if p < 3:
                    load_cols(4 * p + 7, 0, win_d, COL_K + P * (p + 2) if p < 2 else COL_GP)
                else:
                    load_cols(C_GATE + 3, 0, win_d, COL_GA + P)
                store_at(p, 2)
                if p == 3:
                    load_branches(C_GATE + 4, 0, 0)
                store_at(p, 3)
                if p < 3:
                    wait(sp, s_pjev, fill_units(p, 6, False))
                    sp.dma_start(u_d[p], u_st[:]).then_inc(s_ust, 16)

            wait(sp, s_atst[0], 16 * 8)
            wait(sp, s_atst[1], 16 * 8)
            wait(sp, s_pvev, 16)
            wait(sp, s_ust, 16 * 3)
            for n in range(1, 3):
                sp.dma_start(u_sb[n % 2][:], u_d[NG - 1 - n]).then_inc(s_uld[n % 2], 16)
            sp.dma_start(mix_raw[:], mix_d).then_inc(s_mixw, 16)
            for g in range(NG):
                sp.dma_start(pscale[:, g:g + 1], scale_d[g].rearrange("(c o) -> c o", o=1),
                             allow_slow_non_contiguous=True).then_inc(s_mixw, 16)
            wait(sp, s_sga, 2)
            for n in range(2):
                sp.dma_start(a_raw[n][:], at_rows[P * n:P * n + P, :]).then_inc(s_araw[n], 16)
            for n in range(2, 4):
                wait(sp, s_alo, n - 1)
                sp.dma_start(a_raw[n % 2][:], at_rows[P * n:P * n + P, :]).then_inc(s_araw[n % 2], 16)

            wait(sp, s_pool, 2)
            sp.dma_start(u_sb[1][:], u_d[0]).then_inc(s_uld[1], 16)
            load_branches(C_GATE + 5, 0, P)

            def load_gates(j, u):
                c, dc = C_GATE + 3 * u, 6 * j - 6
                col = 2 * P * j + P * (u - 2)
                load_cols(c, dc, win_d, COL_GP + col)
                load_cols(c + 1, dc, win_d, COL_GA + col)
                load_branches(c + 2, dc, col)

            with sp.Fori(2, KD // 2 + 1) as j:
                for u in range(2):
                    load_gates(j, u)

            def rows_chunk(c, dc, w, k):
                load_chunk(c, dc, w[k, :, 0:512], w[k, :, 512:1024])

            for n in range(2 * KD):
                rows_chunk(C_OUT + n, 0, wout_d, n % KD)
                if n == 2:
                    wait(sp, s_xn, NT)
                    wait(sp, s_pool, 1)
                    sp.dma_start(gain[:], norm2_g[0].partition_broadcast(P)).then_inc(s_gain, 16)
                if n == 3:
                    wait(sp, s_py, 2 * KD)
                    wait(sp, s_ay, 2 * KD)
                if 3 <= n < 3 + NT:
                    sp.dma_start(x2[:, n - 3, :], x_d[n - 3]).then_inc(s_xr[(n - 3) // 4], 16)
            load_cols(C_FFN, 0, wgate_d, 0)
            load_cols(C_FFN + 1, 0, wup_d, 0)
            for t in range(NT):
                wait(sp, s_add, 2 * (t + 1))
                sp.dma_start(x2_d[t], x2[:, t, :]).then_inc(s_x2st, 16)

            with sp.Fori(1, KF) as m:
                load_cols(C_FFN, 2 * m, wgate_d, m * P)
                load_cols(C_FFN + 1, 2 * m, wup_d, m * P)
            wait(sp, s_xn2, NT)
            sp.dma_start(gain[:], norm_f_g.partition_broadcast(P)).then_inc(s_gain, 16)

            def down_chunks(j0, j1, hh):
                with sp.Fori(j0, j1) as j:
                    for u in range(2):
                        rows_chunk(C_DOWN + KF * hh + u, 2 * j, wdown_d, 2 * j + u)

            down_chunks(0, KF // 2 - 3, 0)
            wait(sp, s_x2st, 16 * NT)
            wait(sp, s_prod, 2 * KF)
            for tt in range(4):
                sp.dma_start(y[:, tt, :], x2_d[tt]).then_inc(s_yld, 16)
            down_chunks(KF // 2 - 3, KF // 2, 0)
            down_chunks(0, KF // 2, 1)
            wait(sp, s_out[0], 16 * 4)
            wait(sp, s_out[1], 16 * 4)

        @block.gpsimd
        def _(pool):
            g = nc.gpsimd

            def w_low(c, dc=0, width=1024):
                hi, lo = chunk_parts(c)
                wait(pool, s_whi, c + 1 + dc)
                g.tensor_tensor(lo[:, 0:width], w_raw[c % 2][:, 0:width], hi[:, 0:width].bitcast(f32),
                                ALU.subtract).then_inc(s_wlo, 1)

            def inv_root(n, col):
                wait(pool, s_var, n + 1)
                g.tensor_tensor(rstd[:, bass.ds(col, 1)], var[:, bass.ds(col, 1)], neg_half[:],
                                ALU.pow).then_inc(s_rstd, 1)

            g.memset(neg_half[:], -0.5).then_inc(s_cid, 1)
            g.memset(ident[:], 0.0).then_inc(s_cid, 1)
            pool.wait_ge(s_cid, 2)
            g.affine_select(out=ident[:], in_=ident[:], compare_op=ALU.not_equal, fill=1.0, base=0,
                            pattern=[[-1, P]], channel_multiplier=1).then_inc(s_const, 1)
            inv_root(0, 0)
            inv_root(1, 1)
            g.memset(mask_f[:], 0.0).then_inc(s_cid, 1)
            g.memset(tri[:], 1.0).then_inc(s_cid, 1)
            g.memset(ones[:], 1.0).then_inc(s_const, 1)
            g.memset(f_one[:], 1.0).then_inc(s_const, 1)
            pool.wait_ge(s_cid, 4)
            g.affine_select(out=mask_f[:], in_=mask_f[:], compare_op=ALU.is_ge, fill=NEG, base=0,
                            pattern=[[-1, P]], channel_multiplier=1).then_inc(s_const, 1)
            g.affine_select(out=tri[:], in_=tri[:], compare_op=ALU.is_ge, fill=0.0, base=0,
                            pattern=[[1, P]], channel_multiplier=-1).then_inc(s_const, 1)
            for t in range(16):
                last = g.memset(inv_cnt[:, t:t + 1], 1.0 / (t + 1))
            last.then_inc(s_const, 1)
            for n in range(2, NT):
                inv_root(n, n)
            w_low(0)
            w_low(1)

            def stack_low(p, e):
                r = slice(DH * e, DH * e + DH)
                wait(pool, s_std, 3 * (2 * p + e) + 2)
                wait(pool, s_z, 4)
                if not isinstance(p, int) or 2 * p + e > 1:
                    wait(pool, s_s, 16 * p + (0 if e else -8))
                g.tensor_tensor(k2[e][r, :], k_raw[r, :], k1[e][r, :].bitcast(f32),
                                ALU.subtract).then_inc(s_stp, 1)
                wait(pool, s_stp, 2 * p + e + 1)

            def v_low(p, e):
                wait(pool, s_vshi, 2 * p + e + 1)
                g.tensor_tensor(vs[e][:, :, DH:2 * DH], v_raw[:, :, bass.ds((2 * p + e) * DH, DH)],
                                vs[e][:, :, 0:DH].bitcast(f32), ALU.subtract).then_inc(s_vslo, 1)

            wait(pool, s_v, NT)
            wait(pool, s_wlo, 2)
            for e in range(2):
                r = slice(DH * (1 - e), DH * (1 - e) + DH)
                g.memset(q2[e][r, :].bitcast(f32), 0.0).then_inc(s_z, 1)
                g.memset(k2[e][r, :].bitcast(f32), 0.0).then_inc(s_z, 1)
                wait(pool, s_z, 2 * e + 2)
            v_low(0, 0)
            w_low(2)
            stack_low(0, 0)
            w_low(3)
            wait(pool, s_wlo, 4)

            def attention(p, last):
                stack_low(p, 1)
                v_low(p, 1)
                if not last:
                    w_low(4, 4 * p, 512)
                    w_low(5, 4 * p, 512)
                    stack_low(p + 1, 0)
                    v_low(p + 1, 0)
                    w_low(6, 4 * p)
                    w_low(7, 4 * p)
                    wait(pool, s_wlo, 4 * p + 8)
                else:
                    for c in range(C_GATE + 1, C_GATE + 4):
                        w_low(c)

            attention(0, False)
            with pool.Fori(1, 3) as p:
                attention(p, False)
            attention(3, True)

            wait(pool, s_mixhi, 1)
            g.tensor_tensor(mix_lo[:], mix_raw[:], mix_hi[:].bitcast(f32), ALU.subtract).then_inc(s_mixlo, 1)

            def a_low(n):
                wait(pool, s_ahi, n + 1)
                g.tensor_tensor(a_lo[:, n, :], a_raw[n % 2][:], a_hi[:, n, :].bitcast(f32),
                                ALU.subtract).then_inc(s_alo, 1)

            for n in range(NG):
                a_low(n)
                if n == 1:
                    w_low(C_GATE + 4)
            for c in range(C_GATE + 5, C_GATE + 8):
                w_low(c)
            with pool.Fori(1, KD // 2) as j:
                for i in range(6):
                    w_low(C_GATE + 2 + i, 6 * j)
            for c in range(C_OUT + 2, C_FFN):
                w_low(c)
                if c - C_OUT - 2 >= 8 and c - C_OUT - 2 < 12:
                    inv_root(c - C_OUT - 2, c - C_OUT - 2)
            for n in range(4):
                if n == 2:
                    w_low(C_FFN)
                inv_root(12 + n, 12 + n)
            w_low(C_FFN + 1)
            with pool.Fori(0, KF) as m:
                w_low(C_FFN + 2, 2 * m)
                w_low(C_FFN + 3, 2 * m)
            w_low(C_DOWN + 2)
            w_low(C_DOWN + 3)
            with pool.Fori(0, KF // 2 - 1) as j:
                w_low(C_DOWN + 4, 2 * j)
                w_low(C_DOWN + 5, 2 * j)
            for n in range(4):
                w_low(C_DOWN + KF + 2 + n)
                inv_root(16 + n, 16 + n)
            with pool.Fori(0, (KF - 6) // 2 - 1) as j:
                w_low(C_DOWN + KF + 6, 2 * j)
                w_low(C_DOWN + KF + 7, 2 * j)
            w_low(C_END - 2)
            w_low(C_END - 1)
            for n in range(4, 8):
                inv_root(16 + n, 16 + n)

        @block.scalar
        def _(act):
            a = nc.scalar

            def w_high(c, dc=0, width=1024):
                wait(act, s_wraw[c % 2], 32 * (c // 2 + 1) + 16 * dc)
                hi = chunk_parts(c)[0]
                a.activation(hi[:, 0:width], w_raw[c % 2][:, 0:width], ACT.Copy).then_inc(s_whi, 1)

            def square(j, u):
                wait(act, s_x[u], 16 * (j + 1))
                wait(act, s_tp, 2 * (2 * j + u - 1))
                a.activation(xn[u][:], xt[u][:], ACT.Square,
                             accum_out=ssq[:, bass.ds(2 * j + u, 1)]).then_inc(s_sq, 1)

            def high_h(j, u):
                t = 2 * j + u
                wait(act, s_v, t - 1)
                for b in range(2):
                    wait(act, s_tp, 2 * t + b + 1)
                    src = ps[:, 2 * u + b, :].rearrange("p (k n) -> p k n", n=P)
                    a.activation(hs_hi[u][:, 4 * b:4 * b + 4, :], src, ACT.Copy).then_inc(s_hshi, 1)
                    a.activation(h_hi[:, 4 * b:4 * b + 4, bass.ds(t * P, P)], src, ACT.Copy).then_inc(s_hthi, 1)

            def evac_v(j, u):
                t = 2 * j + u
                wait(act, s_v, t + 1)
                a.activation(v_raw[:, bass.ds(t, 1), 0:VH],
                             ps[:, 4 + 2 * u, 0:VH].rearrange("p (o n) -> p o n", o=1),
                             ACT.Copy).then_inc(s_vev_a, 1)

            square(0, 0)
            for i in range(4):
                if i == 2:
                    high_h(0, 0)
                    square(0, 1)
                act.wait_ge(s_wv[i], 16)
                a.activation(wv_hi[:, 2 * i:2 * i + 2, :], wv_raw[:, 2 * i:2 * i + 2, :],
                             ACT.Copy).then_inc(s_wvhi, 1)

            def stage_a(j):
                square(j + 1, 0)
                high_h(j, 1)
                evac_v(j, 0)
                square(j + 1, 1)
                high_h(j + 1, 0)
                evac_v(j, 1)

            stage_a(0)
            with act.Fori(1, 3) as j:
                stage_a(j)
            w_high(0)
            w_high(1)
            high_h(3, 1)
            evac_v(3, 0)
            evac_v(3, 1)

            act.wait_ge(s_fz, 3)
            a.activation(fe[:], fa[:], ACT.Exp, scale=-1.0).then_inc(s_fa, 1)
            act.wait_ge(s_fa, 1)
            a.activation(fl[:], fe[:], ACT.Ln, bias=1.0).then_inc(s_fa, 1)

            def evac_qk(p, n, bank):
                wait(act, s_pj, qk_units(p, n))
                dst = (q_raw, k_raw)[n // 2]
                a.activation(dst[:, HALF * (n % 2):HALF * (n % 2) + HALF], ps[:, bank, :], ACT.Copy,
                             scale=(DH ** -0.5 if n < 2 else 1.0)).then_inc(s_pjev, 1)

            def evac_fill(p, n, last):
                wait(act, s_pj, fill_units(p, n + 1, last))
                if n == 4:
                    wait(act, s_ust, 16 * p)
                dst = (u_st, q_raw, k_raw)[n // 2 - 2]
                a.activation(dst[:, HALF * (n % 2):HALF * (n % 2) + HALF], ps[:, 7, :],
                             ACT.Copy).then_inc(s_pjev, 1)

            def stack_high(p, e):
                r = slice(DH * e, DH * e + DH)
                wait(act, s_pjev, qk_units(p, 1))
                wait(act, s_s, 16 * p + (0 if e else -8))
                a.activation(q2[e][r, :], q_raw[r, :], ACT.Copy).then_inc(s_sta, 1)
                a.activation(q1[e][r, :], q_raw[r, :], ACT.Copy).then_inc(s_sta, 1)

            def v_high(p, e):
                wait(act, s_pv, 4 * p + (0 if e else -2))
                a.activation(vs[e][:, :, 0:DH], v_raw[:, :, bass.ds((2 * p + e) * DH, DH)],
                             ACT.Copy).then_inc(s_vshi, 1)

            def softmax_exp(p, s):
                n = ((s % 8) + 1) * P
                wait(act, s_mx, 16 * p + s + 1)
                wait(act, s_plo, 16 * p + s - 1)
                wait(act, s_rc, 16 * p + s - 1)
                b = 1024 * (s % 2)
                a.activation(p_raw[s % 2][:, 0:n], ps_flat[:, b:b + n], ACT.Exp, bias=negmax[s % 2][:],
                             accum_out=rowsum[s % 2][:]).then_inc(s_exp, 1)

            def p_high(p, s):
                n = ((s % 8) + 1) * P
                wait(act, s_rc, 16 * p + s + 1)
                wait(act, s_exp, 16 * p + s + 1)
                wait(act, s_th, RPAIR * p + RSUM[s - 1] if s > 0 else RPAIR * p - ROUNDS[15])
                a.activation(p_hi[s % 2][:, 0:n], p_raw[s % 2][:, 0:n], ACT.Copy,
                             scale=rowinv[s % 2][:]).then_inc(s_phi, 1)

            def evac_t(p, s):
                i = s % 8
                if i % 4 == 0:
                    wait(act, s_pv, 4 * p + s // 4)
                for r in range(ROUNDS[s]):
                    n = min(4, i + 1 - 4 * r)
                    wait(act, s_th, RPAIR * p + RSUM[s] + r + 1)
                    a.activation(pt_hi[:, 4 * r:4 * r + n, (i % 4) * P:(i % 4) * P + P],
                                 ps[:, 4, 0:n * P].rearrange("p (k n) -> p k n", n=P),
                                 ACT.Copy).then_inc(s_evh, 1)

            def evac_pv(p, g4):
                wait(act, s_pv, 4 * p + g4 + 1)
                wait(act, s_pvev, 4 * p + g4)
                a.activation(pv_tmp[:], ps[DH:2 * DH, 6, :], ACT.Copy).then_inc(s_pvt, 1)

            def f_high(b):
                act.wait_ge(s_frow, b + 1)
                a.activation(f_hi[:, 0, HALF * b:HALF * b + HALF].bitcast(f32r),
                             ps[0:NH, 1 + b, :], ACT.Copy).then_inc(s_fhi, 1)
                act.wait_ge(s_fhi, 2 * b + 1)
                a.activation(f_neg[:, 0, HALF * b:HALF * b + HALF],
                             f_hi[:, 0, HALF * b:HALF * b + HALF], ACT.Copy, scale=-1.0).then_inc(s_fhi, 1)

            act.wait_ge(s_v, NT)
            v_high(0, 0)
            evac_qk(0, 0, 7)
            evac_qk(0, 1, 6)
            w_high(2)
            act.wait_ge(s_z, 4)
            stack_high(0, 0)
            f_high(0)
            f_high(1)
            evac_qk(0, 2, 5)
            evac_qk(0, 3, 4)
            w_high(3)
            softmax_exp(0, 0)
            p_high(0, 0)
            softmax_exp(0, 1)
            act.wait_ge(s_fst, 64)

            def attention(p, last):
                for s in range(16):
                    if s == 0:
                        stack_high(p, 1)
                    if s < 15 or not last:
                        p_high(p, s + 1)
                    if s < 14 or not last:
                        softmax_exp(p, s + 2)
                    unit, _, until = (FILL_LAST if last else FILL).get(s, (0, 0, 0))
                    unit = unit if until == 24 else None
                    if unit in (0, 6):
                        wait(act, s_std, 3 * (2 * p + 2))
                        wait(act, s_stp, 2 * p + 2)
                    if unit in (0, 1, 2, 3):
                        evac_qk(p + 1, unit, 7)
                    elif unit is not None:
                        evac_fill(p, unit, last)
                    if unit == 3:
                        w_high(5, 4 * p, 512)
                    evac_t(p, s)
                    if s in (4, 8, 12):
                        evac_pv(p, s // 4 - 1)
                    if s == 1:
                        v_high(p, 1)
                    if last:
                        if unit in (5, 7, 9):
                            w_high(C_GATE + (unit - 3) // 2)
                        continue
                    if unit == 1:
                        w_high(4, 4 * p, 512)
                    if unit == 5:
                        w_high(6, 4 * p)
                        w_high(7, 4 * p)
                    if s == 7:
                        stack_high(p + 1, 0)
                    if s == 12:
                        v_high(p + 1, 0)
                evac_pv(p, 3)

            attention(0, False)
            with act.Fori(1, 3) as p:
                attention(p, False)
            attention(3, True)

            act.wait_ge(s_pjev, fill_units(3, 10, True))
            for src, dst, done in ((q_raw, sig_p, s_sgp), (k_raw, sig_a, s_sga)):
                for b in range(2):
                    h = slice(HALF * b, HALF * b + HALF)
                    a.activation(dst[:, h], src[:, h], ACT.Sigmoid).then_inc(done, 1)
            act.wait_ge(s_mixw, 16 * (1 + NG))
            a.activation(mix_hi[:], mix_raw[:], ACT.Copy).then_inc(s_mixhi, 1)

            def a_high(n):
                wait(act, s_araw[n % 2], 16 * (n // 2 + 1))
                a.activation(a_hi[:, n, :], a_raw[n % 2][:], ACT.Copy).then_inc(s_ahi, 1)

            def pool_high(n):
                wait(act, s_pool, n + 1)
                wait(act, s_mix, 2 * (n - 1))
                a.activation(pool_hi[n % 2][:], pool[:], ACT.Copy).then_inc(s_plh, 1)

            def pp_high(n):
                g = NG - 1 - n
                for b in range(2):
                    wait(act, s_mix, 2 * n + b + 1)
                    a.activation(pp_hi[:, g, HALF * b:HALF * b + HALF], ps[:, 6 - 2 * (n % 2) + b, :], ACT.Copy,
                                 scale=pscale[:, g:g + 1]).then_inc(s_pph, 1)

            def left_high(n, src, k, hh, dst):
                a.activation(dst[n % 2][:], src[:, k, HALF * hh:HALF * hh + HALF] if isinstance(k, int)
                             else src[:, bass.ds(k, 1), HALF * hh:HALF * hh + HALF].rearrange("p o n -> p (o n)"),
                             ACT.Copy).then_inc(s_lhi, 1)

            def sigmoids(m, i):
                s_in, s_done, dst, bank = ((s_gp, s_sgp, sig_p, 0), (s_ga, s_sga, sig_a, 2))[i]
                for b in range(2):
                    wait(act, s_in, 2 * m + b - 1)
                    if b == 0:
                        wait(act, s_mrg, m)
                    a.activation(dst[:, HALF * b:HALF * b + HALF], ps[:, bank + b, :],
                                 ACT.Sigmoid).then_inc(s_done, 1)

            def gates(j, u):
                m, c = 2 * j + u, C_GATE + 3 * u
                for i in range(2):
                    sigmoids(m, i)
                    w_high(c + 2 + i, 6 * j)
                wait(act, s_ay, 2 * m + 2)
                w_high(c + 4, 6 * j)

            pool_high(0)
            a_high(0)
            a_high(1)
            wait(act, s_gp, 2)
            w_high(C_GATE + 4)
            pp_high(0)
            pool_high(1)
            a_high(2)
            a_high(3)
            pool_high(2)
            wait(act, s_ga, 2)
            w_high(C_GATE + 5)
            pool_high(3)
            for n in range(1, NG):
                pp_high(n)
            wait(act, s_py, 2)
            w_high(C_GATE + 6)
            sigmoids(1, 0)
            sigmoids(1, 1)
            wait(act, s_ay, 4)
            w_high(C_GATE + 7)
            act.wait_ge(s_mrg, 2)
            left_high(0, merged, 0, 0, le_hi)
            left_high(1, merged, 1, 0, le_hi)
            with act.Fori(1, KD // 2) as j:
                for u in range(2):
                    gates(j, u)

            def norm_square(n, src, junk):
                wait(act, s_sq, n)
                a.activation(junk[:], src, ACT.Square, accum_out=ssq[:, n:n + 1]).then_inc(s_sq, 1)

            for n in range(2 * KD - 2):
                if n == KD - 1:
                    wait(act, s_tile, 4)
                else:
                    wait(act, s_kused, n + 1 - n // KD)
                wait(act, s_mrg, min(n + 3, KD))
                left_high(n + 2, merged, (n + 2) % KD, (n + 2) // KD, le_hi)
                if n < 2 * KD - 3:
                    w_high(C_OUT + 2 + n)
                if n == 2 * KD - 4:
                    w_high(C_FFN - 1)
                if n in (8, 9, 10, 11):
                    wait(act, s_add, 2 * (n - 7))
                    norm_square(n, x2[:, n - 8, :], junk_e)

            def h2_high(t):
                for b in range(2):
                    wait(act, s_tp2, 2 * t + b + 1)
                    a.activation(h_hi[:, 4 * b:4 * b + 4, t * P:t * P + P],
                                 ps[:, 2 * (t % 2) + b, :].rearrange("p (k n) -> p k n", n=P),
                                 ACT.Copy).then_inc(s_h2hi, 1)

            def square2(t):
                wait(act, s_add, 2 * (t + 1))
                norm_square(8 + t, x2[:, t, :], junk_e)

            square2(4)
            h2_high(0)
            square2(5)
            h2_high(1)
            square2(6)
            wait(act, s_tile, 8)
            w_high(C_FFN)
            h2_high(2)
            h2_high(3)
            square2(7)
            w_high(C_FFN + 1)
            h2_high(4)
            h2_high(5)

            def ffn_gate(m, dm, b):
                wait(act, s_fg, 2 * m + 2 * dm + b + 1)
                wait(act, s_silu, 2 * m + 2 * dm + b - 1)
                a.activation(sig_g[b][:], ps[:, 4 - 4 * (m % 2) + b, :], ACT.Sigmoid).then_inc(s_sig, 1)

            def ffn(m, dm, first=False):
                for b in range(2):
                    ffn_gate(m, dm, b)
                    if first and b == 0:
                        for t in range(6, 8):
                            h2_high(t)
                w_high(C_FFN + 2 + 2 * m, 2 * dm)
                wait(act, s_fu, 2 * m + 2 * dm + 2)
                w_high(C_FFN + 3 + 2 * m, 2 * dm)

            ffn(0, 0, True)
            ffn(1, 0)
            act.wait_ge(s_prod, 4)
            left_high(0, prod, 0, 0, lg_hi)
            left_high(1, prod, 1, 0, lg_hi)
            with act.Fori(1, KF // 2) as j:
                ffn(0, 2 * j)
                ffn(1, 2 * j)

            act.wait_ge(s_prod, 2 * KF)
            used0 = 2 * KD - 3

            def down(n, dn, hh, k):
                wait(act, s_kused, used0 + n + 1 - hh + dn)
                left_high(n, prod, k, hh, lg_hi)
                w_high(C_DOWN + 2 + n, dn)

            with act.Fori(0, KF // 2 - 1) as j:
                down(0, 2 * j, 0, 2 * j + 2)
                down(1, 2 * j, 0, 2 * j + 3)
            wait(act, s_kused, used0 + KF - 1)
            left_high(0, prod, 0, 1, lg_hi)
            w_high(C_DOWN + KF)
            wait(act, s_tile, 8 + 4)
            left_high(1, prod, 1, 1, lg_hi)
            w_high(C_DOWN + KF + 1)

            def store(t):
                wait(act, s_yn, t + 1)
                act.dma_start(out_d[t], y_out[t % 2][:]).then_inc(s_out[t % 2], 16)

            for i in range(6):
                down(KF + i, 0, 1, 2 + i)
                if i < 4:
                    wait(act, s_add, 16 + 2 * (i + 1))
                    norm_square(16 + i, y[:, i, :], junk_g)
                if 0 < i < 5:
                    store(i - 1)
                    act.dma_start(y[:, i - 1, :], x2_d[3 + i]).then_inc(s_yld, 16)
            with act.Fori(3, KF // 2 - 2) as j:
                down(KF, 2 * j, 1, 2 * j + 2)
                down(KF + 1, 2 * j, 1, 2 * j + 3)
            down(2 * KF - 4, 0, 1, KF - 2)
            w_high(C_END - 1)
            wait(act, s_kused, used0 + 2 * KF - 3)
            left_high(1, prod, KF - 1, 1, lg_hi)
            for t in range(4):
                wait(act, s_add, 16 + 2 * (5 + t))
                norm_square(20 + t, y[:, t, :], junk_g)
                if t:
                    store(3 + t)
            store(7)

        @block.vector
        def _(dve):
            v = nc.vector

            def variance(n):
                wait(dve, s_sq, n + 1)
                v.tensor_scalar(var[:, bass.ds(n, 1)], ssq[:, bass.ds(n, 1)], 1.0 / D, EPS,
                                ALU.mult, ALU.add).then_inc(s_var, 1)

            def normalise(n, dst, src, done):
                wait(dve, s_rstd, n + 1)
                v.scalar_tensor_tensor(dst, src, rstd[:, bass.ds(n, 1)], gain[:],
                                       ALU.mult, ALU.mult).then_inc(done, 1)

            def norm_x(j, u):
                variance(2 * j + u)
                wait(dve, s_tp, 2 * (2 * j + u - 1))
                normalise(2 * j + u, xn[u][:], xt[u][:], s_xn)

            def low_h(j, u):
                t = 2 * j + u
                wait(dve, s_v, t - 1)
                for b in range(2):
                    wait(dve, s_hshi, 2 * t + b + 1)
                    wait(dve, s_hthi, 2 * t + b + 1)
                    v.tensor_tensor(hs_lo[u][:, 4 * b:4 * b + 4, :],
                                    ps[:, 2 * u + b, :].rearrange("p (k n) -> p k n", n=P),
                                    hs_hi[u][:, 4 * b:4 * b + 4, :].bitcast(f32),
                                    ALU.subtract).then_inc(s_hslo, 1)
                wait(dve, s_hslo, 2 * t + 2)
                v.tensor_copy(h_lo[:, :, bass.ds(t * P, P)], hs_lo[u][:].bitcast(f32)).then_inc(s_htlo, 1)

            def evac_v(j, u):
                t = 2 * j + u
                wait(dve, s_v, t + 1)
                v.tensor_copy(v_raw[:, bass.ds(t, 1), VH:BW],
                              ps[:, 5 + 2 * u, 0:BW - VH].rearrange("p (o n) -> p o n", o=1))
                v.tensor_copy(fz[:, bass.ds(t, 1), :],
                              ps[:, 5 + 2 * u, BW - VH:VH].rearrange("p (o n) -> p o n", o=1)).then_inc(s_vev_d, 1)

            dve.wait_ge(s_gain, 16)
            norm_x(0, 0)
            for i in range(4):
                if i == 2:
                    low_h(0, 0)
                    norm_x(0, 1)
                dve.wait_ge(s_wvhi, i + 1)
                v.tensor_tensor(wv_lo[:, 2 * i:2 * i + 2, :], wv_raw[:, 2 * i:2 * i + 2, :],
                                wv_hi[:, 2 * i:2 * i + 2, :].bitcast(f32), ALU.subtract).then_inc(s_wvlo, 1)

            def stage_a(j):
                norm_x(j + 1, 0)
                low_h(j, 1)
                evac_v(j, 0)
                norm_x(j + 1, 1)
                low_h(j + 1, 0)
                evac_v(j, 1)

            stage_a(0)
            with dve.Fori(1, 3) as j:
                stage_a(j)
            low_h(3, 1)
            evac_v(3, 0)
            dve.wait_ge(s_const, 6)
            v.tensor_copy(ident_r[:], ident[:]).then_inc(s_cid, 1)
            v.tensor_copy(mask_r[:], mask_f[:]).then_inc(s_cid, 1)
            evac_v(3, 1)

            dve.wait_ge(s_fb, 16)
            dve.wait_ge(s_vev_d, NT)
            v.tensor_tensor(fz[:], fz[:], fbias[:].rearrange("p (o h) -> p o h", o=1).to_broadcast([P, NT, NH]),
                            ALU.add).then_inc(s_fz, 1)
            dve.wait_ge(s_fz, 1)
            v.tensor_scalar(fa[:], fz[:], -1.0, None, ALU.mult).then_inc(s_fz, 1)
            dve.wait_ge(s_fz, 2)
            v.tensor_tensor(fa[:], fa[:], fz[:], ALU.max).then_inc(s_fz, 1)
            dve.wait_ge(s_fa, 2)
            v.scalar_tensor_tensor(fe[:], fz[:], 0.0, fl[:], ALU.min, ALU.subtract).then_inc(s_fz, 1)
            dve.wait_ge(s_fcum, 1)
            v.tensor_copy(fa[:], ps[:, 0, 0:NT * NH].rearrange("p (t h) -> p t h", h=NH)).then_inc(s_fz, 1)
            for b in range(2):
                dve.wait_ge(s_fhi, 2 * b + 2)
                dst = f_hi[:, 1, HALF * b:HALF * b + HALF]
                v.tensor_tensor(dst.bitcast(f32r), ps[0:NH, 1 + b, :], f_hi[:, 0, HALF * b:HALF * b + HALF],
                                ALU.subtract).then_inc(s_flo, 1)
                dve.wait_ge(s_flo, 2 * b + 1)
                v.tensor_scalar(f_neg[:, 1, HALF * b:HALF * b + HALF], dst, -1.0, None,
                                ALU.mult).then_inc(s_flo, 1)

            def stack_q(p, e):
                r = slice(DH * e, DH * e + DH)
                o = slice(DH * (1 - e), DH * (1 - e) + DH)
                wait(dve, s_pjev, qk_units(p, 1))
                wait(dve, s_s, 16 * p + (0 if e else -8))
                wait(dve, s_sta, 2 * (2 * p + e) + 1)
                v.tensor_tensor(q1[e][o, :], q_raw[r, :], q2[e][r, :].bitcast(f32),
                                ALU.subtract).then_inc(s_std, 1)

            def stack_k(p, e):
                r = slice(DH * e, DH * e + DH)
                o = slice(DH * (1 - e), DH * (1 - e) + DH)
                wait(dve, s_pjev, qk_units(p, 3))
                v.tensor_copy(k1[e][r, :], k_raw[r, :]).then_inc(s_std, 1)
                v.tensor_copy(k1[e][o, :], k_raw[r, :]).then_inc(s_std, 1)

            def row_max(p, s):
                n = ((s % 8) + 1) * P
                wait(dve, s_s, 16 * p + s + 1)
                wait(dve, s_exp, 16 * p + s - 1)
                b = 1024 * (s % 2)
                v.reduce_max(negmax[s % 2][:], ps_flat[:, b:b + n], axis=AX.X, negate=True).then_inc(s_mx, 1)

            def row_inv(p, s):
                wait(dve, s_exp, 16 * p + s + 1)
                wait(dve, s_phi, 16 * p + s - 1)
                v.reciprocal(rowinv[s % 2][:], rowsum[s % 2][:]).then_inc(s_rc, 1)

            def p_low(p, s):
                n = ((s % 8) + 1) * P
                wait(dve, s_phi, 16 * p + s + 1)
                wait(dve, s_rc, 16 * p + s + 1)
                wait(dve, s_tl, RPAIR * p + RSUM[s - 1] if s > 0 else RPAIR * p - ROUNDS[15])
                v.scalar_tensor_tensor(p_lo[s % 2][:, 0:n], p_raw[s % 2][:, 0:n], rowinv[s % 2][:],
                                       p_hi[s % 2][:, 0:n].bitcast(f32), ALU.mult,
                                       ALU.subtract).then_inc(s_plo, 1)

            def evac_t(p, s):
                i = s % 8
                if i % 4 == 0:
                    wait(dve, s_pv, 4 * p + s // 4)
                for r in range(ROUNDS[s]):
                    n = min(4, i + 1 - 4 * r)
                    wait(dve, s_tl, RPAIR * p + RSUM[s] + r + 1)
                    v.tensor_copy(pt_lo[:, 4 * r:4 * r + n, (i % 4) * P:(i % 4) * P + P],
                                  ps[:, 5, 0:n * P].rearrange("p (k n) -> p k n", n=P)).then_inc(s_evl, 1)

            def evac_pv(p, g4):
                wait(dve, s_pvt, 4 * p + g4 + 1)
                wait(dve, s_atst[g4 % 2], 16 * (2 * p + g4 // 2))
                v.tensor_tensor(at_st[g4 % 2][:], ps[0:DH, 6, :], pv_tmp[:], ALU.add).then_inc(s_pvev, 1)

            dve.wait_ge(s_z, 4)
            stack_q(0, 0)
            stack_k(0, 0)
            row_max(0, 0)
            row_max(0, 1)
            row_inv(0, 0)
            p_low(0, 0)
            row_inv(0, 1)
            row_max(0, 2)
            dve.wait_ge(s_fst, 64)

            def attention(p, last):
                for s in range(16):
                    if s == 0:
                        stack_q(p, 1)
                        stack_k(p, 1)
                    if s < 15 or not last:
                        p_low(p, s + 1)
                    if s < 14 or not last:
                        row_inv(p, s + 2)
                    evac_t(p, s)
                    if s < 13 or not last:
                        row_max(p, s + 3)
                    if s in (4, 8, 12):
                        evac_pv(p, s // 4 - 1)
                    if s == 8 and not last:
                        stack_q(p + 1, 0)
                    if s == 10 and not last:
                        stack_k(p + 1, 0)
                evac_pv(p, 3)

            attention(0, False)
            with dve.Fori(1, 3) as p:
                attention(p, False)
            attention(3, True)

            link = [0]

            def chain(ins):
                link[0] += 1
                ins.then_inc(s_dve, 1)
                dve.wait_ge(s_dve, link[0])

            def pp_low(n):
                g = NG - 1 - n
                for b in range(2):
                    wait(dve, s_pph, 2 * n + b + 1)
                    v.scalar_tensor_tensor(pp_lo[:, g, HALF * b:HALF * b + HALF],
                                           ps[:, 6 - 2 * (n % 2) + b, :], pscale[:, g:g + 1],
                                           pp_hi[:, g, HALF * b:HALF * b + HALF].bitcast(f32),
                                           ALU.mult, ALU.subtract).then_inc(s_ppl, 1)

            def pool_low_part(n):
                wait(dve, s_plh, n + 1)
                wait(dve, s_mix, 2 * (n - 1))
                v.tensor_tensor(pool_lo[n % 2][:], pool[:], pool_hi[n % 2][:].bitcast(f32),
                                ALU.subtract).then_inc(s_pll, 1)

            for n in range(NG):
                g = NG - 1 - n
                w = 2 << g
                if n == 0:
                    wait(dve, s_pjev, fill_units(3, 6, True))
                else:
                    wait(dve, s_uld[n % 2], 16 * ((n + 1) // 2))
                u = u_sb[n % 2] if n else u_st
                cur = u
                for i in range(g + 1):
                    d = 1 << i
                    nxt = win[i % 2]
                    v.tensor_copy(nxt[:, 0:d], cur[:, 0:d])
                    chain(v.tensor_tensor(nxt[:, d:S], cur[:, d:S], cur[:, 0:S - d], ALU.add))
                    cur = nxt
                if n >= 2:
                    pool_low_part(n - 1)
                if n == 2:
                    pp_low(0)
                wait(dve, s_plh, n)
                wait(dve, s_pll, n)
                v.tensor_tensor(head_tmp[:, 0:w], cur[:, 0:w], inv_cnt[:, 0:w], ALU.mult)
                chain(v.scalar_tensor_tensor(pool[:, w:S], cur[:, w:S], 1.0 / w, u[:, w:S],
                                             ALU.mult, ALU.subtract))
                v.tensor_tensor(pool[:, 0:w], head_tmp[:, 0:w], u[:, 0:w], ALU.subtract).then_inc(s_pool, 1)
                if n in (0, NG - 1):
                    pool_low_part(n)
            for n in range(1, NG):
                pp_low(n)

            def merge(j):
                for u in range(2):
                    m = 2 * j + u
                    for s_in, s_gate, sig, bank in ((s_py, s_sgp, sig_p, 4), (s_ay, s_sga, sig_a, 6)):
                        for b in range(2):
                            wait(dve, s_gate, 2 * m + b + 1)
                            wait(dve, s_in, 2 * m + b + 1)
                            h = slice(HALF * b, HALF * b + HALF)
                            v.tensor_tensor(sig[:, h], ps[:, bank + b, :], sig[:, h], ALU.mult).then_inc(s_mul, 1)
                    wait(dve, s_mul, 4 * m + 4)
                    v.tensor_tensor(merged[:, bass.ds(m, 1), :],
                                    sig_p[:].rearrange("p (o n) -> p o n", o=1),
                                    sig_a[:].rearrange("p (o n) -> p o n", o=1), ALU.add).then_inc(s_mrg, 1)

            def left_low(n, src, k, hh, hi, lo):
                s_ap = (src[:, k, HALF * hh:HALF * hh + HALF] if isinstance(k, int)
                        else src[:, bass.ds(k, 1), HALF * hh:HALF * hh + HALF].rearrange("p o n -> p (o n)"))
                v.tensor_tensor(lo[n % 2][:], s_ap, hi[n % 2][:].bitcast(f32), ALU.subtract).then_inc(s_llo, 1)

            merge(0)
            for n in range(2):
                dve.wait_ge(s_lhi, n + 1)
                left_low(n, merged, n, 0, le_hi, le_lo)
            with dve.Fori(1, KD // 2) as j:
                merge(j)

            def add_tile(t, n, dst):
                wait(dve, s_tile, n + 1)
                for f in range(2):
                    d = dst[:, HALF * f:HALF * f + HALF]
                    v.tensor_tensor(d, ps[:, 2 * (t % 4) + f, :], d, ALU.add).then_inc(s_add, 1)

            def h2_low(t):
                for b in range(2):
                    wait(dve, s_h2hi, 2 * t + b + 1)
                    hd = h_hi[:, 4 * b:4 * b + 4, t * P:t * P + P]
                    v.tensor_tensor(h_lo[:, 4 * b:4 * b + 4, t * P:t * P + P],
                                    ps[:, 2 * (t % 2) + b, :].rearrange("p (k n) -> p k n", n=P),
                                    hd.bitcast(f32), ALU.subtract).then_inc(s_h2lo, 1)

            def norm2(t):
                normalise(KD + t, xn2[:, t, :], x2[:, t, :], s_xn2)

            for n in range(2, 2 * KD):
                dve.wait_ge(s_lhi, n + 1)
                left_low(n, merged, n % KD, n // KD, le_hi, le_lo)
                if n == KD:
                    dve.wait_ge(s_xr[0], 64)
                    dve.wait_ge(s_gain, 32)
                    for t in range(4):
                        add_tile(t, t, x2[:, t, :])
                if KD + 1 < n < KD + 6:
                    norm2(n - 2 - KD)
                if KD < n < KD + 5:
                    variance(n - 1)
            dve.wait_ge(s_xr[1], 64)
            for t in range(4, 8):
                add_tile(t, t, x2[:, t, :])
                if t > 4:
                    variance(KD + t - 1)
                    h2_low(t - 5)
            h2_low(3)
            variance(KD + 7)
            for t in range(4, 8):
                norm2(t)
            h2_low(4)
            h2_low(5)

            def silu_half(m, dm, b):
                wait(dve, s_sig, 2 * m + 2 * dm + b + 1)
                wait(dve, s_prod, 2 * m + 2 * dm + b - 1)
                v.tensor_tensor(silu[b][:], ps[:, 4 - 4 * (m % 2) + b, :], sig_g[b][:], ALU.mult).then_inc(s_silu, 1)

            def prod_half(m, dm, b):
                wait(dve, s_fu, 2 * m + 2 * dm + b + 1)
                wait(dve, s_silu, 2 * m + 2 * dm + b + 1)
                v.tensor_tensor(prod[:, bass.ds(m + dm, 1), HALF * b:HALF * b + HALF],
                                ps[:, 6 - 4 * (m % 2) + b, :].rearrange("p (o n) -> p o n", o=1),
                                silu[b][:].rearrange("p (o n) -> p o n", o=1), ALU.mult).then_inc(s_prod, 1)

            def ffn(m, dm, first=False):
                if first:
                    silu_half(m, dm, 0)
                    for t in range(6, 8):
                        h2_low(t)
                    prod_half(m, dm, 0)
                    silu_half(m, dm, 1)
                    prod_half(m, dm, 1)
                    return
                for b in range(2):
                    silu_half(m, dm, b)
                for b in range(2):
                    prod_half(m, dm, b)

            dve.wait_ge(s_x2st, 16 * NT)
            ffn(0, 0, True)
            ffn(1, 0)
            for n in range(2):
                dve.wait_ge(s_lhi, 2 * KD + n + 1)
                left_low(n, prod, n, 0, lg_hi, lg_lo)
            with dve.Fori(1, KF // 2) as j:
                ffn(0, 2 * j)
                ffn(1, 2 * j)

            l0 = 2 * KD

            def down(n, dn, hh, k):
                wait(dve, s_lhi, l0 + n + dn + 1)
                left_low(n, prod, k, hh, lg_hi, lg_lo)

            with dve.Fori(1, KF // 2) as j:
                down(0, 2 * j, 0, 2 * j)
                down(1, 2 * j, 0, 2 * j + 1)
            down(KF, 0, 1, 0)
            dve.wait_ge(s_yld, 16 * 4)
            dve.wait_ge(s_gain, 48)
            for t in range(4):
                add_tile(t, 8 + t, y[:, t, :])
            down(KF + 1, 0, 1, 1)

            def final(n, t):
                variance(16 + n)
                wait(dve, s_out[n % 2], 16 * (n // 2))
                normalise(16 + n, y_out[n % 2][:], y[:, t, :], s_yn)

            for t in range(4):
                down(KF + 2 + t, 0, 1, 2 + t)
                final(t, t)
            with dve.Fori(3, KF // 2) as j:
                down(KF, 2 * j, 1, 2 * j)
                down(KF + 1, 2 * j, 1, 2 * j + 1)
            dve.wait_ge(s_yld, 16 * 8)
            add_tile(4, 12, y[:, 0, :])
            for t in range(4):
                if t < 3:
                    add_tile(5 + t, 13 + t, y[:, 1 + t, :])
                final(4 + t, t)

        @block.tensor
        def _(pe):
            mm = nc.tensor.matmul

            def group(bank, stats, movs, first=True, last=True):
                n = len(stats)
                for i in range(n):
                    ins = mm(bank, stats[i], movs[i], start=first and i == 0, stop=last and i == n - 1)
                return ins

            def three(wh, wl, hh, hl):
                return wh + wh + wl, hh + hl + hh

            def w_tiles(c, k0, n):
                cut = lambda t: [t[c % 2][:, P * k:P * k + P] for k in range(k0, k0 + n)]
                return cut(w_hi), cut(w_lo)

            def cols(hi, lo, b, n, k0=0):
                cut = lambda t: [t[:, k, HALF * b:HALF * b + HALF] for k in range(k0, k0 + n)]
                return cut(hi), cut(lo)

            def column_product(c, b, bank):
                return group(ps[:, bank, :], *three(*w_tiles(c, 0, KD), *cols(h_hi, h_lo, b, KD)))

            def transpose_x(j, u):
                t = 2 * j + u
                wait(pe, s_xn, t + 1)
                wait(pe, s_hthi, 2 * (t - 1))
                wait(pe, s_hslo, 2 * (t - 1))
                for b in range(2):
                    for k in range(4):
                        ins = nc.tensor.transpose(ps[:, 2 * u + b, P * k:P * k + P],
                                                  xn[u][:, (4 * b + k) * P:(4 * b + k + 1) * P], ident[:])
                    ins.then_inc(s_tp, 1)

            def v_product(j, u):
                t = 2 * j + u
                wait(pe, s_htlo, t + 1)
                wait(pe, s_hthi, 2 * t + 2)
                wait(pe, s_vev_a, t - 1)
                wait(pe, s_vev_d, t - 1)
                for k in range(KD):
                    if isinstance(t, int) and t == 0 and k == 4:
                        transpose_x(0, 1)
                    if isinstance(t, int) and t == 0 and k % 2 == 0:
                        pe.wait_ge(s_wvlo, k // 2 + 1)
                    for i, (l, r) in enumerate(((hs_hi, wv_hi), (hs_hi, wv_lo), (hs_lo, wv_hi))):
                        for b in range(2):
                            ins = mm(ps[:, 4 + 2 * u + b, 0:VH], l[u][:, k, :], r[:, k, VH * b:VH * b + VH],
                                     start=(k == 0 and i == 0), stop=(k == KD - 1 and i == 2))
                ins.then_inc(s_v, 1)

            pe.wait_ge(s_const, 1)
            transpose_x(0, 0)

            def stage_a(j):
                if not isinstance(j, int):
                    transpose_x(j, 1)
                v_product(j, 0)
                transpose_x(j + 1, 0)
                v_product(j, 1)

            stage_a(0)
            with pe.Fori(1, 3) as j:
                stage_a(j)
            transpose_x(3, 1)
            v_product(3, 0)
            v_product(3, 1)

            pe.wait_ge(s_htlo, NT)
            pe.wait_ge(s_hthi, 2 * NT)
            pe.wait_ge(s_vev_a, NT)
            pe.wait_ge(s_vev_d, NT)
            for n in range(4):
                if n % 2 == 0:
                    wait(pe, s_wlo, 1 + n // 2)
                column_product(n // 2, n % 2, 7 - n).then_inc(s_pj, 1)
                if n == 0:
                    pe.wait_ge(s_fz, 4)
                    mm(ps[:, 0, 0:NT * NH], tri[:], fe[:].rearrange("p t h -> p (t h)"), start=True, stop=False)
                    for t in range(NT - 1):
                        rest = NT - 1 - t
                        ins = mm(ps[:, 0, NH * (t + 1):NH * NT].rearrange("p (t h) -> p t h", h=NH), ones[:],
                                 fe[:, t:t + 1, :].to_broadcast([P, rest, NH]),
                                 start=False, stop=(t == NT - 2))
                    ins.then_inc(s_fcum, 1)
                if n == 1:
                    pe.wait_ge(s_fz, 5)
                    for b in range(2):
                        for t in range(4):
                            ins = nc.tensor.transpose(ps[0:NH, 1 + b, P * t:P * t + P], fa[:, 4 * b + t, :], ident[:])
                        ins.then_inc(s_frow, 1)

            def scores(p, s):
                e, i = (s // 8) % 2, s % 8
                n = (i + 1) * P
                if i == 0:
                    b = 2 * p + s // 8
                    wait(pe, s_sta, 2 * (b + 1))
                    wait(pe, s_std, 3 * (b + 1))
                    wait(pe, s_stp, b + 1)
                    wait(pe, s_frd[e], 32 * (p + s // 16 + 1))
                wait(pe, s_exp, 16 * p + s - 1)
                qt = slice(i * P, i * P + P)
                for h in range(0, n, HALF):
                    w = min(HALF, n - h)
                    bank = ps[:, 2 * (s % 2) + h // HALF, :]
                    diag = h + w == n
                    mm(bank[:, 0:w], q1[e][:, qt], k1[e][:, h:h + w], start=True, stop=False)
                    ins = mm(bank[:, 0:w], q2[e][:, qt], k2[e][:, h:h + w], start=False, stop=not diag)
                    if diag:
                        ins = mm(bank[:, w - P:w], ident_r[:], mask_r[:], start=False, stop=True)
                ins.then_inc(s_s, 1)

            def transposes(p, s, r):
                i = s % 8
                n = min(4, i + 1 - 4 * r)
                for src, ready, free, done, bank in ((p_hi, s_phi, s_evh, s_th, 4), (p_lo, s_plo, s_evl, s_tl, 5)):
                    if r == 0:
                        wait(pe, ready, 16 * p + s + 1)
                    wait(pe, free, RPAIR * p + RSUM[s] + r)
                    for k in range(n):
                        ins = nc.tensor.transpose(ps[:, bank, P * k:P * k + P].bitcast(f32r),
                                                  src[s % 2][:, (4 * r + k) * P:(4 * r + k + 1) * P], ident_r[:])
                    ins.then_inc(done, 1)

            def values(p, s):
                e, g = s // 8, (s % 8) // 4
                wait(pe, s_vslo, 2 * p + e + 1)
                wait(pe, s_evh, RPAIR * p + RSUM[s + 1])
                wait(pe, s_evl, RPAIR * p + RSUM[s + 1])
                wait(pe, s_pvev, 4 * p + s // 4)
                nk = 4 * g + 4
                for x_, pt in enumerate((pt_hi, pt_lo)):
                    for k in range(nk):
                        q0 = max(0, k - 4 * g) * P
                        ins = mm(ps[:, 6, q0:HALF], vs[e][:, k, :], pt[:, k, q0:HALF],
                                 start=(x_ == 0 and k == 0), stop=(x_ == 1 and k == nk - 1))
                ins.then_inc(s_pv, 1)

            def fill(p, s, last):
                n, a, b = (FILL_LAST if last else FILL)[s]
                if a == 0:
                    wait(pe, s_pjev, fill_units(p, n, last))
                    if n % 2 == 0:
                        wait(pe, s_wlo, C_U3 + n // 2 - 1 if last else 4 * p + 3 + n // 2)
                if n == 4 and b > 12 and not last:
                    wait(pe, s_wlo, 4 * p + 6)
                if n < 4 or last:
                    st, mv = three(*w_tiles(n // 2 % 2, 0, KD), *cols(h_hi, h_lo, n % 2, KD))
                else:
                    st, mv = [], []
                    for k0 in range(0, KD, 4):
                        part = three(*w_tiles(k0 // 4, 0, 4), *cols(h_hi, h_lo, n % 2, 4, k0))
                        st, mv = st + part[0], mv + part[1]
                ins = group(ps[:, 7, :], st[a:b], mv[a:b], first=(a == 0), last=(b == 3 * KD))
                if b == 3 * KD:
                    ins.then_inc(s_pj, 1)

            pe.wait_ge(s_cid, 6)
            pe.wait_ge(s_flo, 4)
            pe.wait_ge(s_fhi, 4)
            for s in range(AHEAD):
                scores(0, s)

            def attention(p, last):
                for s in range(16):
                    if s in (FILL_LAST if last else FILL):
                        fill(p, s, last)
                    transposes(p, s, 0)
                    if s + AHEAD < 16 or not last:
                        scores(p, s + AHEAD)
                    if ROUNDS[s] == 2:
                        transposes(p, s, 1)
                    if s % 4 == 3:
                        values(p, s)

            attention(0, False)
            with pe.Fori(1, 3) as p:
                attention(p, False)
            attention(3, True)

            def mix(n):
                g = NG - 1 - n
                wait(pe, s_pvev, 16)
                wait(pe, s_pjev, fill_units(3, 10, True))
                wait(pe, s_mixlo, 1)
                wait(pe, s_plh, n + 1)
                wait(pe, s_pll, n + 1)
                wait(pe, s_pph, 2 * (n - 1))
                wait(pe, s_ppl, 2 * (n - 1))
                for b in range(2):
                    h = slice(HALF * b, HALF * b + HALF)
                    w, l = mix_hi[:, g, :], mix_lo[:, g, :]
                    hi, lo = pool_hi[n % 2][:, h], pool_lo[n % 2][:, h]
                    group(ps[:, 6 - 2 * (n % 2) + b, :], [w, w, l], [hi, lo, hi]).then_inc(s_mix, 1)

            pe.wait_ge(s_exp, 64)
            pe.wait_ge(s_evh, 4 * RPAIR)
            pe.wait_ge(s_evl, 4 * RPAIR)

            def gate(m, c, dc, i):
                done, free, bank = ((s_gp, s_sgp, 0), (s_ga, s_sga, 2))[i]
                wait(pe, s_wlo, c + 1 + dc)
                if not isinstance(m, int):
                    wait(pe, free, 2 * m)
                for b in range(2):
                    column_product(c, b, bank + b).then_inc(done, 1)

            def branch(c, i):
                hi, lo, done, bank = ((pp_hi, pp_lo, s_py, 4), (a_hi, a_lo, s_ay, 6))[i]
                for b in range(2):
                    group(ps[:, bank + b, :],
                          *three(*w_tiles(c, 4 * i, 4), *cols(hi, lo, b, 4))).then_inc(done, 1)

            gate(1, C_GATE + 2, 0, 0)
            mix(0)
            gate(1, C_GATE + 3, 0, 1)
            for n in range(1, NG):
                mix(n)
            wait(pe, s_wlo, C_GATE + 5)
            pe.wait_ge(s_alo, NG)
            pe.wait_ge(s_ppl, 2 * NG - 2)
            pe.wait_ge(s_pph, 2 * NG - 2)
            branch(C_GATE + 4, 1)
            pe.wait_ge(s_ppl, 2 * NG)
            pe.wait_ge(s_pph, 2 * NG)
            branch(C_GATE + 4, 0)
            wait(pe, s_wlo, C_GATE + 6)
            wait(pe, s_mul, 4)
            branch(C_GATE + 5, 0)
            branch(C_GATE + 5, 1)
            with pe.Fori(1, KD // 2) as j:
                for u in range(2):
                    m, c = 2 * j + u, C_GATE + 3 * u
                    gate(m, c, 6 * j, 0)
                    gate(m, c + 1, 6 * j, 1)
                    wait(pe, s_wlo, c + 3 + 6 * j)
                    wait(pe, s_mul, 4 * m)
                    branch(c + 2, 0)
                    branch(c + 2, 1)

            def row_tile(t, n, c, lhi, llo, first, last):
                cut = slice(P * t, P * t + P)
                hi, lo = lhi[n % 2][:, cut], llo[n % 2][:, cut]
                whi, wlo = chunk_parts(c)
                for i, (l, w) in enumerate(((hi, whi), (hi, wlo), (lo, whi))):
                    for f in range(2):
                        ins = mm(ps[:, 2 * t + f, :], l, w[:, HALF * f:HALF * f + HALF],
                                 start=first and i == 0, stop=last and i == 2)
                return ins

            def row_step(n, c, lhi, llo, first, last, free=None, tiles=None):
                for t in range(4) if tiles is None else tiles:
                    if free is not None:
                        free(t)
                    ins = row_tile(t, n, c, lhi, llo, first, last)
                    if last:
                        ins.then_inc(s_tile, 1)
                if not last:
                    ins.then_inc(s_kused, 1)

            def row_end(n, c, lhi, llo, l0=0, between=lambda t: None):
                pe.wait_ge(s_wlo, c + 1)
                pe.wait_ge(s_llo, l0 + n + 1)
                for t in range(4):
                    row_tile(t, n, c, lhi, llo, False, False)
                    if t == 0:
                        pe.wait_ge(s_wlo, c + 2)
                        pe.wait_ge(s_llo, l0 + n + 2)
                    row_tile(t, n + 1, c + 1, lhi, llo, False, True).then_inc(s_tile, 1)
                    between(t)

            def free_e(t):
                if t < 2:
                    pe.wait_ge(s_sga, 2 * KD)
                else:
                    pe.wait_ge(s_mul, 4 * KD - 6 + 2 * t)

            for n in range(2 * KD - 2):
                pe.wait_ge(s_wlo, C_OUT + n + 1)
                pe.wait_ge(s_llo, n + 1)
                row_step(n, C_OUT + n, le_hi, le_lo, n % KD == 0, n % KD == KD - 1,
                         free_e if n == 0 else (lambda t: pe.wait_ge(s_add, 2 * t + 2)) if n == KD else None)

            def transpose_h2(t):
                wait(pe, s_xn2, t + 1)
                if t < 2:
                    wait(pe, s_add, 2 * (5 + t))
                else:
                    wait(pe, s_h2lo, 2 * (t - 1))
                    wait(pe, s_h2hi, 2 * (t - 1))
                for b in range(2):
                    for k in range(4):
                        ins = nc.tensor.transpose(ps[:, 2 * (t % 2) + b, P * k:P * k + P],
                                                  xn2[:, t, (4 * b + k) * P:(4 * b + k + 1) * P], ident[:])
                    ins.then_inc(s_tp2, 1)

            row_end(2 * KD - 2, C_OUT + 2 * KD - 2, le_hi, le_lo,
                    between=lambda t: transpose_h2(t - 1) if t else None)
            transpose_h2(3)

            def ffn(m, dm):
                for i, done in enumerate((s_fg, s_fu)):
                    wait(pe, s_wlo, C_FFN + 2 * m + i + 1 + 2 * dm)
                    wait(pe, s_silu if i == 0 else s_prod, 2 * m + 2 * dm - 2)
                    for b in range(2):
                        column_product(C_FFN + i, b, 4 - 4 * (m % 2) + 2 * i + b).then_inc(done, 1)

            for b in range(2):
                pe.wait_ge(s_h2lo, NT * (b + 1))
                pe.wait_ge(s_h2hi, NT * (b + 1))
                for i, done in enumerate((s_fg, s_fu)):
                    wait(pe, s_wlo, C_FFN + i + 1)
                    wait(pe, s_add, 14 + 2 * i)
                    st, mv = three(*w_tiles(C_FFN + i, 0, KD), *cols(h_hi, h_lo, b, KD))
                    cut, bank = 3 * KD // 2, ps[:, 4 + 2 * i + b, :]
                    group(bank, st[:cut], mv[:cut], last=False)
                    if b == 0 and i == 1:
                        transpose_h2(6)
                        transpose_h2(7)
                    group(bank, st[cut:], mv[cut:], first=False).then_inc(done, 1)
                    if b == 0 and i == 0:
                        transpose_h2(4)
                        transpose_h2(5)
            ffn(1, 0)
            with pe.Fori(1, KF // 2) as j:
                ffn(0, 2 * j)
                ffn(1, 2 * j)

            l0 = 2 * KD

            def free_g(hh, t):
                if hh:
                    pe.wait_ge(s_add, 18 + 2 * t)
                else:
                    pe.wait_ge(s_prod, 2 * KF if t < 2 else 2 * KF - 2)

            def down(n, dn, first=False, last=False, free=None, tiles=None):
                wait(pe, s_wlo, C_DOWN + n + 1 + dn)
                wait(pe, s_llo, l0 + n + 1 + dn)
                row_step(n, C_DOWN + n, lg_hi, lg_lo, first, last, free, tiles)

            for hh in range(2):
                n0 = KF * hh
                down(n0, 0, first=True, free=lambda t: free_g(hh, t), tiles=None if hh else (2, 3, 0, 1))
                down(n0 + 1, 0)
                with pe.Fori(1, KF // 2 - 1) as j:
                    down(n0, 2 * j)
                    down(n0 + 1, 2 * j)
                if hh == 0:
                    down(n0 + KF - 2, 0)
                    down(n0 + KF - 1, 0, last=True)
            row_end(2 * KF - 2, C_END - 2, lg_hi, lg_lo, l0)


_INS = ["x", "norm1_g", "w_in", "b_forget", "pool_mix", "pool_scale", "w_pool_out", "w_attn_out",
        "w_out", "norm2_g", "w_ffn_gate", "w_ffn_up", "w_ffn_down", "norm_f_g"]


def kernel(**inputs):
    import numpy as np
    import concourse.bacc as bacc
    from concourse.bass_utils import run_bass_kernel_spmd

    nc = bacc.Bacc("TRN2", target_bir_lowering=False, num_devices=1, dynamic_dma_scratch_size=1024)
    arrays, args = {}, []
    for name in _INS:
        a = np.ascontiguousarray(inputs[name])
        arrays[f"in_{name}"] = a
        args.append(nc.dram_tensor(f"in_{name}", a.shape, mybir.dt.from_np(a.dtype), kind="ExternalInput").ap())
    out = nc.dram_tensor("out_0", (1, S, D), mybir.dt.float32, kind="ExternalOutput").ap()
    hybrid_block(nc, *args, out)
    r = run_bass_kernel_spmd(nc, [arrays], core_ids=[0])
    return r.results[0]["out_0"]
```
